# Optimizing a Trainium2 kernel written in Bass

```python
import math
import jax, jax.numpy as jnp
from jax import lax
import numpy as np

D_MODEL = 1024
BATCH = 1
SEQ = 256
DEPTH = 2

N_MIXERS = 4
LAYERS_PER_MIXER = tuple(len(range(m, DEPTH, N_MIXERS)) for m in range(N_MIXERS))
DN_ALPHA = (2.0 * DEPTH) ** 0.25
DN_BETA = (8.0 * DEPTH) ** -0.25
LN_EPS = 1e-5
NEG_INF = -1e30
Q_BLOCK = 128
GATHER_BLOCK = 32

MLA_HEADS = 16
MLA_Q_RANK = 384
MLA_KV_RANK = 256
MLA_NOPE = 64
MLA_ROPE = 32
MLA_V = 64
ROPE_THETA = 10000.0
MLA_IN = MLA_Q_RANK + MLA_KV_RANK + MLA_ROPE

NSA_HEADS = 16
NSA_KV_GROUPS = 4
NSA_HD = 64
NSA_CMP_LEN = 32
NSA_CMP_STRIDE = 16
NSA_SLC_LEN = 64
NSA_TOP_N = 8
NSA_WINDOW = 512
NSA_FORCE = 1e4
NSA_IN = NSA_HEADS * NSA_HD + 6 * NSA_KV_GROUPS * NSA_HD + 3 * NSA_HEADS

DIFF_HEADS = 8
DIFF_HD = 64
DIFF_IN = 3 * DIFF_HEADS * 2 * DIFF_HD

DIL_PATTERNS = ((128, 1), (512, 4), (2048, 16))
DIL_HEADS = 8
DIL_HD = 64
DIL_IN = len(DIL_PATTERNS) * 3 * DIL_HEADS * DIL_HD

MOE_GROUPS = 4
MOE_EXPERTS_PER_GROUP = 4
MOE_EXPERTS = MOE_GROUPS * MOE_EXPERTS_PER_GROUP
MOE_FF = 512
MOE_TOPK = 2

kernel_name = 'hybrid_mla_nsa_diff_dilated_hmoe_deepnorm'

def layer_norm(x, g, b):
    xf = x.astype(jnp.float32)
    mu = jnp.mean(xf, axis=-1, keepdims=True)
    var = jnp.mean(jnp.square(xf - mu), axis=-1, keepdims=True)
    return ((xf - mu) * lax.rsqrt(var + LN_EPS) * g + b).astype(x.dtype)

def rms_norm(x, g, eps=1e-6):
    xf = x.astype(jnp.float32)
    return (xf * lax.rsqrt(jnp.mean(xf * xf, axis=-1, keepdims=True) + eps) * g).astype(x.dtype)

def alibi_slopes(n):
    return jnp.asarray(2.0 ** (-8.0 * np.arange(1, n + 1) / n), jnp.float32)

def rope(x, pos):
    half = x.shape[-1] // 2
    freq = ROPE_THETA ** (-jnp.arange(half, dtype=jnp.float32) / half)
    ang = pos.astype(jnp.float32)[:, None] * freq
    cos, sin = jnp.cos(ang)[:, None, :], jnp.sin(ang)[:, None, :]
    x1, x2 = x[..., :half].astype(jnp.float32), x[..., half:].astype(jnp.float32)
    return jnp.concatenate([x1 * cos - x2 * sin, x1 * sin + x2 * cos], axis=-1).astype(x.dtype)

def split_blocks(a, blk):
    b, s = a.shape[:2]
    return jnp.moveaxis(a.reshape(b, s // blk, blk, *a.shape[2:]), 1, 0)

def merge_blocks(a):
    nb, b, blk = a.shape[:3]
    return jnp.moveaxis(a, 0, 1).reshape(b, nb * blk, *a.shape[3:])

def mla_mixer(x, w_in, q_norm, kv_norm, w_qb, w_kvb, w_o):
    b, s, _ = x.shape
    h, dq = MLA_HEADS, MLA_NOPE + MLA_ROPE
    c_q, c_kv, k_rope = jnp.split(x @ w_in, [MLA_Q_RANK, MLA_Q_RANK + MLA_KV_RANK], axis=-1)
    q = (rms_norm(c_q, q_norm) @ w_qb).reshape(b, s, h, dq)
    kv = (rms_norm(c_kv, kv_norm) @ w_kvb).reshape(b, s, h, MLA_NOPE + MLA_V)
    pos = jnp.arange(s)
    q = jnp.concatenate([q[..., :MLA_NOPE], rope(q[..., MLA_NOPE:], pos)], axis=-1)
    k_r = jnp.broadcast_to(rope(k_rope[:, :, None, :], pos), (b, s, h, MLA_ROPE))
    k = jnp.concatenate([kv[..., :MLA_NOPE], k_r], axis=-1)
    v = kv[..., MLA_NOPE:]
    scale = dq ** -0.5

    def attend(args):
        i, q_blk = args
        t = i * Q_BLOCK + jnp.arange(Q_BLOCK)
        sc = jnp.einsum('bqhd,bkhd->bhqk', q_blk, k).astype(jnp.float32) * scale
        sc = jnp.where(pos[None, :] <= t[:, None], sc, NEG_INF)
        p = jax.nn.softmax(sc, axis=-1).astype(v.dtype)
        return jnp.einsum('bhqk,bkhd->bqhd', p, v)

    o = merge_blocks(lax.map(attend, (jnp.arange(s // Q_BLOCK), split_blocks(q, Q_BLOCK))))
    return o.reshape(b, s, h * MLA_V) @ w_o

def nsa_mixer(x, w_in, w_phi_k, w_phi_v, cmp_pos, w_o):
    b, s, _ = x.shape
    h, g, d = NSA_HEADS, NSA_KV_GROUPS, NSA_HD
    hpg = h // g
    blk, W, Ls = GATHER_BLOCK, NSA_WINDOW, NSA_SLC_LEN
    cuts = [h * d + i * g * d for i in range(7)]
    q, kc, vc, ks, vs, kw, vw, gl = jnp.split(x @ w_in, cuts, axis=-1)
    q = q.reshape(b, s, g, hpg, d)
    kc, vc, ks, vs, kw, vw = [a.reshape(b, s, g, d) for a in (kc, vc, ks, vs, kw, vw)]
    gates = jax.nn.sigmoid(gl.astype(jnp.float32)).reshape(b, s, g, hpg, 3)
    slopes = alibi_slopes(h).reshape(g, hpg)
    scale = d ** -0.5
    n_cmp = (s - NSA_CMP_LEN) // NSA_CMP_STRIDE + 1
    cmp_start = np.arange(n_cmp) * NSA_CMP_STRIDE
    cmp_idx = cmp_start[:, None] + np.arange(NSA_CMP_LEN)[None, :]

    def compress(a, w_phi):
        blocks = a[:, cmp_idx] + cmp_pos[:, None, :]
        blocks = jnp.swapaxes(blocks, 2, 3).reshape(b, n_cmp, g, NSA_CMP_LEN * d)
        return blocks @ w_phi

    k_cmp, v_cmp = compress(kc, w_phi_k), compress(vc, w_phi_v)
    cmp_end = jnp.asarray(cmp_start + NSA_CMP_LEN - 1, jnp.float32)
    n_slc = s // Ls
    slc_start = np.arange(n_slc) * Ls
    overlap = (cmp_start[:, None] < slc_start[None, :] + Ls) & (cmp_start[:, None] + NSA_CMP_LEN > slc_start[None, :])
    cmp_to_slc = jnp.asarray(overlap, jnp.float32)
    top_n = min(NSA_TOP_N, n_slc)
    ks_blk = jnp.moveaxis(ks.reshape(b, n_slc, Ls, g, d), 3, 1)
    vs_blk = jnp.moveaxis(vs.reshape(b, n_slc, Ls, g, d), 3, 1)
    kw_pad = jnp.pad(kw, ((0, 0), (W, 0), (0, 0), (0, 0)))
    vw_pad = jnp.pad(vw, ((0, 0), (W, 0), (0, 0), (0, 0)))
    bi = jnp.arange(b)[:, None, None, None]
    gi = jnp.arange(g)[None, :, None, None]
    sidx = jnp.arange(n_slc)
    slc_start_j = jnp.asarray(slc_start)

    def attend(args):
        i, q_blk, g_blk = args
        t = i * blk + jnp.arange(blk)
        tf = t.astype(jnp.float32)
        dist_c = tf[:, None] - cmp_end[None, :]
        vis_c = dist_c >= 0
        sc = jnp.einsum('bqgjd,bngd->bgjqn', q_blk, k_cmp).astype(jnp.float32) * scale
        sc = jnp.where(vis_c, sc - slopes[:, :, None, None] * dist_c, NEG_INF)
        p_c = jax.nn.softmax(sc, axis=-1) * jnp.any(vis_c, axis=-1)[:, None]
        o_c = jnp.einsum('bgjqn,bngd->bqgjd', p_c.astype(v_cmp.dtype), v_cmp)
        imp = jnp.einsum('bgjqn,ns->bgqs', p_c, cmp_to_slc)
        forced = (sidx[None, :] == 0) | (sidx[None, :] == (t // Ls)[:, None])
        future = slc_start_j[None, :] > t[:, None]
        score = imp + jnp.where(forced, NSA_FORCE, 0.0) - jnp.where(future, 2.0 * NSA_FORCE, 0.0)
        _, top = lax.top_k(score, top_n)
        k_sel = ks_blk[bi, gi, top]
        v_sel = vs_blk[bi, gi, top]
        pos_sel = top[..., None] * Ls + jnp.arange(Ls)
        dist_s = (t[:, None, None] - pos_sel).astype(jnp.float32)[:, :, None]
        sc = jnp.einsum('bqgjd,bgqnld->bgjqnl', q_blk, k_sel).astype(jnp.float32) * scale
        sc = jnp.where(dist_s >= 0, sc - slopes[:, :, None, None, None] * dist_s, NEG_INF)
        p_s = jax.nn.softmax(sc.reshape(b, g, hpg, blk, top_n * Ls), axis=-1).reshape(sc.shape)
        o_s = jnp.einsum('bgjqnl,bgqnld->bqgjd', p_s.astype(v_sel.dtype), v_sel)
        k_w = lax.dynamic_slice_in_dim(kw_pad, i * blk, W + blk, axis=1)
        v_w = lax.dynamic_slice_in_dim(vw_pad, i * blk, W + blk, axis=1)
        pos_w = i * blk - W + jnp.arange(W + blk)
        dist_w = t[:, None] - pos_w[None, :]
        vis_w = (dist_w >= 0) & (dist_w < W) & (pos_w[None, :] >= 0)
        sc = jnp.einsum('bqgjd,bkgd->bgjqk', q_blk, k_w).astype(jnp.float32) * scale
        sc = jnp.where(vis_w, sc - slopes[:, :, None, None] * dist_w.astype(jnp.float32), NEG_INF)
        p_w = jax.nn.softmax(sc, axis=-1).astype(v_w.dtype)
        o_w = jnp.einsum('bgjqk,bkgd->bqgjd', p_w, v_w)
        o = g_blk[..., 0:1] * o_c + g_blk[..., 1:2] * o_s + g_blk[..., 2:3] * o_w
        return o.astype(x.dtype)

    o = merge_blocks(lax.map(attend, (jnp.arange(s // blk), split_blocks(q, blk), split_blocks(gates, blk))))
    return o.reshape(b, s, h * d) @ w_o

def diff_mixer(x, w_in, lam_q1, lam_k1, lam_q2, lam_k2, subln, w_o, layer_idx):
    b, s, _ = x.shape
    h, d = DIFF_HEADS, DIFF_HD
    q, k, v = jnp.split(x @ w_in, 3, axis=-1)
    q = q.reshape(b, s, h, 2, d)
    k = k.reshape(b, s, h, 2, d)
    v = v.reshape(b, s, h, 2 * d)
    lam_init = 0.8 - 0.6 * math.exp(-0.3 * layer_idx)
    f32 = jnp.float32
    lam = (jnp.exp(jnp.sum(lam_q1.astype(f32) * lam_k1.astype(f32)))
           - jnp.exp(jnp.sum(lam_q2.astype(f32) * lam_k2.astype(f32))) + lam_init)
    slopes = alibi_slopes(h)
    pos = jnp.arange(s)
    scale = d ** -0.5

    def attend(args):
        i, q_blk = args
        t = i * Q_BLOCK + jnp.arange(Q_BLOCK)
        dist = (t[:, None] - pos[None, :]).astype(f32)
        sc = jnp.einsum('bqhmd,bkhmd->bmhqk', q_blk, k).astype(f32) * scale
        sc = jnp.where(dist >= 0, sc - slopes[:, None, None] * dist, NEG_INF)
        p = jax.nn.softmax(sc, axis=-1)
        a = (p[:, 0] - lam * p[:, 1]).astype(v.dtype)
        return jnp.einsum('bhqk,bkhd->bqhd', a, v)

    o = merge_blocks(lax.map(attend, (jnp.arange(s // Q_BLOCK), split_blocks(q, Q_BLOCK))))
    o = rms_norm(o, subln, eps=1e-5) * (1.0 - lam_init)
    return o.reshape(b, s, h * 2 * d) @ w_o

def dilated_mixer(x, w_in, w_o):
    b, s, _ = x.shape
    h, d, blk = DIL_HEADS, DIL_HD, GATHER_BLOCK
    n_pat = len(DIL_PATTERNS)
    qkv = (x @ w_in).reshape(b, s, n_pat, 3, h, d)
    q = qkv[:, :, :, 0]
    k_pats = [qkv[:, :, p, 1] for p in range(n_pat)]
    v_pats = [qkv[:, :, p, 2] for p in range(n_pat)]
    slopes = alibi_slopes(h)
    scale = d ** -0.5

    def attend(args):
        i, q_blk = args
        t = i * blk + jnp.arange(blk)
        outs, maxes, denoms = [], [], []
        for p, (win, dil) in enumerate(DIL_PATTERNS):
            dist = np.arange(win // dil + 1) * dil
            idx = t[:, None] - dist[None, :]
            valid = idx >= 0
            idx = jnp.maximum(idx, 0)
            k_g = k_pats[p][:, idx]
            v_g = v_pats[p][:, idx]
            sc = jnp.einsum('bqhd,bqkhd->bhqk', q_blk[:, :, p], k_g).astype(jnp.float32) * scale
            sc = jnp.where(valid, sc - slopes[:, None, None] * jnp.asarray(dist, jnp.float32), NEG_INF)
            mx = jnp.max(sc, axis=-1)
            e = jnp.exp(sc - mx[..., None])
            den = jnp.sum(e, axis=-1)
            outs.append(jnp.einsum('bhqk,bqkhd->bqhd', (e / den[..., None]).astype(v_g.dtype), v_g))
            maxes.append(mx)
            denoms.append(den)
        m_all = jnp.max(jnp.stack(maxes), axis=0)
        wts = jnp.stack([den * jnp.exp(mx - m_all) for mx, den in zip(maxes, denoms)])
        wts = wts / jnp.sum(wts, axis=0)
        o = sum(jnp.swapaxes(wt, 1, 2)[..., None] * o_p for wt, o_p in zip(wts, outs))
        return o.astype(x.dtype)

    o = merge_blocks(lax.map(attend, (jnp.arange(s // blk), split_blocks(q, blk))))
    return o.reshape(b, s, h * d) @ w_o

def hier_moe(x, wg, bg, we, be, w1, w3, w2):
    b, s, dm = x.shape
    xt = x.reshape(b * s, dm)
    n = xt.shape[0]
    pg = jax.nn.softmax((xt @ wg + bg).astype(jnp.float32), axis=-1)
    g_top = jnp.argmax(pg, axis=-1)
    pg_top = jnp.take_along_axis(pg, g_top[:, None], axis=-1)[:, 0]
    le = jnp.einsum('nd,gde->nge', xt, we) + be
    le = jnp.take_along_axis(le, g_top[:, None, None], axis=1)[:, 0]
    pe = jax.nn.softmax(le.astype(jnp.float32), axis=-1)
    top_v, top_i = lax.top_k(pe, MOE_TOPK)
    top_v = top_v / jnp.sum(top_v, axis=-1, keepdims=True)
    expert_id = g_top[:, None] * MOE_EXPERTS_PER_GROUP + top_i
    gate = jnp.sum(jax.nn.one_hot(expert_id, MOE_EXPERTS, dtype=jnp.float32)
                   * (top_v * pg_top[:, None])[..., None], axis=1).astype(x.dtype)
    y = jnp.zeros_like(xt)
    for e in range(MOE_EXPERTS):
        hid = jax.nn.silu(xt @ w1[e]) * (xt @ w3[e])
        y = y + gate[:, e:e + 1] * (hid @ w2[e])
    return y.reshape(b, s, dm)

def setup_inputs(seed: int = 0) -> dict:
    key = jax.random.key(seed)
    keys = jax.random.split(key, 40)
    counter = iter(range(40))
    f32 = jnp.float32
    D = D_MODEL
    nA, nB, nC, nD = LAYERS_PER_MIXER

    def nrm(shape, std):
        return jax.random.normal(keys[next(counter)], shape, f32) * std

    def gain(shape):
        return 1.0 + nrm(shape, 0.02)

    return {
        'x': nrm((BATCH, SEQ, D), 1.0),
        'mla_w_in': nrm((nA, D, MLA_IN), D ** -0.5),
        'mla_q_norm': gain((nA, MLA_Q_RANK)),
        'mla_kv_norm': gain((nA, MLA_KV_RANK)),
        'mla_w_qb': nrm((nA, MLA_Q_RANK, MLA_HEADS * (MLA_NOPE + MLA_ROPE)), MLA_Q_RANK ** -0.5),
        'mla_w_kvb': nrm((nA, MLA_KV_RANK, MLA_HEADS * (MLA_NOPE + MLA_V)), MLA_KV_RANK ** -0.5),
        'mla_w_o': nrm((nA, MLA_HEADS * MLA_V, D), DN_BETA * (MLA_HEADS * MLA_V) ** -0.5),
        'nsa_w_in': nrm((nB, D, NSA_IN), D ** -0.5),
        'nsa_w_phi_k': nrm((nB, NSA_CMP_LEN * NSA_HD, NSA_HD), (NSA_CMP_LEN * NSA_HD) ** -0.5),
        'nsa_w_phi_v': nrm((nB, NSA_CMP_LEN * NSA_HD, NSA_HD), (NSA_CMP_LEN * NSA_HD) ** -0.5),
        'nsa_cmp_pos': nrm((nB, NSA_CMP_LEN, NSA_HD), 0.1),
        'nsa_w_o': nrm((nB, NSA_HEADS * NSA_HD, D), DN_BETA * (NSA_HEADS * NSA_HD) ** -0.5),
        'diff_w_in': nrm((nC, D, DIFF_IN), D ** -0.5),
        'diff_lam_q1': nrm((nC, DIFF_HD), 0.1),
        'diff_lam_k1': nrm((nC, DIFF_HD), 0.1),
        'diff_lam_q2': nrm((nC, DIFF_HD), 0.1),
        'diff_lam_k2': nrm((nC, DIFF_HD), 0.1),
        'diff_subln': gain((nC, 2 * DIFF_HD)),
        'diff_w_o': nrm((nC, DIFF_HEADS * 2 * DIFF_HD, D), DN_BETA * (DIFF_HEADS * 2 * DIFF_HD) ** -0.5),
        'dil_w_in': nrm((nD, D, DIL_IN), D ** -0.5),
        'dil_w_o': nrm((nD, DIL_HEADS * DIL_HD, D), DN_BETA * (DIL_HEADS * DIL_HD) ** -0.5),
        'ln1_g': gain((DEPTH, D)),
        'ln1_b': nrm((DEPTH, D), 0.02),
        'ln2_g': gain((DEPTH, D)),
        'ln2_b': nrm((DEPTH, D), 0.02),
        'moe_wg': nrm((DEPTH, D, MOE_GROUPS), D ** -0.5),
        'moe_bg': nrm((DEPTH, MOE_GROUPS), 0.01),
        'moe_we': nrm((DEPTH, MOE_GROUPS, D, MOE_EXPERTS_PER_GROUP), D ** -0.5),
        'moe_be': nrm((DEPTH, MOE_GROUPS, MOE_EXPERTS_PER_GROUP), 0.01),
        'moe_w1': nrm((DEPTH, MOE_EXPERTS, D, MOE_FF), D ** -0.5),
        'moe_w3': nrm((DEPTH, MOE_EXPERTS, D, MOE_FF), D ** -0.5),
        'moe_w2': nrm((DEPTH, MOE_EXPERTS, MOE_FF, D), DN_BETA * MOE_FF ** -0.5),
    }

def reference(x, mla_w_in, mla_q_norm, mla_kv_norm, mla_w_qb, mla_w_kvb, mla_w_o,
              nsa_w_in, nsa_w_phi_k, nsa_w_phi_v, nsa_cmp_pos, nsa_w_o,
              diff_w_in, diff_lam_q1, diff_lam_k1, diff_lam_q2, diff_lam_k2, diff_subln, diff_w_o,
              dil_w_in, dil_w_o,
              ln1_g, ln1_b, ln2_g, ln2_b,
              moe_wg, moe_bg, moe_we, moe_be, moe_w1, moe_w3, moe_w2):
    for i in range(DEPTH):
        m, j = i % N_MIXERS, i // N_MIXERS
        if m == 0:
            y = mla_mixer(x, mla_w_in[j], mla_q_norm[j], mla_kv_norm[j], mla_w_qb[j], mla_w_kvb[j], mla_w_o[j])
        elif m == 1:
            y = nsa_mixer(x, nsa_w_in[j], nsa_w_phi_k[j], nsa_w_phi_v[j], nsa_cmp_pos[j], nsa_w_o[j])
        elif m == 2:
            y = diff_mixer(x, diff_w_in[j], diff_lam_q1[j], diff_lam_k1[j], diff_lam_q2[j], diff_lam_k2[j],
                           diff_subln[j], diff_w_o[j], i)
        else:
            y = dilated_mixer(x, dil_w_in[j], dil_w_o[j])
        x = layer_norm(DN_ALPHA * x + y, ln1_g[i], ln1_b[i])
        y = hier_moe(x, moe_wg[i], moe_bg[i], moe_we[i], moe_be[i], moe_w1[i], moe_w3[i], moe_w2[i])
        x = layer_norm(DN_ALPHA * x + y, ln2_g[i], ln2_b[i])
    return x


_drawn_inputs = setup_inputs


def setup_inputs(seed=0):
    import zlib

    import numpy as np

    out = dict(_drawn_inputs(seed))
    spreads = {}
    factors = {'mla_q_norm': 8.0,
     'mla_kv_norm': 8.0,
     'nsa_cmp_pos': 3.23,
     'moe_bg': 23.869,
     'moe_be': 21.959}
    for name, (base, spread) in spreads.items():
        noise = np.random.default_rng([zlib.crc32(name.encode()), seed]).standard_normal(out[name].shape)
        drawn = base * np.exp(spread * noise) if base else spread * noise
        out[name] = __import__('jax').numpy.asarray(drawn.astype(out[name].dtype))
    for name, factor in factors.items():
        out[name] = (out[name] * factor).astype(out[name].dtype)
    return out
```

```python
from contextlib import ExitStack

import numpy as np

import concourse.bass as bass
from concourse import mybir

F32 = mybir.dt.float32
I32 = mybir.dt.int32
ALU = mybir.AluOpType
ACT = mybir.ActivationFunctionType
AX = mybir.AxisListType.X

P = 128
S = 256
NT = S // P
D = 1024
KD = D // P
DEPTH = 2
ALPHA = (2.0 * DEPTH) ** 0.25
LN_EPS = 1e-5
RMS_EPS = 1e-6
NEG = -1e30
H = 16
QR, KVR, NOPE, ROPE, VD = 384, 256, 64, 32, 64
CQ, CKV = QR // P, KVR // P
LAT = QR + KVR + ROPE
DQ = NOPE + ROPE
MLA_SCALE = DQ ** -0.5
HD = 64
G = 4
HPG = H // G
CMP_LEN, CMP_STRIDE = 32, 16
NCMP = (S - CMP_LEN) // CMP_STRIDE + 1
CMP_PAD = 32
NSA_SCALE = HD ** -0.5
NSA_COLS = 512
NGATE = 3 * H
NE = 16
NG = 4
EPG = NE // NG
FF = 512
KF = FF // P
CAP = 64
PAIRS = NE // 2
NR = NG + NE
RING = 6
SLOT = 4096
NB = 512

C_ID = 0
C_AID = C_ID + P
C_TRI = C_AID + P
C_MASK = C_TRI + P
C_IOTA = C_MASK + 3 * P
C_DESC = C_IOTA + CAP
C_COS = C_DESC + EPG
C_SIN = C_COS + NT * ROPE // 2
C_CB = C_SIN + NT * ROPE // 2
C_VIS = C_CB + NT * H * NCMP
C_END = C_VIS + NT


def shape_constants():
    c = np.zeros((P, C_END), np.float32)
    p = np.arange(P)
    c[:, C_ID:C_ID + P] = np.eye(P)
    c[:, C_AID:C_AID + P] = np.eye(P) * ALPHA
    c[:, C_TRI:C_TRI + P] = p[:, None] < p[None, :]
    causal = np.where(p[None, :] <= p[:, None], 0.0, NEG)
    c[:, C_MASK:C_MASK + P] = causal
    c[:, C_MASK + 2 * P:C_MASK + 3 * P] = causal
    c[:, C_IOTA:C_IOTA + CAP] = np.arange(CAP)
    c[:, C_DESC:C_DESC + EPG] = EPG - np.arange(EPG)
    half = ROPE // 2
    freq = np.float32(10000.0) ** (-np.arange(half, dtype=np.float32) / half)
    tok = (np.arange(NT)[None, :] * P + p[:, None])
    ang = tok[:, :, None].astype(np.float32) * freq
    c[:, C_COS:C_SIN] = np.cos(ang).reshape(P, -1)
    c[:, C_SIN:C_CB] = np.sin(ang).reshape(P, -1)
    slopes = (2.0 ** (-8.0 * np.arange(1, H + 1) / H)).astype(np.float32)
    end = np.arange(NCMP) * CMP_STRIDE + CMP_LEN - 1
    dist = (tok[:, :, None] - end).astype(np.float32)
    cb = np.where(dist[:, :, None, :] >= 0, -slopes[:, None] * dist[:, :, None, :], NEG)
    c[:, C_CB:C_VIS] = cb.reshape(P, -1)
    c[:, C_VIS:C_END] = (dist >= 0).any(-1)
    parts = []
    for t in range(NT):
        d = (tok[:, t, None] - np.arange((t + 1) * P)).astype(np.float32)
        parts.append(np.where(d[:, None, :] >= 0, -slopes[:, None] * d[:, None, :], NEG).reshape(P, -1))
    return c, np.concatenate(parts, 1).astype(np.float32)


class PsumPlan:

    def __init__(self):
        self.count = [0] * 8
        self.at = {}

    def add(self, name, bank):
        self.count[bank] += 1
        self.at[name] = (bank, self.count[bank], 0)

    def add_loop(self, names_banks, iterations):
        per = [sum(1 for _, b in names_banks if b == k) for k in range(8)]
        seen = [0] * 8
        for name, bank in names_banks:
            seen[bank] += 1
            self.at[name] = (bank, self.count[bank] + seen[bank], per[bank])
        for k in range(8):
            self.count[k] += per[k] * iterations


def psum_plan():
    plan = PsumPlan()

    def transposed(name):
        for s in range(4):
            plan.add(f"{name}{s}", s)

    def experts(l):
        plan.add(f"logits{l}", 4)
        plan.add(f"position{l}", 5)
        plan.add(f"overflow{l}", 6)
        plan.add(f"gather_a{l}", 2)
        plan.add(f"gather_b{l}", 3)
        names = [("h1", 0), ("h3", 1), ("next_a", 2), ("next_b", 3), ("hidT", 0), ("scatT", 1), ("w2_0", 2), ("w2_1", 3)]
        plan.add_loop([(f"{n}.{l}", b) for n, b in names], PAIRS - 1)
        for n, b in names:
            if not n.startswith("next"):
                plan.add(f"{n}.{l}last", b)
        for q in range(4):
            plan.add(f"moe_y{l}{q}", 4 + q)

    for q in range(4):
        plan.add(f"lat{q}", q)
    for q in range(3):
        plan.add(f"latT{q}", 4 + q)
    for o in range(14):
        plan.add(f"qkv{o}", (o + 7) % 8)
    for step in range(H + 3):
        if step < H:
            plan.add(f"headT{step}", 0)
        if 1 <= step <= H:
            plan.add(f"score{step - 1}", 1 + (step - 1) % 2)
        if 2 <= step <= H + 1:
            plan.add(f"probT{step - 2}", 3)
    for q in range(4):
        plan.add(f"mla_o{q}", 4 + q)
    transposed("mla_oT")
    for q in range(4):
        plan.add(f"mla_y{q}", 4 + q)
    transposed("x1T")
    experts(0)
    transposed("x2T")
    for q in range(4):
        plan.add(f"nq{q}", 4 + q)
    for n, b in (("kc", 0), ("vc", 1), ("ks", 2), ("vs", 3), ("kw", 4), ("vw", 5), ("gate", 6),
                 ("kcmp0", 7), ("kcmp1", 0), ("vcmp0", 1), ("vcmp1", 2), ("cs0", 3), ("cs1", 4), ("pcT0", 5), ("pcT1", 6)):
        plan.add(n, b)
    for n in range(NT * H):
        plan.add(f"nscore{n}", n % 2)
        plan.add(f"nprobT{n}", 2 + n % 2)
    for q in range(4):
        plan.add(f"nsa_o{q}", 4 + q)
    transposed("nsa_oT")
    for q in range(4):
        plan.add(f"nsa_y{q}", 4 + q)
    transposed("x3T")
    experts(1)
    return plan


MLA_LOADS = 6
NSA_LOADS = 8
MOE_LOADS = 6 * PAIRS
LOAD0 = {"mla": 0, "moe0": MLA_LOADS, "nsa": MLA_LOADS + MOE_LOADS, "moe1": MLA_LOADS + MOE_LOADS + NSA_LOADS}
MLA_DONE = ["lat3", "qkv5", "qkv5", "qkv13", "mla_y3", "mla_y3"]
NSA_DONE = ["nq1", "nq3", "vc", "vs", "vw", "vcmp1", "nsa_y3", "nsa_y3"]
PAIR_DONE = ["h1", "h1", "h3", "h3", "w2_1", "w2_1"]


def build(nc, a):
    plan = psum_plan()
    with ExitStack() as ctx:
        def sb(name, cols, dt=F32):
            return ctx.enter_context(nc.sbuf_tensor(name, [P, cols], dt))

        def sem(name):
            return ctx.enter_context(nc.semaphore(name))

        ring = sb("ring", RING * SLOT)
        const = sb("const", C_END)
        x_t = sb("x_tok", NT * D)
        xT_t = sb("xT", KD * S)
        lnp = sb("ln_params", 2 * D)
        small = sb("small", 640)
        counts = sb("counts", 4, I32)
        WORK = 19060
        work = sb("work", WORK)
        bank = [ctx.enter_context(nc.psum_tensor(f"bank{b}", [P, NB], F32)) for b in range(8)]

        class Region:
            def __init__(self, base, at=0):
                self.base, self.at = base, at

            def take(self, cols):
                self.at += cols
                assert self.at <= self.base.shape[1], (self.at, self.base.shape)
                return self.base[:, self.at - cols:self.at]

        def slot(s):
            return ring[:, s * SLOT:(s + 1) * SLOT]

        ident = const[:, C_ID:C_ID + P]
        alpha_ident = const[:, C_AID:C_AID + P]
        tri = const[:, C_TRI:C_TRI + P]
        mask3 = const[:, C_MASK:C_MASK + 3 * P]
        iota = const[:, C_IOTA:C_IOTA + CAP]
        desc = const[:, C_DESC:C_DESC + EPG]
        cos = const[:, C_COS:C_SIN].rearrange("p (t f) -> p t f", t=NT)
        sin = const[:, C_SIN:C_CB].rearrange("p (t f) -> p t f", t=NT)
        cmp_bias = const[:, C_CB:C_VIS].rearrange("p (t h n) -> p t h n", t=NT, h=H)
        any_visible = const[:, C_VIS:C_END]
        x_tok = x_t[:, :].rearrange("p (t d) -> p t d", t=NT)
        xT = xT_t[:, :].rearrange("p (k s) -> p k s", k=KD)
        gain, shift = lnp[:, 0:D], lnp[:, D:2 * D]

        sm = Region(small)
        bn = sm.take(NT * 2 * 6).rearrange("p (t c s) -> p t c s", t=NT, c=2)
        mv = sm.take(NT * 2).rearrange("p (t s) -> p t s", t=NT)
        var_eps = sm.take(4)
        neg_half = sm.take(4)
        rstd = sm.take(4)
        sumsq = sm.take(4)
        rms = sm.take(4)
        rms_gain = sm.take(CQ + CKV)
        router_b = sm.take(NR)
        ones = sb("ones", P)
        lg = sm.take(NT * NR).rearrange("p (t c) -> p t c", t=NT)

        def per_token(cols):
            return sm.take(NT * cols).rearrange("p (t c) -> p t c", t=NT)
        r1, r2, pg_top = per_token(1), per_token(1), per_token(1)
        e4, p4, k4, group1h = per_token(4), per_token(4), per_token(4), per_token(4)
        first1h, second1h, gate4 = per_token(4), per_token(4), per_token(4)
        v1, v2 = per_token(1), per_token(1)
        m4 = per_token(4)
        prod16 = per_token(NE)
        member = per_token(NE)
        gates = per_token(NE)
        posm = per_token(NE)
        over = per_token(NE)
        rest_gates = per_token(NE)
        router_w = sb("router_w", KD * NR)
        rw = router_w[:, :].rearrange("p (k c) -> p k c", k=KD)

        m = Region(work)
        q_tok = m.take(NT * H * DQ)
        k_tok = m.take(NT * H * DQ)
        v_tok = m.take(NT * H * VD)
        lat = m.take(NT * LAT)
        latT = m.take((CQ + CKV) * S)
        mo = m.take(NT * D)
        m_spt = m.take(6 * 3 * P)
        m_s = [m_spt[:, i * 3 * P:(i + 1) * 3 * P] for i in range(4)]
        m_pt = [m_spt[:, i * 3 * P:(i + 1) * 3 * P] for i in (4, 5)]
        RT = NT * H * ROPE // 2
        rt = [m_spt[:, i * RT:(i + 1) * RT] for i in range(4)]
        m_qk = [m.take(2 * S) for _ in range(4)]
        m_z = m.take(NT * H)
        m_rz = m.take(NT * H)
        m_mx = m.take(H * NT)
        m_nm = m.take(H * NT)
        m_oT = q_tok[:, 0:KD * S]
        q4 = q_tok.rearrange("p (t h d) -> p t h d", t=NT, h=H)
        k4d = k_tok.rearrange("p (t h d) -> p t h d", t=NT, h=H)
        v4 = v_tok.rearrange("p (t h d) -> p t h d", t=NT, h=H)
        lat3 = lat.rearrange("p (t c) -> p t c", t=NT)
        latT3 = latT.rearrange("p (j s) -> p j s", j=CQ + CKV)
        mo3 = mo.rearrange("p (t d) -> p t d", t=NT)
        z3 = m_z.rearrange("p (t h) -> p t h", t=NT)
        rz3 = m_rz.rearrange("p (t h) -> p t h", t=NT)
        mx3 = m_mx.rearrange("p (h t) -> p h t", h=H)
        nm3 = m_nm.rearrange("p (h t) -> p h t", h=H)
        moT = m_oT.rearrange("p (k s) -> p k s", k=KD)

        n = Region(work)
        nqT_f = n.take(H // 2 * S)
        kall_f = n.take(G * 2 * S)
        kct_f = n.take(G * 16)
        vsw_f = n.take(2 * NT * G * HD)
        ab_f = n.take(4 * 2 * S)
        vbd_f = n.take(G * HPG * HD)
        alibi_f = n.take(H * P + H * S)
        pct_f = n.take(NT * G * P)
        n_s4 = n.take(4 * 2 * S)
        n_s = [n_s4[:, i * 2 * S:(i + 1) * 2 * S] for i in range(4)]
        sc_f = n_s4[:, 0:NT * H * CMP_PAD]
        n_pt = [n.take(2 * S) for _ in range(2)]
        gate_w = n.take(KD * NGATE)
        nqT = nqT_f.rearrange("p (i s) -> p i s", i=H // 2)
        kall = kall_f.rearrange("p (g b s) -> p g b s", g=G, b=2)
        kct = kct_f.rearrange("p (g n) -> p g n", g=G)
        vsw = vsw_f.rearrange("p (b t c) -> p b t c", b=2, t=NT)
        ab = ab_f.rearrange("p (w q s) -> p w q s", w=4, q=2)
        no3 = ab_f.rearrange("p (t d) -> p t d", t=NT)
        noT = nqT_f.rearrange("p (k s) -> p k s", k=KD)
        vbd = vbd_f.rearrange("p (g c) -> p g c", g=G)
        alibi = [alibi_f[:, 0:H * P].rearrange("p (h s) -> p h s", h=H),
                 alibi_f[:, H * P:].rearrange("p (h s) -> p h s", h=H)]
        sc = sc_f.rearrange("p (r c) -> p r c", c=CMP_PAD)
        pct = pct_f.rearrange("p (r c) -> p r c", c=P)
        gw = gate_w.rearrange("p (k c) -> p k c", k=KD)
        nsm = sb("nsa_small", 520)
        ns = Region(nsm)
        n_gate = ns.take(NT * NGATE)
        n_mx = ns.take(NT * H * 2)
        n_nm = ns.take(NT * H * 2)
        n_z = ns.take(NT * H * 2)
        n_rz = ns.take(NT * H * 2)
        n_cf = ns.take(NT * H * 2)
        c_mx = ns.take(NT * H)
        c_z = ns.take(NT * H)
        c_cf = ns.take(NT * H)
        pos_t = sb("cmp_posT", CMP_LEN)
        gate3 = n_gate.rearrange("p (r b) -> p r b", b=3)
        v3 = {k: v.rearrange("p (r b) -> p r b", b=2) for k, v in
              dict(mx=n_mx, nm=n_nm, z=n_z, rz=n_rz, cf=n_cf).items()}

        e = Region(work)
        xe_f = e.take(KD * 2 * CAP)
        xe = xe_f.rearrange("p (k c) -> p k c", k=KD)
        pick_f = e.take(NT * 2 * CAP)
        pick = pick_f.rearrange("p (t c) -> p t c", t=NT)
        scat_f = e.take(NT * 2 * CAP)
        scat = scat_f.rearrange("p (t c) -> p t c", t=NT)
        scatT_f = e.take(NT * P)
        silu = e.take(FF)
        hid = e.take(FF)
        hidT_f = e.take(KF * P)
        hidT = hidT_f.rearrange("p (c s) -> p c s", c=KF)
        ye = e.take(D)

        bank_filled = [sem(f"bank{b}_filled") for b in range(8)]
        bank_drained = [sem(f"bank{b}_drained") for b in range(8)]
        slot_loaded = [sem(f"slot{s}_loaded") for s in range(RING)]
        xT_loaded, x_loaded, const_loaded = sem("xT_loaded"), sem("x_loaded"), sem("const_loaded")
        w_qb2_loaded = sem("w_qb_last_chunk_loaded")
        rms_loaded, router_loaded, ln_loaded = sem("rms_loaded"), sem("router_loaded"), sem("ln_loaded")
        nsa_loaded = sem("nsa_tables_loaded")
        consts_set = sem("consts_set")
        dve_step, act_step = sem("dve_step"), sem("act_step")
        var_ready, rstd_ready = sem("variance_ready"), sem("rstd_ready")
        x_ready = sem("x_ready")
        sumsq_ready = sem("sumsq_ready")
        lat_ready, rope_ready = sem("latents_ready"), sem("rope_ready")
        score_ready, prob_ready, pv_done = sem("scores_ready"), sem("probs_ready"), sem("pv_done")
        logit_exp_in, logit_exp_out = sem("router_exp_in"), sem("router_exp_out")
        member_ready, over_ready, count_ready = sem("member_ready"), sem("over_ready"), sem("count_ready")
        pick_ready, scat_ready, silu_ready, scattered = sem("pick_ready"), sem("scat_ready"), sem("silu_ready"), sem("scattered")
        gate_exp_ready = sem("gate_exp_ready")
        cmp_in, cmp_exp, cmp_prob = sem("cmp_scores_ready"), sem("cmp_exp_ready"), sem("cmp_probs_ready")
        raw_prob, nscore_ready, nprob_ready, npv_done = sem("raw_probs"), sem("nsa_scores_ready"), sem("nsa_probs_ready"), sem("nsa_pv_done")
        rest = [{k: sem(f"rest{l}_{k}") for k in ("loaded", "h", "silu", "hid", "hidT", "hidT_copied", "w2", "added")}
                for l in range(DEPTH)]
        out_written = sem("out_written")

        def number(name, i):
            b, first, per = plan.at[name]
            return b, first if i is None or not per else first + per * i

        def filled(eng, name, i=None):
            b, k = number(name, i)
            eng.wait_ge(bank_filled[b], k)

        def drained(eng, name, i=None):
            b, k = number(name, i)
            eng.wait_ge(bank_drained[b], k)

        def may_fill(eng, name, i=None):
            b, k = number(name, i)
            if not (isinstance(k, int) and k == 1):
                eng.wait_ge(bank_drained[b], k - 1)

        def fill(ins, name):
            ins.then_inc(bank_filled[plan.at[name][0]], 1)

        def drain(ins, name):
            ins.then_inc(bank_drained[plan.at[name][0]], 1)

        def bk(name):
            return bank[plan.at[name][0]]

        class Steps:

            def __init__(self, eng, sem_):
                self.eng, self.sem, self.n = eng, sem_, 0

            def __call__(self, ins):
                ins.then_inc(self.sem, 1)
                self.n += 1

            def wait(self):
                self.eng.wait_ge(self.sem, self.n)

        def loaded(eng, j, i=None, per=1):
            k = 16 * (j // RING + 1)
            eng.wait_ge(slot_loaded[j % RING], k if i is None else k + 16 * per * i)

        block = ctx.enter_context(nc.Block())
        w_in = a["mla_w_in"].rearrange("(p k) n -> p k n", k=KD)
        w_qb = a["mla_w_qb"].rearrange("(p c) n -> p c n", c=CQ)
        w_kvb = a["mla_w_kvb"].rearrange("(p c) n -> p (c n)", c=CKV)
        w_o = [a[k].rearrange("(p k) n -> p k n", k=KD) for k in ("mla_w_o", "nsa_w_o")]
        n_in = a["nsa_w_in"].rearrange("(p k) n -> p k n", k=KD)
        w1 = a["moe_w1"].rearrange("e (p k) n -> e p (k n)", k=KD)
        w3 = a["moe_w3"].rearrange("e (p k) n -> e p (k n)", k=KD)
        w2 = a["moe_w2"].rearrange("e (p c) n -> e p (c n)", c=KF)
        KA = SLOT // LAT
        KB = KD - KA

        def s3(s, cols, chunks, off=0):
            return ring[:, s * SLOT + off:s * SLOT + off + cols * chunks].rearrange("p (k n) -> p k n", k=chunks)

        def at_expert(w, idx):
            return w[bass.ds(idx, 1), :, :].rearrange("o p n -> (o p) n")

        def qkv_copy(eng, copy, o):
            nm = f"qkv{o}"
            b = bk(nm)
            if o < 6:
                t, nn = divmod(o, 3)
                drain(copy(q_tok[:, (t * 3 + nn) * NB:(t * 3 + nn + 1) * NB], b[:, :]), nm)
            else:
                t, nn = divmod(o - 6, 4)
                src = b[:, :].rearrange("p (h d) -> p h d", h=4)
                copy(k4d[:, t, 4 * nn:4 * nn + 4, 0:NOPE], src[:, :, 0:NOPE])
                drain(copy(v4[:, t, 4 * nn:4 * nn + 4, :], src[:, :, NOPE:]), nm)

        def mla_pv_done(eng, h):
            if h % 8 == 7:
                filled(eng, f"mla_o{2 + h // 8}")
            else:
                eng.wait_ge(pv_done, h + 1 - h // 8)

        def nsa_pv_done(eng, r):
            if r % 8 == 7:
                filled(eng, f"nsa_o{r // 8}")
            else:
                eng.wait_ge(npv_done, r + 1 - r // 8)

        @block.sync
        def _(sp):
            def done_name(j):
                if j < LOAD0["moe0"]:
                    return MLA_DONE[j], None
                for l, key in enumerate(("moe0", "moe1")):
                    r = j - LOAD0[key]
                    if 0 <= r < MOE_LOADS:
                        nm = f"{PAIR_DONE[r % 6]}.{l}"
                        return (nm + "last", None) if r // 6 == PAIRS - 1 else (nm, r // 6)
                return NSA_DONE[j - LOAD0["nsa"]], None

            def free(j):
                if j >= RING:
                    nm, i = done_name(j - RING)
                    filled(sp, nm, i)

            def load(j, out, in_):
                free(j)
                sp.dma_start(out, in_).then_inc(slot_loaded[j % RING], 16)

            sp.dma_start(xT_t[:, :], a["xT"]).then_inc(xT_loaded, 16)
            sp.dma_start(s3(0, LAT, KA), w_in[:, 0:KA, :]).then_inc(slot_loaded[0], 16)
            sp.dma_start(s3(1, LAT, KB), w_in[:, KA:KD, :]).then_inc(slot_loaded[1], 16)
            sp.dma_start(s3(1, H * DQ, 1, off=KB * LAT), w_qb[:, 2:3, :]).then_inc(w_qb2_loaded, 16)
            sp.dma_start(s3(2, H * DQ, 2), w_qb[:, 0:2, :]).then_inc(slot_loaded[2], 16)
            sp.dma_start(slot(3), w_kvb).then_inc(slot_loaded[3], 16)
            sp.dma_start(s3(4, D, 4), w_o[0][:, 0:4, :]).then_inc(slot_loaded[4], 16)
            sp.dma_start(s3(5, D, 4), w_o[0][:, 4:8, :]).then_inc(slot_loaded[5], 16)

            def pair_loads(l, j0, i, expert):
                for s in range(6):
                    w = (w1, w1, w3, w3, w2, w2)[s]
                    j = j0 + s
                    if i is None:
                        free(j)
                    else:
                        filled(sp, f"{PAIR_DONE[s]}.{l}", i)
                    sp.dma_start(slot(j % RING), at_expert(w, expert + s % 2)).then_inc(slot_loaded[j % RING], 16)

            def experts(l):
                j0 = LOAD0[f"moe{l}"]
                pair_loads(l, j0, None, l * NE)
                with sp.Fori(0, PAIRS - 1) as i:
                    pair_loads(l, j0 + RING, i, i * 2 + (l * NE + 2))

            def rest_of_tokens(l):
                r = rest[l]
                sp.wait_ge(count_ready, l + 1)
                total = sp.value_load(counts[0:1, l:l + 1], min_val=0, max_val=S * 2)
                with sp.If(total > 0):
                    filled(sp, f"w2_1.{l}last")
                    with sp.Fori(0, NE) as i:
                        sp.wait_ge(r["added"], i * NT + 1)
                        for s, w in enumerate((w1, w3, w2)):
                            sp.dma_start(slot(s), at_expert(w, i + l * NE)).then_inc(r["loaded"], 16)
                    sp.wait_ge(r["added"], NE * NT + 1)
                sp.nop()

            experts(0)
            rest_of_tokens(0)
            j = LOAD0["nsa"]
            for c in range(5):
                load(j + c, s3((j + c) % RING, NSA_COLS, KD), n_in[:, :, c * NSA_COLS:(c + 1) * NSA_COLS])
            load(j + 5, slot((j + 5) % RING), a["phi"])
            load(j + 6, s3((j + 6) % RING, D, 4), w_o[1][:, 0:4, :])
            load(j + 7, s3((j + 7) % RING, D, 4), w_o[1][:, 4:8, :])
            experts(1)
            rest_of_tokens(1)
            for t in range(NT):
                sp.wait_ge(x_ready, 3 * NT + t + 1)
                sp.dma_start(a["out"][t * P:(t + 1) * P, :], x_tok[:, t, :]).then_inc(out_written, 16)
            sp.wait_ge(out_written, 16 * NT)

        @block.gpsimd
        def _(pool):
            pool.dma_start(const[:, :], a["const"]).then_inc(const_loaded, 16)
            pool.dma_start(rms_gain, a["rms_gain"]).then_inc(rms_loaded, 16)
            pool.dma_start(x_tok, a["x"].rearrange("(t p) d -> p t d", t=NT)).then_inc(x_loaded, 16)
            pool.memset(neg_half, -0.5).then_inc(consts_set, 1)
            pool.memset(ones[:, :], 1.0).then_inc(consts_set, 1)

            def load_router(l):
                pool.dma_start(router_w[:, :], a["router_w"][l]).then_inc(router_loaded, 16)
                pool.dma_start(router_b, a["router_b"][l:l + 1, :].to_broadcast([P, NR])).then_inc(router_loaded, 16)

            def load_ln(k):
                if k:
                    pool.wait_ge(x_ready, NT * k)
                pool.dma_start(gain, a["ln"][2 * k:2 * k + 1, :].to_broadcast([P, D])).then_inc(ln_loaded, 16)
                pool.dma_start(shift, a["ln"][2 * k + 1:2 * k + 2, :].to_broadcast([P, D])).then_inc(ln_loaded, 16)

            pool.wait_ge(consts_set, 2)

            def inverse_root(k, out, in_):
                pool.wait_ge(var_ready, k + 1)
                pool.tensor_tensor(out, in_, neg_half[:, 0:out.shape[1]], ALU.pow).then_inc(rstd_ready, 1)

            load_ln(0)
            load_router(0)
            inverse_root(0, rms, sumsq)
            inverse_root(1, rstd[:, 0:NT], var_eps[:, 0:NT])
            load_ln(1)
            inverse_root(2, rstd[:, 0:NT], var_eps[:, 0:NT])
            load_ln(2)
            load_router(1)
            pool.dma_start(alibi_f, a["alibi"]).then_inc(nsa_loaded, 16)
            pool.dma_start(gate_w, a["nsa_gate_w"]).then_inc(nsa_loaded, 16)
            pool.dma_start(pos_t[:, :], a["cmp_posT"]).then_inc(nsa_loaded, 16)
            inverse_root(3, rstd[:, 0:NT], var_eps[:, 0:NT])
            load_ln(3)
            inverse_root(4, rstd[:, 0:NT], var_eps[:, 0:NT])

        @block.tensor
        def _(pe):
            def transposes(name, src, k0=0):
                for s in range(4):
                    t, kh = divmod(s, 2)
                    may_fill(pe, f"{name}{s}")
                    for c in range(4):
                        ins = pe.transpose(bk(f"{name}{s}")[:, c * P:(c + 1) * P], src[:, t, 4 * kh + c::KD], ident)
                    fill(ins, f"{name}{s}")

            def out_projection(name, j, srcT, ready):
                for s in range(4):
                    drained(pe, f"{ready}{s}")
                for q in range(4):
                    may_fill(pe, f"{name}{q}")
                for k in range(KD):
                    if k % 4 == 0:
                        loaded(pe, j + k // 4)
                    w = s3((j + k // 4) % RING, D, 4)
                    for q in range(4):
                        t, half = divmod(q, 2)
                        ins = pe.matmul(bk(f"{name}{q}")[:, :], srcT[:, k, t * P:(t + 1) * P],
                                        w[:, k % 4, half * NB:(half + 1) * NB], start=(k == 0), stop=(k == KD - 1))
                        if k == KD - 1:
                            fill(ins, f"{name}{q}")

            def experts(l, xname):
                for s in range(4):
                    drained(pe, f"{xname}{s}")
                pe.wait_ge(router_loaded, 32 * (l + 1))
                may_fill(pe, f"logits{l}")
                for t in range(NT):
                    for k in range(KD):
                        ins = pe.matmul(bk(f"logits{l}")[:, t * NR:(t + 1) * NR], xT[:, k, t * P:(t + 1) * P], rw[:, k, :],
                                        start=(k == 0), stop=(k == KD - 1))
                fill(ins, f"logits{l}")
                pe.wait_ge(member_ready, l + 1)
                may_fill(pe, f"position{l}")
                pos = bk(f"position{l}")
                pe.matmul(pos[:, 0:NE], tri, member[:, 0, :], start=True, stop=True)
                pe.matmul(pos[:, NE:2 * NE], ones[:, :], member[:, 0, :], start=True, stop=False)
                fill(pe.matmul(pos[:, NE:2 * NE], tri, member[:, 1, :], start=False, stop=True), f"position{l}")
                pe.wait_ge(over_ready, l + 1)
                may_fill(pe, f"overflow{l}")
                fill(pe.matmul(bk(f"overflow{l}")[:, 0:NT * NE], ones[:, :], over.rearrange("p t c -> p (t c)"),
                               start=True, stop=True), f"overflow{l}")

                def gather(names, i, first):
                    for half, nm in enumerate(names):
                        may_fill(pe, nm, i)
                        for c in range(4):
                            for t in range(NT):
                                ins = pe.matmul(bk(nm)[:, c * P:(c + 1) * P], x_tok[:, t, 4 * half + c::KD], pick[:, t, :],
                                                start=(t == 0), stop=(t == NT - 1))
                        fill(ins, nm)

                pe.wait_ge(pick_ready, l * PAIRS + 1)
                gather((f"gather_a{l}", f"gather_b{l}"), None, True)
                for q in range(4):
                    t, half = divmod(q, 2)
                    may_fill(pe, f"moe_y{l}{q}")
                    ins = pe.matmul(bk(f"moe_y{l}{q}")[:, :], alpha_ident, x_tok[:, t, half * NB:(half + 1) * NB],
                                    start=True, stop=False, skip_group_check=True)
                ins.then_inc(scattered, 1)
                j0 = LOAD0[f"moe{l}"]

                def two_experts(out, src, ws, chunks, cols):
                    for k in range(chunks):
                        for x in range(2):
                            ins = pe.matmul(out[CAP * x:CAP * (x + 1), :], src[:, k, CAP * x:CAP * (x + 1)],
                                            ws[x][:, k, cols], start=(k == 0), stop=(k == chunks - 1))
                    return ins

                def pair(i, tag, last):
                    j = j0 if not last else j0 + RING * (PAIRS - 1)
                    n_ = [f"{k}.{l}{tag}" for k in ("h1", "h3", "hidT", "scatT", "w2_0", "w2_1")]
                    h1, h3, hT, sT, y0, y1 = n_

                    def slots(a_, b_, cols, chunks):
                        loaded(pe, j + a_, i)
                        loaded(pe, j + b_, i)
                        return [s3((j + a_) % RING, cols, chunks), s3((j + b_) % RING, cols, chunks)]

                    may_fill(pe, h1, i)
                    ws = slots(0, 1, FF, KD)
                    fill(two_experts(bk(h1), xe, ws, KD, slice(0, FF)), h1)
                    may_fill(pe, h3, i)
                    ws = slots(2, 3, FF, KD)
                    fill(two_experts(bk(h3), xe, ws, KD, slice(0, FF)), h3)
                    if not last:
                        pe.wait_ge(pick_ready, i + (l * PAIRS + 2))
                        gather((f"next_a.{l}", f"next_b.{l}"), i, False)
                    drained(pe, h3, i)
                    may_fill(pe, hT, i)
                    for c in range(KF):
                        ins = pe.transpose(bk(hT)[:, c * P:(c + 1) * P], hid[:, c::KF], ident)
                    fill(ins, hT)
                    pe.wait_ge(scat_ready, l * PAIRS + PAIRS if last else i + (l * PAIRS + 1))
                    may_fill(pe, sT, i)
                    for t in range(NT):
                        ins = pe.transpose(bk(sT)[:, t * P:(t + 1) * P], scat[:, t, :], ident)
                    fill(ins, sT)
                    drained(pe, hT, i)
                    ws = slots(4, 5, D, KF)
                    for half, nm in enumerate((y0, y1)):
                        may_fill(pe, nm, i)
                        fill(two_experts(bk(nm), hidT, ws, KF, slice(half * NB, (half + 1) * NB)), nm)
                    drained(pe, sT, i)
                    for half, nm in enumerate((y0, y1)):
                        drained(pe, nm, i)
                        for t in range(NT):
                            q = 2 * t + half
                            ins = pe.matmul(bk(f"moe_y{l}{q}")[:, :], scatT_f[:, t * P:(t + 1) * P],
                                            ye[:, half * NB:(half + 1) * NB], start=False, stop=last, skip_group_check=True)
                            if last:
                                fill(ins, f"moe_y{l}{q}")
                    if not last:
                        ins.then_inc(scattered, 1)

                for nm in (f"gather_a{l}", f"gather_b{l}"):
                    drained(pe, nm)
                with pe.Fori(0, PAIRS - 1) as i:
                    pair(i, "", False)
                    for nm in (f"next_a.{l}", f"next_b.{l}"):
                        drained(pe, nm, i)
                pair(None, "last", True)

            def rest_of_tokens(l):
                r = rest[l]
                pe.wait_ge(count_ready, l + 1)
                total = pe.value_load(counts[0:1, l:l + 1], min_val=0, max_val=S * 2)
                with pe.If(total > 0):
                    pe.wait_ge(r["added"], 1)
                    with pe.Fori(0, NE) as i:
                        pe.wait_ge(r["loaded"], i * 48 + 48)
                        for t in range(NT):
                            u = i * NT + t
                            pe.wait_ge(r["added"], u + 1)
                            for b, s in ((0, 0), (1, 1)):
                                for k in range(KD):
                                    ins = pe.matmul(bank[b][:, :], xT[:, k, t * P:(t + 1) * P], s3(s, FF, KD)[:, k, :],
                                                    start=(k == 0), stop=(k == KD - 1))
                            ins.then_inc(r["h"], 1)
                            pe.wait_ge(r["hid"], u + 1)
                            for c in range(KF):
                                ins = pe.transpose(bank[2][:, c * P:(c + 1) * P], hid[:, c::KF], ident)
                            ins.then_inc(r["hidT"], 1)
                            pe.wait_ge(r["hidT_copied"], u + 1)
                            for half in range(2):
                                for c in range(KF):
                                    ins = pe.matmul(bank[4 + half][:, :], hidT[:, c, :],
                                                    s3(2, D, KF)[:, c, half * NB:(half + 1) * NB],
                                                    start=(c == 0), stop=(c == KF - 1))
                            ins.then_inc(r["w2"], 1)
                    pe.wait_ge(r["added"], NE * NT + 1)
                pe.nop()

            pe.wait_ge(const_loaded, 16)
            pe.wait_ge(consts_set, 2)
            pe.wait_ge(xT_loaded, 16)
            for k in range(KD):
                if k in (0, KA):
                    loaded(pe, 0 if k == 0 else 1)
                w = s3(0, LAT, KA)[:, k, :] if k < KA else s3(1, LAT, KB)[:, k - KA, :]
                for q in range(4):
                    t, part = divmod(q, 2)
                    c0, c1 = (0, NB) if part == 0 else (NB, LAT)
                    ins = pe.matmul(bk(f"lat{q}")[:, 0:c1 - c0], xT[:, k, t * P:(t + 1) * P], w[:, c0:c1],
                                    start=(k == 0), stop=(k == KD - 1))
                    if k == KD - 1:
                        fill(ins, f"lat{q}")
            pe.wait_ge(lat_ready, 2 * NT)
            for c in range(CQ + CKV):
                nm = f"latT{c // 2}"
                for t in range(NT):
                    src = lat3[:, t, c:QR:CQ] if c < CQ else lat3[:, t, QR + c - CQ:QR + KVR:CKV]
                    ins = pe.transpose(bk(nm)[:, (c % 2) * S + t * P:(c % 2) * S + (t + 1) * P], src, ident)
                if c % 2 or c == CQ + CKV - 1:
                    fill(ins, nm)
            for q in range(3):
                drained(pe, f"latT{q}")
            wq = [s3(2, H * DQ, 2)[:, 0, :], s3(2, H * DQ, 2)[:, 1, :], s3(1, H * DQ, 1, off=KB * LAT)[:, 0, :]]
            wkv = s3(3, H * (NOPE + VD), CKV)
            loaded(pe, 2)
            pe.wait_ge(w_qb2_loaded, 16)
            for o in range(14):
                may_fill(pe, f"qkv{o}")
                if o == 6:
                    loaded(pe, 3)
                t, nn = divmod(o, 3) if o < 6 else divmod(o - 6, 4)
                chunks = CQ if o < 6 else CKV
                for c in range(chunks):
                    w = wq[c] if o < 6 else wkv[:, c, :]
                    j = c if o < 6 else CQ + c
                    ins = pe.matmul(bk(f"qkv{o}")[:, :], latT3[:, j, t * P:(t + 1) * P], w[:, nn * NB:(nn + 1) * NB],
                                    start=(c == 0), stop=(c == chunks - 1))
                fill(ins, f"qkv{o}")
            for o in range(14):
                drained(pe, f"qkv{o}")
            pe.wait_ge(rope_ready, 2)
            for step in range(H + 3):
                h = step
                if h < H:
                    may_fill(pe, f"headT{h}")
                    b = bk(f"headT{h}")
                    for w in range(2):
                        for t in range(NT):
                            src = (q4, k4d)[w][:, t, h, :]
                            ins = pe.transpose(b[0:DQ, w * S + t * P:w * S + (t + 1) * P], src, ident)
                    fill(ins, f"headT{h}")
                h = step - 1
                if 0 <= h < H:
                    drained(pe, f"headT{h}")
                    may_fill(pe, f"score{h}")
                    qk, b = m_qk[h % 4], bk(f"score{h}")
                    pe.matmul(b[:, 0:P], qk[0:DQ, 0:P], qk[0:DQ, S:S + P], start=True, stop=True)
                    fill(pe.matmul(b[:, P:3 * P], qk[0:DQ, P:S], qk[0:DQ, S:2 * S], start=True, stop=True), f"score{h}")
                h = step - 2
                if 0 <= h < H:
                    pe.wait_ge(prob_ready, 2 * h + 2)
                    may_fill(pe, f"probT{h}")
                    for c in range(3):
                        ins = pe.transpose(bk(f"probT{h}")[:, c * P:(c + 1) * P], m_s[h % 4][:, c * P:(c + 1) * P], ident)
                    fill(ins, f"probT{h}")
                h = step - 3
                if 0 <= h < H:
                    drained(pe, f"probT{h}")
                    pt = m_pt[h % 2]
                    for t in range(NT):
                        nm = f"mla_o{2 * t + h // 8}"
                        if h % 8 == 0:
                            may_fill(pe, nm)
                        o = bk(nm)[:, (h % 8) * VD:(h % 8 + 1) * VD]
                        for kt in range(t + 1):
                            c = kt if t == 0 else 1 + kt
                            ins = pe.matmul(o, pt[:, c * P:(c + 1) * P], v4[:, kt, h, :], start=(kt == 0), stop=(kt == t))
                        if h % 8 == 7:
                            fill(ins, nm)
                    if h % 8 != 7:
                        ins.then_inc(pv_done, 1)
            for q in range(4):
                drained(pe, f"mla_o{q}")
            transposes("mla_oT", mo3)
            out_projection("mla_y", 4, moT, "mla_oT")
            pe.wait_ge(x_ready, NT)
            transposes("x1T", x_tok)
            experts(0, "x1T")
            rest_of_tokens(0)

            pe.wait_ge(x_ready, 2 * NT)
            transposes("x2T", x_tok)
            for s in range(4):
                drained(pe, f"x2T{s}")
            j0 = LOAD0["nsa"]

            def nsa_slot(c):
                loaded(pe, j0 + c)
                return s3((j0 + c) % RING, NSA_COLS, KD)

            def columns_T(out, w, c0):
                for k in range(KD):
                    ins = pe.matmul(out, w[:, k, c0:c0 + P], xT[:, k, :], start=(k == 0), stop=(k == KD - 1))
                return ins

            for c in range(5):
                w = nsa_slot(c)
                if c < 2:
                    for half in range(2):
                        nm = f"nq{2 * c + half}"
                        may_fill(pe, nm)
                        for x in range(2):
                            ins = columns_T(bk(nm)[:, x * S:(x + 1) * S], w, (2 * half + x) * P)
                        fill(ins, nm)
                    continue
                nm, nv = (("kc", "vc"), ("ks", "vs"), ("kw", "vw"))[c - 2]
                may_fill(pe, nm)
                for x in range(2):
                    ins = columns_T(bk(nm)[:, x * S:(x + 1) * S], w, x * P)
                fill(ins, nm)
                may_fill(pe, nv)
                if c == 2:
                    for x in range(2):
                        ins = columns_T(bk(nv)[:, x * S:(x + 1) * S], w, (2 + x) * P)
                else:
                    for t in range(NT):
                        for k in range(KD):
                            ins = pe.matmul(bk(nv)[:, t * S:(t + 1) * S], xT[:, k, t * P:(t + 1) * P], w[:, k, S:2 * S],
                                            start=(k == 0), stop=(k == KD - 1))
                fill(ins, nv)
            pe.wait_ge(nsa_loaded, 48)
            may_fill(pe, "gate")
            for t in range(NT):
                for k in range(KD):
                    ins = pe.matmul(bk("gate")[:, t * NGATE:(t + 1) * NGATE], xT[:, k, t * P:(t + 1) * P], gw[:, k, :],
                                    start=(k == 0), stop=(k == KD - 1))
            fill(ins, "gate")
            loaded(pe, j0 + 5)
            phi = ring[:, ((j0 + 5) % RING) * SLOT:((j0 + 5) % RING + 1) * SLOT].rearrange("p (w l e) -> p w l e", w=2, l=CMP_LEN)
            drained(pe, "kc")
            for x in range(2):
                may_fill(pe, f"kcmp{x}")
            for l in range(CMP_LEN):
                hi, r = divmod(l, CMP_STRIDE)
                for x in range(2):
                    rows = slice(64 * x, 64 * x + 64)
                    c0 = r + CMP_STRIDE * hi
                    src = ab[rows, hi, :, c0:c0 + CMP_STRIDE * (NCMP - 1) + 1:CMP_STRIDE]
                    out = bk(f"kcmp{x}")[rows, 0:2 * NCMP].rearrange("p (q n) -> p q n", q=2)
                    ins = pe.matmul(out, phi[rows, 0, l, :], src, start=(l == 0), stop=(l == CMP_LEN - 1))
                    if l == CMP_LEN - 1:
                        fill(ins, f"kcmp{x}")
            drained(pe, "vc")
            for x in range(2):
                may_fill(pe, f"vcmp{x}")
            for l in range(CMP_LEN):
                hi, r = divmod(l, CMP_STRIDE)
                for g in range(G):
                    x, q = g % 2, g // 2
                    rows = slice(64 * x, 64 * x + 64)
                    c0 = r + CMP_STRIDE * hi
                    src = ab[rows, 2 + hi, q, c0:c0 + CMP_STRIDE * (NCMP - 1) + 1:CMP_STRIDE]
                    ins = pe.matmul(bk(f"vcmp{x}")[32 * g:32 * g + NCMP, 0:HD], src, phi[rows, 1, l, :],
                                    start=(l == 0), stop=(l == CMP_LEN - 1))
                    if l == CMP_LEN - 1 and g >= 2:
                        fill(ins, f"vcmp{x}")
            for q in range(4):
                drained(pe, f"nq{q}")
            for x in range(2):
                drained(pe, f"kcmp{x}")
                may_fill(pe, f"cs{x}")
            for t in range(NT):
                for i in range(H // 2):
                    for x in range(2):
                        rows = slice(64 * x, 64 * x + 64)
                        c0 = (t * (H // 2) + i) * 16
                        ins = pe.matmul(bk(f"cs{x}")[:, c0:c0 + NCMP], nqT[rows, i, t * P:(t + 1) * P], kct[rows, i // 2, 0:NCMP],
                                        start=True, stop=True)
                        if t == NT - 1 and i == H // 2 - 1:
                            fill(ins, f"cs{x}")
            pe.wait_ge(cmp_prob, 1)
            for t in range(NT):
                may_fill(pe, f"pcT{t}")
                for g in range(G):
                    ins = pe.transpose(bk(f"pcT{t}")[:, g * P:(g + 1) * P],
                                       sc[:, t * H + g * HPG:t * H + (g + 1) * HPG, :].rearrange("p h n -> p (h n)"), ident)
                fill(ins, f"pcT{t}")
            for t in range(NT):
                drained(pe, f"pcT{t}")
            for x in range(2):
                drained(pe, f"vcmp{x}")
            for t in range(NT):
                for g in range(G):
                    nm = f"nsa_o{2 * t + g // 2}"
                    if g % 2 == 0:
                        may_fill(pe, nm)
                    pe.matmul(bk(nm)[:, (g % 2) * S:(g % 2 + 1) * S], pct[:, t * G + g, :], vbd[:, g, :],
                              start=(g % 2 == 0), stop=False, skip_group_check=True)
            for nm in ("ks", "vs", "kw", "vw"):
                drained(pe, nm)

            def nsa_values(r):
                t, h = divmod(r, H)
                drained(pe, f"nprobT{r}")
                pt = n_pt[r % 2]
                g = h // HPG
                o = bk(f"nsa_o{2 * t + h // 8}")[:, (h % 8) * HD:(h % 8 + 1) * HD]
                for b in range(2):
                    for kt in range(t + 1):
                        c = b * (t + 1) + kt
                        ins = pe.matmul(o, pt[:, c * P:(c + 1) * P], vsw[:, b, kt, g * HD:(g + 1) * HD],
                                        start=False, stop=True, skip_group_check=True)
                if h % 8 == 7:
                    fill(ins, f"nsa_o{2 * t + h // 8}")
                else:
                    ins.then_inc(npv_done, 1)

            for step in range(NT * H // 2 + 2):
                if step < NT * H // 2:
                    t, i = divmod(step, H // 2)
                    for x in range(2):
                        may_fill(pe, f"nscore{2 * step + x}")
                    for x in range(2):
                        rows = slice(64 * x, 64 * x + 64)
                        nm = f"nscore{2 * step + x}"
                        w = (t + 1) * P
                        out = bk(nm)[:, 0:2 * w].rearrange("p (b s) -> p b s", b=2)
                        fill(pe.matmul(out, nqT[rows, i, t * P:(t + 1) * P], kall[rows, i // 2, :, 0:w], start=True, stop=True), nm)
                if step >= 1 and step <= NT * H // 2:
                    for x in range(2):
                        r = 2 * (step - 1) + x
                        t = r // H
                        pe.wait_ge(nprob_ready, r + 1)
                        may_fill(pe, f"nprobT{r}")
                        for c in range(2 * (t + 1)):
                            ins = pe.transpose(bk(f"nprobT{r}")[:, c * P:(c + 1) * P], n_s[r % 4][:, c * P:(c + 1) * P], ident)
                        fill(ins, f"nprobT{r}")
                if step >= 2:
                    for x in range(2):
                        nsa_values(2 * (step - 2) + x)
            for q in range(4):
                drained(pe, f"nsa_o{q}")
            transposes("nsa_oT", no3)
            out_projection("nsa_y", j0 + 6, noT, "nsa_oT")
            pe.wait_ge(x_ready, 3 * NT)
            transposes("x3T", x_tok)
            experts(1, "x3T")
            rest_of_tokens(1)

        @block.scalar
        def _(act):
            def copy(out, in_):
                return act.activation(out, in_, ACT.Copy)

            def xT_copies(name, dst):
                for s in (1, 3):
                    t, kh = divmod(s, 2)
                    filled(act, f"{name}{s}")
                    drain(copy(dst[:, 4 * kh:4 * kh + 4, t * P:(t + 1) * P],
                               bk(f"{name}{s}")[:, :].rearrange("p (k s) -> p k s", k=4)), f"{name}{s}")

            def router_exps(l):
                for s in range(2):
                    act.wait_ge(logit_exp_in, 2 * l + s + 1)
                    act.activation(e4 if s == 0 else p4, e4 if s == 0 else p4, ACT.Exp).then_inc(logit_exp_out, 1)

            def experts(l):
                filled(act, f"gather_a{l}")
                drain(copy(xe[:, 0:4, :], bk(f"gather_a{l}")[:, :].rearrange("p (k s) -> p k s", k=4)), f"gather_a{l}")

                def pair(i, tag, last):
                    n_ = [f"{k}.{l}{tag}" for k in ("h1", "h3", "hidT", "scatT", "w2_0", "w2_1")]
                    h1, h3, hT, sT, y0, y1 = n_
                    filled(act, h1, i)
                    b, k = number(h3, i)
                    act.wait_ge(bank_drained[b], k - 2)
                    drain(act.activation(silu, bk(h1)[:, :], ACT.Silu), h1)
                    if not last:
                        filled(act, f"next_a.{l}", i)
                        drain(copy(xe[:, 0:4, :], bk(f"next_a.{l}")[:, :].rearrange("p (k s) -> p k s", k=4)), f"next_a.{l}")
                    filled(act, sT, i)
                    act.wait_ge(scattered, (l + 1) * PAIRS if last else i + (l * PAIRS + 1))
                    drain(copy(scatT_f, bk(sT)[:, 0:NT * P]), sT)
                    filled(act, y0, i)
                    drain(copy(ye[:, 0:NB], bk(y0)[:, :]), y0)

                with act.Fori(0, PAIRS - 1) as i:
                    pair(i, "", False)
                pair(None, "last", True)

            def rest_of_tokens(l):
                r = rest[l]
                act.wait_ge(count_ready, l + 1)
                total = act.value_load(counts[0:1, l:l + 1], min_val=0, max_val=S * 2)
                with act.If(total > 0):
                    act.wait_ge(r["added"], 1)
                    with act.Fori(0, NE) as i:
                        for t in range(NT):
                            act.wait_ge(r["h"], i * NT + t + 1)
                            act.activation(silu, bank[0][:, :], ACT.Silu).then_inc(r["silu"], 1)
                            act.wait_ge(r["hid"], i * NT + t + 1)
                act.nop()

            for q in range(4):
                t, part = divmod(q, 2)
                c0, c1 = (0, NB) if part == 0 else (NB, LAT)
                filled(act, f"lat{q}")
                drain(copy(lat3[:, t, c0:c1], bk(f"lat{q}")[:, 0:c1 - c0]), f"lat{q}")
            for q in range(4):
                drained(act, f"lat{q}")
            for t in range(NT):
                for w, (c0, c1) in enumerate(((0, QR), (QR, QR + KVR))):
                    act.activation(mo[:, 0:c1 - c0], lat3[:, t, c0:c1], ACT.Square,
                                   accum_out=sumsq[:, 2 * t + w:2 * t + w + 1]).then_inc(sumsq_ready, 1)
                    act.wait_ge(sumsq_ready, 2 * t + w + 1)
            for o in range(1, 14, 2):
                filled(act, f"qkv{o}")
                qkv_copy(act, copy, o)
            for step in range(H + 3):
                h = step - 1
                if 0 <= h < H:
                    act.wait_ge(score_ready, h + 1)
                    s = m_s[h % 4]
                    for t, (c0, c1) in enumerate(((0, P), (P, 3 * P))):
                        act.activation(s[:, c0:c1], s[:, c0:c1], ACT.Exp, bias=nm3[:, h, t:t + 1], scale=MLA_SCALE,
                                       accum_out=z3[:, t, h:h + 1]).then_inc(prob_ready, 1)
                h = step - 2
                if 0 <= h < H:
                    filled(act, f"probT{h}")
                    if h >= 2:
                        mla_pv_done(act, h - 2)
                    drain(copy(m_pt[h % 2], bk(f"probT{h}")[:, 0:3 * P]), f"probT{h}")
            xT_copies("mla_oT", moT)
            xT_copies("x1T", xT)
            router_exps(0)
            experts(0)
            rest_of_tokens(0)

            xT_copies("x2T", xT)
            for q in (1, 3):
                filled(act, f"nq{q}")
                drain(copy(nqT[:, 2 * q:2 * q + 2, :], bk(f"nq{q}")[:, :].rearrange("p (i s) -> p i s", i=2)), f"nq{q}")
            for b, nm in enumerate(("ks", "kw")):
                filled(act, nm)
                src = bk(nm)[:, :].rearrange("p (q s) -> p q s", q=2)
                for x in range(2):
                    for y in range(2):
                        ins = copy(kall[64 * y:64 * y + 64, x::2, b, :], src[64 * x:64 * x + 64, :, :])
                drain(ins, nm)
            filled(act, "gate")
            act.activation(n_gate, bk("gate")[:, 0:NT * NGATE], ACT.Exp, scale=-1.0).then_inc(bank_drained[plan.at["gate"][0]], 1)
            act.wait_ge(cmp_in, 1)
            act.activation(sc[:, :, 0:NCMP], sc[:, :, 0:NCMP], ACT.Exp).then_inc(cmp_exp, 1)
            for t in (1,):
                filled(act, f"pcT{t}")
                drain(copy(pct[:, t * G:(t + 1) * G, :], bk(f"pcT{t}")[:, :].rearrange("p (g s) -> p g s", g=G)), f"pcT{t}")
            for r in range(NT * H + 3):
                if r < NT * H:
                    act.wait_ge(nscore_ready, r + 1)
                    w = (r // H + 1) * P
                    s = n_s[r % 4]
                    for b in range(2):
                        act.activation(s[:, b * w:(b + 1) * w], s[:, b * w:(b + 1) * w], ACT.Exp, bias=v3["nm"][:, r, b:b + 1],
                                       accum_out=v3["z"][:, r, b:b + 1]).then_inc(raw_prob, 1)
                r = r - 3
                if 0 <= r:
                    filled(act, f"nprobT{r}")
                    if r >= 2:
                        nsa_pv_done(act, r - 2)
                    w = 2 * (r // H + 1) * P
                    drain(copy(n_pt[r % 2][:, 0:w], bk(f"nprobT{r}")[:, 0:w]), f"nprobT{r}")
            xT_copies("nsa_oT", noT)
            xT_copies("x3T", xT)
            router_exps(1)
            experts(1)
            rest_of_tokens(1)

        @block.vector
        def _(dve):
            st = Steps(dve, dve_step)
            copy = dve.tensor_copy

            def bc(ap, shape):
                return ap.to_broadcast(shape)

            def xT_copies(name, dst):
                for s in (0, 2):
                    t, kh = divmod(s, 2)
                    filled(dve, f"{name}{s}")
                    drain(copy(dst[:, 4 * kh:4 * kh + 4, t * P:(t + 1) * P],
                               bk(f"{name}{s}")[:, :].rearrange("p (k s) -> p k s", k=4)), f"{name}{s}")

            def layer_norm(k):
                for t in range(NT):
                    for c in range(2):
                        st(dve.bn_stats(bn[:, t, c, :], x_tok[:, t, c * NB:(c + 1) * NB]))
                st.wait()
                for t in range(NT):
                    st(dve.bn_aggr(mv[:, t, :], bn[:, t, :, :].rearrange("p c s -> p (c s)")))
                st.wait()
                dve.tensor_scalar(var_eps[:, 0:NT], mv[:, :, 1], LN_EPS, None, ALU.add).then_inc(var_ready, 1)
                dve.wait_ge(ln_loaded, 32 * (k + 1))
                for t in range(NT):
                    st(dve.scalar_tensor_tensor(out=x_tok[:, t, :], in0=x_tok[:, t, :], scalar=mv[:, t, 0:1], in1=gain,
                                                op0=ALU.subtract, op1=ALU.mult))
                dve.wait_ge(rstd_ready, k + 2)
                st.wait()
                for t in range(NT):
                    dve.scalar_tensor_tensor(out=x_tok[:, t, :], in0=x_tok[:, t, :], scalar=rstd[:, t:t + 1], in1=shift,
                                             op0=ALU.mult, op1=ALU.add).then_inc(x_ready, 1)
                dve.wait_ge(x_ready, NT * (k + 1))

            def residual(name):
                for q in range(4):
                    t, half = divmod(q, 2)
                    filled(dve, f"{name}{q}")
                    cols = slice(half * NB, (half + 1) * NB)
                    drain(dve.scalar_tensor_tensor(out=x_tok[:, t, cols], in0=x_tok[:, t, cols], scalar=ALPHA,
                                                   in1=bk(f"{name}{q}")[:, :], op0=ALU.mult, op1=ALU.add), f"{name}{q}")
                for q in range(4):
                    drained(dve, f"{name}{q}")

            def reduce(out, in_, op):
                st(dve.tensor_reduce(out, in_, AX, op))
                st.wait()

            def tt(out, a_, b_, op):
                st(dve.tensor_tensor(out, a_, b_, op))
                st.wait()

            W4 = [P, NT, EPG]
            W16 = [P, NT, NG, EPG]

            def top_one_hot(out, probs, top):
                reduce(top[:, :, 0], probs, ALU.max)
                tt(k4, probs, bc(top, W4), ALU.is_equal)
                tt(k4, k4, bc(desc.unsqueeze(1), W4), ALU.mult)
                reduce(r1[:, :, 0], k4, ALU.max)
                tt(out, k4, bc(r1, W4), ALU.is_equal)

            def softmax4(out, in_, k, buf):
                reduce(r1[:, :, 0], in_, ALU.max)
                dve.tensor_tensor(buf, in_, bc(r1, W4), ALU.subtract).then_inc(logit_exp_in, 1)
                dve.wait_ge(logit_exp_out, k + 1)
                reduce(r1[:, :, 0], buf, ALU.add)
                st(dve.reciprocal(r2, r1))
                st.wait()
                tt(out, buf, bc(r2, W4), ALU.mult)

            def route(l):
                dve.wait_ge(router_loaded, 32 * (l + 1))
                filled(dve, f"logits{l}")
                drain(dve.tensor_tensor(lg, bk(f"logits{l}")[:, 0:NT * NR].rearrange("p (t c) -> p t c", t=NT),
                                        bc(router_b.unsqueeze(1), [P, NT, NR]), ALU.add), f"logits{l}")
                drained(dve, f"logits{l}")
                softmax4(e4, lg[:, :, 0:NG], 2 * l, e4)
                top_one_hot(group1h, e4, pg_top)
                le = lg[:, :, NG:].rearrange("p t (g e) -> p t g e", g=NG)
                p16 = prod16.rearrange("p t (g e) -> p t g e", g=NG)
                for g in range(NG):
                    st(dve.tensor_tensor(p16[:, :, g, :], le[:, :, g, :], bc(group1h[:, :, g:g + 1], W4), ALU.mult))
                st.wait()
                reduce(m4, prod16.rearrange("p t (g e) -> p t e g", g=NG), ALU.add)
                softmax4(p4, m4, 2 * l + 1, p4)
                top_one_hot(first1h, p4, v1)
                st(dve.scalar_tensor_tensor(out=m4, in0=first1h, scalar=-4.0, in1=p4, op0=ALU.mult, op1=ALU.add))
                st.wait()
                top_one_hot(second1h, m4, v2)
                tt(r1, v1, v2, ALU.add)
                st(dve.reciprocal(r2, r1))
                st.wait()
                for v, hot in ((v1, first1h), (v2, second1h)):
                    tt(v, v, r2, ALU.mult)
                    tt(v, v, pg_top, ALU.mult)
                    tt(m4 if v is v1 else k4, hot, bc(v, W4), ALU.mult)
                tt(gate4, m4, k4, ALU.add)
                tt(k4, first1h, second1h, ALU.add)
                for g in range(NG):
                    cols = slice(g * EPG, (g + 1) * EPG)
                    st(dve.tensor_tensor(gates[:, :, cols], gate4, bc(group1h[:, :, g:g + 1], W4), ALU.mult))
                    ins = dve.tensor_tensor(member[:, :, cols], k4, bc(group1h[:, :, g:g + 1], W4), ALU.mult)
                ins.then_inc(member_ready, 1)
                dve.wait_ge(member_ready, l + 1)
                filled(dve, f"position{l}")
                drain(dve.scalar_tensor_tensor(out=posm, in0=bk(f"position{l}")[:, 0:NT * NE].rearrange("p (t c) -> p t c", t=NT),
                                               scalar=1.0, in1=member, op0=ALU.add, op1=ALU.mult), f"position{l}")
                drained(dve, f"position{l}")
                st(dve.tensor_scalar(posm, posm, -1.0, None, ALU.add))
                st.wait()
                dve.tensor_scalar(over, posm, float(CAP), None, ALU.is_ge).then_inc(over_ready, 1)
                dve.wait_ge(over_ready, l + 1)
                st(dve.tensor_tensor(rest_gates, gates, over, ALU.mult))

            def picks(l, e0):
                for t in range(NT):
                    for x in range(2):
                        ins = dve.tensor_scalar(pick[:, t, CAP * x:CAP * (x + 1)], iota, posm[:, t, bass.ds(e0 + x, 1)], None,
                                                ALU.is_equal)
                ins.then_inc(pick_ready, 1)

            def scatters(l, e0):
                for t in range(NT):
                    for x in range(2):
                        ins = dve.tensor_scalar(scat[:, t, CAP * x:CAP * (x + 1)], iota, posm[:, t, bass.ds(e0 + x, 1)],
                                                gates[:, t, bass.ds(e0 + x, 1)], ALU.is_equal, ALU.mult)
                ins.then_inc(scat_ready, 1)

            def experts(l):
                picks(l, 0)
                filled(dve, f"overflow{l}")
                drain(dve.tensor_reduce(k4[:, 0, 0:1], bk(f"overflow{l}")[:, 0:NT * NE], AX, ALU.add), f"overflow{l}")
                drained(dve, f"overflow{l}")
                dve.tensor_copy(counts[:, l:l + 1], k4[:, 0, 0:1]).then_inc(count_ready, 1)
                filled(dve, f"gather_b{l}")
                drain(copy(xe[:, 4:8, :], bk(f"gather_b{l}")[:, :].rearrange("p (k s) -> p k s", k=4)), f"gather_b{l}")

                def pair(i, tag, last):
                    n_ = [f"{k}.{l}{tag}" for k in ("h1", "h3", "hidT", "scatT", "w2_0", "w2_1")]
                    h1, h3, hT, sT, y0, y1 = n_
                    b, k = number(sT, i)
                    dve.wait_ge(bank_drained[b], k - 2)
                    scatters(l, 2 * (PAIRS - 1) if last else i * 2)
                    if not last:
                        filled(dve, h1, i)
                        picks(l, i * 2 + 2)
                    drained(dve, h1, i)
                    filled(dve, h3, i)
                    drain(dve.tensor_tensor(hid, silu, bk(h3)[:, :], ALU.mult), h3)
                    if not last:
                        filled(dve, f"next_b.{l}", i)
                        drain(copy(xe[:, 4:8, :], bk(f"next_b.{l}")[:, :].rearrange("p (k s) -> p k s", k=4)), f"next_b.{l}")
                    filled(dve, hT, i)
                    drain(copy(hidT_f, bk(hT)[:, :]), hT)
                    filled(dve, y1, i)
                    dve.wait_ge(scattered, (l + 1) * PAIRS if last else i + (l * PAIRS + 1))
                    drain(copy(ye[:, NB:2 * NB], bk(y1)[:, :]), y1)

                with dve.Fori(0, PAIRS - 1) as i:
                    pair(i, "", False)
                pair(None, "last", True)
                for q in range(4):
                    t, half = divmod(q, 2)
                    filled(dve, f"moe_y{l}{q}")
                    drain(copy(x_tok[:, t, half * NB:(half + 1) * NB], bk(f"moe_y{l}{q}")[:, :]), f"moe_y{l}{q}")
                for q in range(4):
                    drained(dve, f"moe_y{l}{q}")

            def rest_of_tokens(l):
                r = rest[l]
                dve.wait_ge(count_ready, l + 1)
                total = dve.value_load(counts[0:1, l:l + 1], min_val=0, max_val=S * 2)
                with dve.If(total > 0):
                    dve.memset(k4[:, 0, 0:1], 0.0).then_inc(r["added"], 1)
                    with dve.Fori(0, NE) as i:
                        for t in range(NT):
                            u = i * NT + t
                            dve.wait_ge(r["silu"], u + 1)
                            dve.scalar_tensor_tensor(out=hid, in0=bank[1][:, :], scalar=rest_gates[:, t, bass.ds(i, 1)],
                                                     in1=silu, op0=ALU.mult, op1=ALU.mult).then_inc(r["hid"], 1)
                            dve.wait_ge(r["hidT"], u + 1)
                            dve.tensor_copy(hidT_f, bank[2][:, :]).then_inc(r["hidT_copied"], 1)
                            dve.wait_ge(r["w2"], u + 1)
                            dve.wait_ge(r["added"], u + 1)
                            for half in range(2):
                                cols = slice(half * NB, (half + 1) * NB)
                                ins = dve.tensor_tensor(x_tok[:, t, cols], x_tok[:, t, cols], bank[4 + half][:, :], ALU.add)
                            ins.then_inc(r["added"], 1)
                    dve.wait_ge(r["added"], NE * NT + 1)
                dve.nop()

            dve.wait_ge(const_loaded, 16)
            dve.wait_ge(sumsq_ready, 2 * NT)
            for t in range(NT):
                for w, c in enumerate((QR, KVR)):
                    ins = dve.tensor_scalar(sumsq[:, 2 * t + w:2 * t + w + 1], sumsq[:, 2 * t + w:2 * t + w + 1], 1.0 / c, RMS_EPS,
                                            ALU.mult, ALU.add)
            ins.then_inc(var_ready, 1)
            dve.wait_ge(rstd_ready, 1)
            for q in range(4):
                drained(dve, f"lat{q}")
            for t in range(NT):
                for w, (c0, c1) in enumerate(((0, QR), (QR, QR + KVR))):
                    dve.tensor_scalar(lat3[:, t, c0:c1], lat3[:, t, c0:c1], rms[:, 2 * t + w:2 * t + w + 1], None,
                                      ALU.mult).then_inc(lat_ready, 1)
            half = ROPE // 2

            def rotate(out1, out2, a1, a2, shape, heads):
                tmp = [r_[:, 0:NT * heads * half].rearrange("p (t h f) -> p t h f", t=NT, h=heads) for r_ in rt]
                cs, sn = bc(cos.unsqueeze(2), shape), bc(sin.unsqueeze(2), shape)
                for buf, (x, y) in zip(tmp, ((a1, cs), (a2, sn), (a1, sn), (a2, cs))):
                    st(dve.tensor_tensor(buf, x, y, ALU.mult))
                st.wait()
                dve.tensor_tensor(out1, tmp[0], tmp[1], ALU.subtract)
                return dve.tensor_tensor(out2, tmp[2], tmp[3], ALU.add)

            kr = lat3[:, :, QR + KVR:LAT].unsqueeze(2)
            st(rotate(kr[:, :, :, 0:half], kr[:, :, :, half:], kr[:, :, :, 0:half], kr[:, :, :, half:], [P, NT, 1, half], 1))
            st.wait()
            for t in range(NT):
                ins = copy(k4d[:, t, :, NOPE:], bc(kr[:, t, :, :], [P, H, ROPE]))
            ins.then_inc(rope_ready, 1)
            dve.wait_ge(rms_loaded, 16)
            for c in range(CQ + CKV):
                nm = f"latT{c // 2}"
                if c % 2 == 0:
                    filled(dve, nm)
                ins = dve.tensor_scalar(latT3[:, c, :], bk(nm)[:, (c % 2) * S:(c % 2 + 1) * S], rms_gain[:, c:c + 1], None, ALU.mult)
                if c % 2 or c == CQ + CKV - 1:
                    drain(ins, nm)
            for o in range(0, 14, 2):
                filled(dve, f"qkv{o}")
                qkv_copy(dve, copy, o)
            for o in range(6):
                drained(dve, f"qkv{o}")
            q1, q2 = q4[:, :, :, NOPE:NOPE + half], q4[:, :, :, NOPE + half:]
            rotate(q1, q2, q1, q2, [P, NT, H, half], H).then_inc(rope_ready, 1)
            for step in range(H + 1):
                h = step
                if h < H:
                    filled(dve, f"headT{h}")
                    if h >= 4:
                        filled(dve, f"score{h - 4}")
                    drain(copy(m_qk[h % 4][0:DQ, :], bk(f"headT{h}")[0:DQ, :]), f"headT{h}")
                h = step - 1
                if 0 <= h:
                    filled(dve, f"score{h}")
                    if h >= 4:
                        filled(dve, f"probT{h - 4}")
                    s = m_s[h % 4]
                    drain(dve.tensor_tensor(s, bk(f"score{h}")[:, 0:3 * P], mask3, ALU.add), f"score{h}")
                    drained(dve, f"score{h}")
                    for t, (c0, c1) in enumerate(((0, P), (P, 3 * P))):
                        st(dve.tensor_reduce(mx3[:, h, t:t + 1], s[:, c0:c1], AX, ALU.max))
                    st.wait()
                    dve.tensor_scalar(nm3[:, h, :], mx3[:, h, :], -MLA_SCALE, None, ALU.mult).then_inc(score_ready, 1)
            dve.wait_ge(prob_ready, 2 * H)
            st(dve.reciprocal(m_rz, m_z))
            st.wait()
            for q in range(4):
                t, hh = divmod(q, 2)
                filled(dve, f"mla_o{q}")
                out = mo3[:, t, hh * NB:(hh + 1) * NB].rearrange("p (h d) -> p h d", h=8)
                ins = dve.tensor_tensor(out, bk(f"mla_o{q}")[:, :].rearrange("p (h d) -> p h d", h=8),
                                        bc(rz3[:, t, hh * 8:(hh + 1) * 8].unsqueeze(2), [P, 8, VD]), ALU.mult)
                drain(ins, f"mla_o{q}")
            xT_copies("mla_oT", moT)
            dve.wait_ge(x_loaded, 16)
            residual("mla_y")
            layer_norm(0)
            xT_copies("x1T", xT)
            route(0)
            experts(0)
            rest_of_tokens(0)
            layer_norm(1)

            xT_copies("x2T", xT)
            st(dve.memset(vbd_f, 0.0))
            st(dve.memset(sc_f, 0.0))
            for q in (0, 2):
                filled(dve, f"nq{q}")
                drain(copy(nqT[:, 2 * q:2 * q + 2, :], bk(f"nq{q}")[:, :].rearrange("p (i s) -> p i s", i=2)), f"nq{q}")
            dve.wait_ge(nsa_loaded, 48)
            for v, nm in enumerate(("kc", "vc")):
                filled(dve, nm)
                src = bk(nm)[:, :].rearrange("p (b r) -> p b r", r=CMP_STRIDE)
                for hi in range(2):
                    out = ab[:, 2 * v + hi, :, :].rearrange("p q (b r) -> p (q b) r", r=CMP_STRIDE)
                    ins = dve.tensor_tensor(out, src, bc(pos_t[:, hi * CMP_STRIDE:(hi + 1) * CMP_STRIDE].unsqueeze(1),
                                                         [P, 2 * S // CMP_STRIDE, CMP_STRIDE]), ALU.add)
                drain(ins, nm)
            for b, nm in enumerate(("vs", "vw")):
                filled(dve, nm)
                drain(copy(vsw[:, b, :, :], bk(nm)[:, :].rearrange("p (t c) -> p t c", t=NT)), nm)
            drained(dve, "gate")
            st(dve.tensor_scalar(n_gate, n_gate, 1.0, None, ALU.add))
            st.wait()
            st(dve.reciprocal(n_gate, n_gate))
            st.wait()
            for x in range(2):
                nm = f"kcmp{x}"
                filled(dve, nm)
                src = bk(nm)[64 * x:64 * x + 64, 0:2 * NCMP].rearrange("p (q n) -> p q n", q=2)
                for y in range(2):
                    ins = copy(kct[64 * y:64 * y + 64, x::2, 0:NCMP], src)
                drain(ins, nm)
            for x in range(2):
                nm = f"vcmp{x}"
                filled(dve, nm)
                for g in (x, x + 2):
                    for h in range(HPG):
                        ins = copy(vbd[32 * h:32 * h + NCMP, g, h * HD:(h + 1) * HD], bk(nm)[32 * g:32 * g + NCMP, 0:HD])
                drain(ins, nm)
            sc4 = sc_f.rearrange("p (t i x c) -> p t i x c", t=NT, i=H // 2, x=2)
            for x in range(2):
                nm = f"cs{x}"
                filled(dve, nm)
                for t in range(NT):
                    src = bk(nm)[:, t * P:(t + 1) * P].rearrange("p (i n) -> p i n", n=16)[:, :, 0:NCMP]
                    ins = dve.scalar_tensor_tensor(out=sc4[:, t, :, x, 0:NCMP], in0=src, scalar=NSA_SCALE,
                                                   in1=cmp_bias[:, t, x::2, :], op0=ALU.mult, op1=ALU.add)
                drain(ins, nm)
            for x in range(2):
                drained(dve, f"cs{x}")
            R = NT * H
            wide = [P, R, NCMP]
            reduce(c_mx, sc[:, :, 0:NCMP], ALU.max)
            dve.tensor_tensor(sc[:, :, 0:NCMP], sc[:, :, 0:NCMP], bc(c_mx.unsqueeze(2), wide), ALU.subtract).then_inc(cmp_in, 1)
            dve.wait_ge(cmp_exp, 1)
            reduce(c_z, sc[:, :, 0:NCMP], ALU.add)
            st(dve.reciprocal(c_cf, c_z))
            st.wait()
            tt(c_cf.rearrange("p (t h) -> p t h", t=NT), c_cf.rearrange("p (t h) -> p t h", t=NT),
               bc(any_visible.unsqueeze(2), [P, NT, H]), ALU.mult)
            tt(c_cf, c_cf, gate3[:, :, 0], ALU.mult)
            dve.tensor_tensor(sc[:, :, 0:NCMP], sc[:, :, 0:NCMP], bc(c_cf.unsqueeze(2), wide), ALU.mult).then_inc(cmp_prob, 1)
            filled(dve, "pcT1")
            filled(dve, "pcT0")
            drain(copy(pct[:, 0:G, :], bk("pcT0")[:, :].rearrange("p (g s) -> p g s", g=G)), "pcT0")
            for r in range(R + 2):
                if r < R:
                    t, h = divmod(r, H)
                    w = (t + 1) * P
                    filled(dve, f"nscore{r}")
                    if r >= 4:
                        filled(dve, f"nprobT{r - 4}")
                    s = n_s[r % 4][:, 0:2 * w].rearrange("p (b s) -> p b s", b=2)
                    drain(dve.scalar_tensor_tensor(out=s, in0=bk(f"nscore{r}")[:, 0:2 * w].rearrange("p (b s) -> p b s", b=2),
                                                   scalar=NSA_SCALE, in1=bc(alibi[t][:, h, :].unsqueeze(1), [P, 2, w]),
                                                   op0=ALU.mult, op1=ALU.add), f"nscore{r}")
                    drained(dve, f"nscore{r}")
                    st(dve.tensor_reduce(v3["mx"][:, r, :], s, AX, ALU.max))
                    st.wait()
                    dve.tensor_scalar(v3["nm"][:, r, :], v3["mx"][:, r, :], -1.0, None, ALU.mult).then_inc(nscore_ready, 1)
                r = r - 2
                if 0 <= r:
                    w = (r // H + 1) * P
                    dve.wait_ge(raw_prob, 2 * r + 2)
                    st(dve.reciprocal(v3["rz"][:, r, :], v3["z"][:, r, :]))
                    st.wait()
                    st(dve.tensor_tensor(v3["cf"][:, r, :], v3["rz"][:, r, :], gate3[:, r, 1:3], ALU.mult))
                    st.wait()
                    for b in range(2):
                        ins = dve.tensor_scalar(n_s[r % 4][:, b * w:(b + 1) * w], n_s[r % 4][:, b * w:(b + 1) * w],
                                                v3["cf"][:, r, b:b + 1], None, ALU.mult)
                    ins.then_inc(nprob_ready, 1)
            for q in range(4):
                t, hh = divmod(q, 2)
                filled(dve, f"nsa_o{q}")
                drain(copy(no3[:, t, hh * NB:(hh + 1) * NB], bk(f"nsa_o{q}")[:, :]), f"nsa_o{q}")
            xT_copies("nsa_oT", noT)
            residual("nsa_y")
            layer_norm(2)
            xT_copies("x3T", xT)
            route(1)
            experts(1)
            rest_of_tokens(1)
            layer_norm(3)


def kernel(**inputs):
    import concourse.bacc as bacc
    from concourse.bass_utils import run_bass_kernel_spmd

    f = {k: np.asarray(v) for k, v in inputs.items()}
    const, alibi = shape_constants()
    lay = {
        "x": f["x"][0],
        "xT": f["x"][0].T.reshape(P, KD * S),
        "const": const,
        "alibi": alibi,
        "rms_gain": np.concatenate([f["mla_q_norm"][0].reshape(P, CQ), f["mla_kv_norm"][0].reshape(P, CKV)], 1),
        "mla_w_in": f["mla_w_in"][0],
        "mla_w_qb": f["mla_w_qb"][0],
        "mla_w_kvb": f["mla_w_kvb"][0],
        "mla_w_o": f["mla_w_o"][0],
        "nsa_w_in": f["nsa_w_in"][0],
        "nsa_w_o": f["nsa_w_o"][0],
        "nsa_gate_w": f["nsa_w_in"][0][:, -NGATE:].reshape(P, KD * NGATE),
        "phi": np.tile(np.concatenate([f[k][0].reshape(CMP_LEN, HD, HD).transpose(1, 0, 2).reshape(HD, -1)
                                       for k in ("nsa_w_phi_k", "nsa_w_phi_v")], 1), (2, 1)),
        "cmp_posT": np.tile(f["nsa_cmp_pos"][0].T, (2, 1)),
        "ln": np.stack([f[k][l] for l in range(DEPTH) for k in ("ln1_g", "ln1_b", "ln2_g", "ln2_b")]),
        "router_w": np.stack([np.concatenate([f["moe_wg"][l], f["moe_we"][l].transpose(1, 0, 2).reshape(D, NE)], 1)
                              .reshape(P, KD * NR) for l in range(DEPTH)]),
        "router_b": np.concatenate([f["moe_bg"], f["moe_be"].reshape(DEPTH, NE)], 1),
        "moe_w1": f["moe_w1"].reshape(DEPTH * NE, D, FF),
        "moe_w3": f["moe_w3"].reshape(DEPTH * NE, D, FF),
        "moe_w2": f["moe_w2"].reshape(DEPTH * NE, FF, D),
    }
    nc = bacc.Bacc("TRN2", target_bir_lowering=False, num_devices=1)
    arrays, a = {}, {}
    for name, v in lay.items():
        arrays[f"in_{name}"] = np.ascontiguousarray(v)
        a[name] = nc.dram_tensor(f"in_{name}", v.shape, F32, kind="ExternalInput").ap()
    a["out"] = nc.dram_tensor("out_0", (S, D), F32, kind="ExternalOutput").ap()
    build(nc, a)
    r = run_bass_kernel_spmd(nc, [arrays], core_ids=[0])
    return r.results[0]["out_0"].reshape(1, S, D)
```

```python
from contextlib import ExitStack

import numpy as np

import concourse.bass as bass
from concourse import mybir

F32 = mybir.dt.float32
I32 = mybir.dt.int32
ALU = mybir.AluOpType
ACT = mybir.ActivationFunctionType
AX = mybir.AxisListType.X

P = 128
S = 256
NT = S // P
D = 1024
KD = D // P
DEPTH = 2
ALPHA = (2.0 * DEPTH) ** 0.25
LN_EPS = 1e-5
RMS_EPS = 1e-6
NEG = -1e30
HUGE = 3e38
H = 16
QR, KVR, NOPE, ROPE, VD = 384, 256, 64, 32, 64
CQ, CKV = QR // P, KVR // P
LAT = QR + KVR + ROPE
DQ = NOPE + ROPE
MLA_SCALE = DQ ** -0.5
HD = 64
G = 4
HPG = H // G
CMP_LEN, CMP_STRIDE = 32, 16
NCMP = (S - CMP_LEN) // CMP_STRIDE + 1
CMP_PAD = 16
NSA_SCALE = HD ** -0.5
NSA_COLS = 512
NGATE = 3 * H
KVC = G * HD
NE = 16
NG = 4
EPG = NE // NG
FF = 512
KF = FF // P
CAP = 64
PAIRS = NE // 2
NR = NG + NE
NRP = 32
EXTRA = 4
RING = 6
SLOT = 4096
NB = 512

C_ID = 0
C_AID = C_ID + P
C_TRI = C_AID + P
C_MASK = C_TRI + P
C_IOTA = C_MASK + 3 * P
C_DESC = C_IOTA + CAP
C_COS = C_DESC + EPG
C_SIN = C_COS + NT * ROPE // 2
C_CB = C_SIN + NT * ROPE // 2
C_VIS = C_CB + NT * H * CMP_PAD
C_DIST = C_VIS + NT
C_BLK = C_DIST + 3 * P
C_STK = C_BLK + P // CMP_PAD
C_END = C_STK + NRP
FAR = 1e32


def shape_constants():
    c = np.zeros((P, C_END), np.float32)
    p = np.arange(P)
    c[:, C_ID:C_ID + P] = np.eye(P)
    c[:, C_AID:C_AID + P] = np.eye(P) * ALPHA
    c[:, C_TRI:C_TRI + P] = p[:, None] < p[None, :]
    hidden = np.where(p[None, :] <= p[:, None], 0.0, -NEG)
    c[:, C_MASK:C_MASK + P] = hidden
    c[:, C_MASK + 2 * P:C_MASK + 3 * P] = hidden
    c[:, C_IOTA:C_IOTA + CAP] = np.arange(CAP)
    c[:, C_DESC:C_DESC + EPG] = EPG - np.arange(EPG)
    half = ROPE // 2
    freq = np.float32(10000.0) ** (-np.arange(half, dtype=np.float32) / half)
    tok = (np.arange(NT)[None, :] * P + p[:, None])
    ang = tok[:, :, None].astype(np.float32) * freq
    c[:, C_COS:C_SIN] = np.cos(ang).reshape(P, -1)
    c[:, C_SIN:C_CB] = np.sin(ang).reshape(P, -1)
    slopes = (2.0 ** (-8.0 * np.arange(1, H + 1) / H)).astype(np.float32)
    end = np.arange(NCMP) * CMP_STRIDE + CMP_LEN - 1
    dist = (tok[:, :, None] - end).astype(np.float32)
    cb = np.full((P, NT, H, CMP_PAD), NEG, np.float32)
    cb[..., 0:NCMP] = np.where(dist[:, :, None, :] >= 0, -slopes[:, None] * dist[:, :, None, :], NEG)
    c[:, C_CB:C_VIS] = cb.reshape(P, -1)
    c[:, C_VIS:C_DIST] = (dist >= 0).any(-1)
    d = np.concatenate([tok[:, t, None] - np.arange((t + 1) * P) for t in range(NT)], 1)
    c[:, C_DIST:C_BLK] = np.where(d >= 0, d, FAR)
    c[:, C_BLK:C_STK] = p[:, None] // CMP_PAD == np.arange(P // CMP_PAD)
    c[:, C_STK:C_END] = p[:, None] % NRP == np.arange(NRP)
    return c, slopes


class PsumPlan:

    def __init__(self):
        self.count = [0] * 8
        self.at = {}

    def add(self, name, bank):
        self.count[bank] += 1
        self.at[name] = (bank, self.count[bank], 0)

    def add_loop(self, names_banks, iterations):
        per = [sum(1 for _, b in names_banks if b == k) for k in range(8)]
        seen = [0] * 8
        for name, bank in names_banks:
            seen[bank] += 1
            self.at[name] = (bank, self.count[bank] + seen[bank], per[bank])
        for k in range(8):
            self.count[k] += per[k] * iterations


def psum_plan():
    plan = PsumPlan()

    def transposed(name):
        for s in range(4):
            plan.add(f"{name}{s}", s)

    def experts(l):
        plan.add(f"logitsT{l}", 0)
        plan.add(f"logits{l}", 1)
        plan.add(f"position{l}", 0)
        plan.add(f"gather_a{l}", 2)
        plan.add(f"gather_b{l}", 3)
        plan.add(f"overflow{l}", 1)
        names = [("h1", 0), ("h3", 1), ("next_a", 2), ("next_b", 3), ("hidT", 0), ("scatT", 1), ("w2_0", 2), ("w2_1", 3)]
        for n, b in names:
            plan.add(f"{n}.{l}first", b)
        plan.add_loop([(f"{n}.{l}", b) for n, b in names], PAIRS - 2)
        for n, b in names:
            if not n.startswith("next"):
                plan.add(f"{n}.{l}last", b)
        for q in range(4):
            plan.add(f"moe_y{l}{q}", 4 + q)

    for q in range(4):
        plan.add(f"lat{q}", q)
    for q in range(3):
        plan.add(f"latT{q}", 4 + q)
    for o in range(14):
        plan.add(f"qkv{o}", (o + 7) % 8)
    for h in range(H):
        plan.add(f"headT{h}", h % 2)
        plan.add(f"score{h}", 2 + h % 2)
        plan.add(f"probT{h}", 4 + h % 2)
    for i in range(H // 2):
        plan.add(f"mla_o{i}", 6 + i % 2)
    for q in range(4):
        plan.add(f"mla_y{q}", 4 + q)
    transposed("x1T")
    experts(0)
    transposed("x2T")
    for q in range(4):
        plan.add(f"nq{q}", 4 + q)
    for n, b in (("kc", 0), ("vc", 1), ("vwg0", 2), ("vwg1", 3), ("cmp", 4), ("ks", 5), ("vrep", 6), ("cs", 7),
                 ("kw", 4), ("vs", 6), ("pcT", 7)):
        plan.add(n, b)
    for h in range(H):
        plan.add(f"near{h}", h % 2)
        plan.add(f"far{h}", 2 + h % 2)
        plan.add(f"nprobT_a{h}", 4)
        plan.add(f"nprobT_b{h}", 5)
    for i in range(H // 2):
        plan.add(f"nsa_o{i}", 6 + i % 2)
    for q in range(4):
        plan.add(f"nsa_y{q}", 4 + q)
    transposed("x3T")
    experts(1)
    return plan


MLA_LOADS = 6
NSA_LOADS = 8
MOE_LOADS = 6 * PAIRS - EXTRA
LOAD0 = {"mla": 0, "moe0": MLA_LOADS, "nsa": MLA_LOADS + MOE_LOADS, "moe1": MLA_LOADS + MOE_LOADS + NSA_LOADS}
MLA_DONE = ["lat3", "qkv5", "qkv5", "qkv13", "mla_y3", "mla_y3"]
NSA_DONE = ["nq1", "nq3", "vc", "kw", "vwg1", "vs", "nsa_y3", "nsa_y3"]
PAIR_DONE = ["h1", "h1", "h3", "h3", "w2_1", "w2_1"]


def build(nc, a):
    plan = psum_plan()
    slopes = shape_constants()[1]
    with ExitStack() as ctx:
        def sb(name, cols, dt=F32):
            return ctx.enter_context(nc.sbuf_tensor(name, [P, cols], dt))

        def sem(name):
            return ctx.enter_context(nc.semaphore(name))

        ring = sb("ring", RING * SLOT)
        const = sb("const", C_END)
        x_t = sb("x_tok", NT * D)
        xT_t = sb("xT", KD * S)
        small = sb("small", 640)
        counts = sb("counts", 4, I32)
        WORK = 21200
        work = sb("work", WORK)
        bank = [ctx.enter_context(nc.psum_tensor(f"bank{b}", [P, NB], F32)) for b in range(8)]

        class Region:
            def __init__(self, base, at=0):
                self.base, self.at = base, at

            def take(self, cols):
                self.at += cols
                assert self.at <= self.base.shape[1], (self.at, self.base.shape)
                return self.base[:, self.at - cols:self.at]

        def slot(s):
            return ring[:, s * SLOT:(s + 1) * SLOT]

        ident = const[:, C_ID:C_ID + P]
        alpha_ident = const[:, C_AID:C_AID + P]
        tri = const[:, C_TRI:C_TRI + P]
        mask = const[:, C_MASK:C_MASK + 3 * P]
        iota = const[:, C_IOTA:C_IOTA + CAP]
        desc = const[:, C_DESC:C_DESC + EPG]
        cos = const[:, C_COS:C_SIN].rearrange("p (t f) -> p t f", t=NT)
        sin = const[:, C_SIN:C_CB].rearrange("p (t f) -> p t f", t=NT)
        cmp_bias = const[:, C_CB:C_VIS].rearrange("p (t h n) -> p t h n", t=NT, h=H)
        any_visible = const[:, C_VIS:C_DIST]
        dist = const[:, C_DIST:C_BLK]
        own_block = const[:, C_BLK:C_STK]
        stacked_ident = const[:, C_STK:C_END]
        x_tok = x_t[:, :].rearrange("p (t d) -> p t d", t=NT)
        xT = xT_t[:, :].rearrange("p (k s) -> p k s", k=KD)
        gain, shift = work[:, 0:D], work[:, D:2 * D]

        sm = Region(small)
        bn = sm.take(NT * 2 * 6).rearrange("p (t c s) -> p t c s", t=NT, c=2)
        mv = sm.take(NT * 2).rearrange("p (t s) -> p t s", t=NT)
        var_eps = sm.take(4)
        neg_half = sm.take(4)
        rstd = sm.take(4)
        sumsq = sm.take(4)
        rms = sm.take(4)
        key_rms = sm.take(NT)
        rms_gain = sm.take(CQ + CKV)
        router_b = sm.take(NR)
        ones = sb("ones", P)
        lg = sm.take(NT * NR).rearrange("p (t c) -> p t c", t=NT)

        def per_token(cols):
            return sm.take(NT * cols).rearrange("p (t c) -> p t c", t=NT)
        r1, r2, gmax, pg_top = per_token(1), per_token(1), per_token(1), per_token(1)
        e4, p4, k4, group1h = per_token(4), per_token(4), per_token(4), per_token(4)
        first1h, second1h, gate4 = per_token(4), per_token(4), per_token(4)
        v1, v2 = per_token(1), per_token(1)
        m4, le4, both = per_token(4), per_token(4), per_token(4)
        prod16 = per_token(NE)
        member = per_token(NE)
        gates = per_token(NE)
        posm = per_token(NE)
        over = per_token(NE)
        rest_gates = per_token(NE)
        router_w = sb("router_w", KD * NRP)
        rw = router_w[:, :].rearrange("p (k c) -> p k c", k=KD)

        OT_AT = 2 * D
        assert OT_AT + KD * S == SLOT
        oT_f = work[:, OT_AT:SLOT]
        EXPERTS_AT = SLOT
        EXTRA_AT = [WORK - (EXTRA - 1 - x) * SLOT for x in range(EXTRA - 1)] + [0]

        m = Region(work, SLOT)
        q_tok = m.take(NT * H * DQ)
        k_tok = m.take(NT * H * DQ)
        v_tok = m.take(NT * H * VD)
        lat = m.take(NT * LAT)
        latT = m.take((CQ + CKV) * S)
        m_spt = m.take(8 * 3 * P)
        m_s = [m_spt[:, i * 3 * P:(i + 1) * 3 * P] for i in range(4)]
        m_pt = [m_spt[:, (4 + i) * 3 * P:(5 + i) * 3 * P] for i in range(4)]
        RT = NT * H * ROPE // 2
        rt = [m_spt[:, i * RT:(i + 1) * RT] for i in range(4)]
        square = m_spt[:, 0:QR]
        m_qk = [m.take(2 * S) for _ in range(3)]
        m_z = m.take(NT * H)
        m_rz = m.take(NT * H)
        m_nm = m.take(H * NT)
        q4 = q_tok.rearrange("p (t h d) -> p t h d", t=NT, h=H)
        k4d = k_tok.rearrange("p (t h d) -> p t h d", t=NT, h=H)
        v4 = v_tok.rearrange("p (t h d) -> p t h d", t=NT, h=H)
        lat3 = lat.rearrange("p (t c) -> p t c", t=NT)
        latT3 = latT.rearrange("p (j s) -> p j s", j=CQ + CKV)
        z3 = m_z.rearrange("p (h t) -> p h t", h=H)
        rz3 = m_rz.rearrange("p (h t) -> p h t", h=H)
        nm3 = m_nm.rearrange("p (h t) -> p h t", h=H)
        oT = oT_f.rearrange("p (i s) -> p i s", i=KD)

        n = Region(work, SLOT)
        nqT_f = oT_f
        kz_f = n.take(2 * G * 2 * S)
        kbd_f = n.take(G * 2 * CMP_PAD)
        vsw_f = n.take(2 * NT * KVC)
        vrep_f = n.take(G * HPG * CMP_PAD)
        vbd_f = n.take(H // 2 * P)
        pct_f = n.take(2 * S)
        n_s4 = n.take(4 * 6 * P)
        n_s = [n_s4[:, i * 6 * P:(i + 1) * 6 * P] for i in range(4)]
        sc_f = n_s[3][:, 0:NT * H * CMP_PAD]
        n_pt4 = n.take(4 * 6 * P)
        n_pt = [n_pt4[:, i * 6 * P:(i + 1) * 6 * P] for i in range(4)]
        streams_f = n_pt4[:, 0:2 * G * S]
        n_bias = [n.take(3 * P) for _ in range(2)]
        cmp_f = n.take(2 * G * CMP_PAD)
        nqT = nqT_f.rearrange("p (i s) -> p i s", i=H // 2)
        kz = kz_f.rearrange("p (x g b s) -> p x g b s", x=2, g=G, b=2)
        kbd = kbd_f.rearrange("p (g n) -> p g n", g=G)
        vsw = vsw_f.rearrange("p (b t c) -> p b t c", b=2, t=NT)
        streams = streams_f.rearrange("p (w g s) -> p w g s", w=2, g=G)
        vbd = vbd_f.rearrange("p (i c) -> p i c", i=H // 2)
        sc = sc_f.rearrange("p (r c) -> p r c", c=CMP_PAD)
        pct = pct_f.rearrange("p (u s) -> p u s", u=2)
        nsm = sb("nsa_small", NT * NGATE + 4 * H * 4 + 3 * NT * H)
        ns = Region(nsm)
        n_gate = ns.take(NT * NGATE)
        n_nm = ns.take(H * NT * 2)
        n_z = ns.take(H * NT * 2)
        n_rz = ns.take(H * NT * 2)
        n_cf = ns.take(H * NT * 2)
        c_mx = ns.take(NT * H)
        c_z = ns.take(NT * H)
        c_cf = ns.take(NT * H)
        pos_t = sb("cmp_posT", CMP_STRIDE)
        gate3 = n_gate.rearrange("p (r b) -> p r b", b=3)
        gate4d = n_gate.rearrange("p (t h b) -> p t h b", t=NT, b=3)
        v4d = {k: v.rearrange("p (h t b) -> p h t b", h=H, t=NT) for k, v in dict(nm=n_nm, z=n_z, rz=n_rz, cf=n_cf).items()}

        e = Region(work, EXPERTS_AT)
        xe_f = e.take(KD * 2 * CAP)
        xe = xe_f.rearrange("p (k c) -> p k c", k=KD)
        pick_f = e.take(NT * 2 * CAP)
        pick = pick_f.rearrange("p (t c) -> p t c", t=NT)
        scat_f = e.take(NT * 2 * CAP)
        scat = scat_f.rearrange("p (t c) -> p t c", t=NT)
        scatT_f = e.take(NT * P)
        silu = e.take(FF)
        lgT = silu[:, 0:S]
        hid = e.take(FF)
        hidT_f = e.take(KF * P)
        hidT = hidT_f.rearrange("p (c s) -> p c s", c=KF)
        ye = e.take(D)
        assert e.at <= EXTRA_AT[0]

        bank_filled = [sem(f"bank{b}_filled") for b in range(8)]
        bank_drained = [sem(f"bank{b}_drained") for b in range(8)]
        slot_loaded = [sem(f"slot{s}_loaded") for s in range(RING)]
        x_loaded, const_loaded = sem("x_loaded"), sem("const_loaded")
        xT_loaded = [sem(f"xT{i}_loaded") for i in range(KD // 2)]
        w_in_loaded = [sem(f"w_in{i}_loaded") for i in range(KD // 2 - 1)]
        phi_loaded = sem("phi_loaded")
        extra_loaded = [sem(f"extra{i}_loaded") for i in range(EXTRA)]
        rms_loaded, router_loaded, ln_loaded = sem("rms_loaded"), sem("router_loaded"), sem("ln_loaded")
        nsa_loaded = sem("nsa_tables_loaded")
        consts_set = sem("consts_set")
        dve_step, act_step = sem("dve_step"), sem("act_step")
        var_ready, rstd_ready = sem("variance_ready"), sem("rstd_ready")
        x_ready = sem("x_ready")
        sumsq_ready = sem("sumsq_ready")
        key_rms_ready, rope_ready = sem("key_rms_ready"), sem("rope_ready")
        raw_prob, prob_ready = sem("raw_probs_ready"), sem("probs_ready")
        logit_exp_in, logit_exp_out = sem("router_exp_in"), sem("router_exp_out")
        member_ready, over_ready, count_ready = sem("member_ready"), sem("over_ready"), sem("count_ready")
        pick_ready, scat_ready, silu_ready, scattered = sem("pick_ready"), sem("scat_ready"), sem("silu_ready"), sem("scattered")
        pos_placed, cmp_kv_ready = sem("cmp_pos_placed"), sem("cmp_keys_values_ready")
        cmp_in, cmp_exp, cmp_prob = sem("cmp_scores_ready"), sem("cmp_exp_ready"), sem("cmp_probs_ready")
        nsa_zeroed, gate_exp, bias_ready = sem("nsa_memory_zeroed"), sem("gate_exp_ready"), sem("alibi_bias_ready")
        nraw_prob, nprob_ready = sem("nsa_raw_probs_ready"), sem("nsa_probs_ready")
        rest = [{k: sem(f"rest{l}_{k}") for k in ("loaded", "h", "silu", "hid", "hidT", "hidT_copied", "rounds")}
                for l in range(DEPTH)]
        out_written = sem("out_written")

        def number(name, i):
            b, first, per = plan.at[name]
            return b, first if i is None or not per else first + per * i

        def filled(eng, name, i=None):
            b, k = number(name, i)
            eng.wait_ge(bank_filled[b], k)

        def drained(eng, name, i=None):
            b, k = number(name, i)
            eng.wait_ge(bank_drained[b], k)

        def may_fill(eng, name, i=None):
            b, k = number(name, i)
            if not (isinstance(k, int) and k == 1):
                eng.wait_ge(bank_drained[b], k - 1)

        def normed(eng, k, t):
            eng.wait_ge(x_ready, 2 * (NT * k + t + 1))

        def fill(ins, name):
            ins.then_inc(bank_filled[plan.at[name][0]], 1)

        def drain(ins, name):
            ins.then_inc(bank_drained[plan.at[name][0]], 1)

        def bk(name):
            return bank[plan.at[name][0]]

        class Steps:

            def __init__(self, eng, sem_):
                self.eng, self.sem, self.n = eng, sem_, 0

            def __call__(self, ins):
                ins.then_inc(self.sem, 1)
                self.n += 1

            def wait(self):
                self.eng.wait_ge(self.sem, self.n)

        def loaded(eng, j, i=None, per=1):
            k = 16 * (j // RING + 1)
            eng.wait_ge(slot_loaded[j % RING], k if i is None else k + 16 * per * i)

        block = ctx.enter_context(nc.Block())
        w_in = a["mla_w_in"].rearrange("(p k) n -> p k n", k=KD)
        w_qb = a["mla_w_qb"].rearrange("(p c) n -> p c n", c=CQ)
        w_kvb = a["mla_w_kvb"].rearrange("(p c) n -> p (c n)", c=CKV)
        w_o = [a[k].rearrange("(k p) n -> p k n", k=KD) for k in ("mla_w_o", "nsa_w_o")]
        n_in = a["nsa_w_in"].rearrange("(p k) n -> p k n", k=KD)
        w1 = a["moe_w1"].rearrange("e (p k) n -> e p (k n)", k=KD)
        w3 = a["moe_w3"].rearrange("e (p k) n -> e p (k n)", k=KD)
        w2 = a["moe_w2"].rearrange("e (p c) n -> e p (c n)", c=KF)
        def s3(s, cols, chunks, off=0):
            return ring[:, s * SLOT + off:s * SLOT + off + cols * chunks].rearrange("p (k n) -> p k n", k=chunks)

        def extra_slot(x, cols, chunks):
            return work[:, EXTRA_AT[x]:EXTRA_AT[x] + SLOT].rearrange("p (k n) -> p k n", k=chunks)

        def at_expert(w, idx):
            return w[bass.ds(idx, 1), :, :].rearrange("o p n -> (o p) n")

        def qkv_copy(scaled, o):
            nm = f"qkv{o}"
            b = bk(nm)
            if o < 6:
                t, nn = divmod(o, 3)
                drain(scaled(q_tok[:, (t * 3 + nn) * NB:(t * 3 + nn + 1) * NB], b[:, :], rms[:, 2 * t:2 * t + 1]), nm)
            else:
                t, nn = divmod(o - 6, 4)
                src = b[:, :].rearrange("p (h d) -> p h d", h=4)
                scaled(k4d[:, t, 4 * nn:4 * nn + 4, 0:NOPE], src[:, :, 0:NOPE], key_rms[:, t:t + 1])
                drain(scaled(v4[:, t, 4 * nn:4 * nn + 4, :], src[:, :, NOPE:], rms[:, 2 * t + 1:2 * t + 2]), nm)

        def shifted_streams(times, nm, w):
            psum = bk(nm)[:, :].rearrange("p (q s) -> p q s", q=2)
            for x in range(2):
                for y in range(2):
                    src = psum[64 * x:64 * x + 64, :, CMP_STRIDE * y:CMP_STRIDE * (y + NCMP)]
                    ins = times(streams[64 * y:64 * y + 64, w, x::2, 0:CMP_STRIDE * NCMP], src, 1.0)
            drain(ins, nm)

        def padded_keys(times, nm, b):
            src = bk(nm)[:, :].rearrange("p (q s) -> p q s", q=2)
            for gx in range(2):
                for x in range(2):
                    ins = times(kz[64 * x:64 * x + 64, x, gx::2, b, :], src[64 * gx:64 * gx + 64, :, :], -1.0)
            drain(ins, nm)

        TILE_COLS = ((0, P), (P, 3 * P))

        @block.sync
        def _(sp):
            def done_name(j):
                if j < LOAD0["moe0"]:
                    return MLA_DONE[j], None
                for l, key in enumerate(("moe0", "moe1")):
                    r = j - LOAD0[key]
                    if 0 <= r < 6 - EXTRA:
                        return f"{PAIR_DONE[r]}.{l}first", None
                    r += EXTRA
                    if 6 <= r < 6 * PAIRS:
                        nm = f"{PAIR_DONE[r % 6]}.{l}"
                        return (nm + "last", None) if r // 6 == PAIRS - 1 else (nm, r // 6 - 1)
                return NSA_DONE[j - LOAD0["nsa"]], None

            def free(j):
                if j >= RING:
                    nm, i = done_name(j - RING)
                    filled(sp, nm, i)

            def load(j, out, in_):
                free(j)
                sp.dma_start(out, in_).then_inc(slot_loaded[j % RING], 16)

            for i in range(KD // 2):
                sp.dma_start(xT[:, 2 * i:2 * i + 2, :], a["xT"][:, 2 * i * S:(2 * i + 2) * S]
                             .rearrange("p (k s) -> p k s", k=2)).then_inc(xT_loaded[i], 16)
                sp.dma_start(s3(0, LAT, KD)[:, 2 * i:2 * i + 2, :], w_in[:, 2 * i:2 * i + 2, :]).then_inc(
                    w_in_loaded[i] if i < KD // 2 - 1 else slot_loaded[0], 16)
            sp.dma_start(s3(0, H * DQ, 1, off=KD * LAT), w_qb[:, 2:3, :]).then_inc(slot_loaded[1], 16)
            sp.dma_start(s3(2, H * DQ, 2), w_qb[:, 0:2, :]).then_inc(slot_loaded[2], 16)
            sp.dma_start(slot(3), w_kvb).then_inc(slot_loaded[3], 16)
            sp.dma_start(s3(4, D, 4), w_o[0][:, 0:4, :]).then_inc(slot_loaded[4], 16)
            sp.dma_start(s3(5, D, 4), w_o[0][:, 4:8, :]).then_inc(slot_loaded[5], 16)

            def experts(l):
                j0 = LOAD0[f"moe{l}"]
                e0 = l * NE
                order = ((w1, 0), (w1, 1), (w3, 0), (w3, 1), (w2, 0), (w2, 1))
                j1 = j0 + 6 - EXTRA

                def ring_load(j, s, e):
                    load(j, slot(j % RING), at_expert(order[s][0], e + order[s][1]))

                def lent(x):
                    w, y = order[6 - EXTRA + x]
                    sp.dma_start(extra_slot(x, SLOT, 1)[:, 0, :], at_expert(w, e0 + y)).then_inc(extra_loaded[x], 16)

                for s in range(6 - EXTRA):
                    ring_load(j0 + s, s, e0)
                for s in (0, 1):
                    ring_load(j1 + s, s, e0 + 2)
                for i in (H // 2 - 2, H // 2 - 1):
                    drained(sp, f"{('mla', 'nsa')[l]}_o{i}")
                for x in range(EXTRA - 1):
                    lent(x)
                for s in (2, 3):
                    ring_load(j1 + s, s, e0 + 2)
                normed(sp, 2 * l, NT - 1)
                lent(EXTRA - 1)
                for s in (4, 5):
                    ring_load(j1 + s, s, e0 + 2)
                with sp.Fori(0, PAIRS - 2) as i:
                    for s, (w, x) in enumerate(order):
                        filled(sp, f"{PAIR_DONE[s]}.{l}", i)
                        sp.dma_start(slot((j1 + s) % RING), at_expert(w, i * 2 + (e0 + 4 + x))).then_inc(
                            slot_loaded[(j1 + s) % RING], 16)

            def rest_of_tokens(l):
                r = rest[l]
                sp.wait_ge(count_ready, l + 1)
                total = sp.value_load(counts[0:1, l:l + 1], min_val=0, max_val=S * 2)
                with sp.If(total > 0):
                    filled(sp, f"w2_1.{l}last")
                    with sp.Fori(0, NE) as i:
                        sp.wait_ge(r["rounds"], i * NT + 1)
                        for s, w in enumerate((w1, w3, w2)):
                            sp.dma_start(slot(s), at_expert(w, i + l * NE)).then_inc(r["loaded"], 16)
                    sp.wait_ge(r["rounds"], NE * NT + 1)
                sp.nop()

            experts(0)
            rest_of_tokens(0)
            j = LOAD0["nsa"]
            for c in range(3):
                load(j + c, s3((j + c) % RING, NSA_COLS, KD), n_in[:, :, c * NSA_COLS:(c + 1) * NSA_COLS])
            free(j + 3)
            sp.dma_start(s3((j + 3) % RING, SLOT // 2, 1)[:, 0, :], a["phi"]).then_inc(phi_loaded, 16)
            sp.dma_start(s3((j + 3) % RING, KVC, KD, off=SLOT // 2), n_in[:, :, H * HD + 4 * KVC:H * HD + 5 * KVC]).then_inc(
                slot_loaded[(j + 3) % RING], 16)
            load(j + 4, s3((j + 4) % RING, KVC + NGATE, KD), n_in[:, :, H * HD + 5 * KVC:])
            load(j + 5, s3((j + 5) % RING, NSA_COLS, KD), n_in[:, :, 3 * NSA_COLS:4 * NSA_COLS])
            load(j + 6, s3((j + 6) % RING, D, 4), w_o[1][:, 0:4, :])
            load(j + 7, s3((j + 7) % RING, D, 4), w_o[1][:, 4:8, :])
            experts(1)
            rest_of_tokens(1)
            for t in range(NT):
                for half in range(2):
                    sp.wait_ge(x_ready, 2 * (3 * NT + t) + half + 1)
                    cols = slice(half * NB, (half + 1) * NB)
                    sp.dma_start(a["out"][t * P:(t + 1) * P, cols], x_tok[:, t, cols]).then_inc(out_written, 16)
            sp.wait_ge(out_written, 16 * 2 * NT)

        @block.gpsimd
        def _(pool):
            pool.dma_start(const[:, :], a["const"]).then_inc(const_loaded, 16)
            pool.dma_start(rms_gain, a["rms_gain"]).then_inc(rms_loaded, 16)
            pool.memset(neg_half, -0.5).then_inc(consts_set, 1)
            pool.memset(ones[:, :], 1.0).then_inc(consts_set, 1)

            def load_router(l):
                pool.dma_start(router_w[:, :], a["router_w"][l]).then_inc(router_loaded, 16)
                pool.dma_start(router_b, a["router_b"][l:l + 1, :].to_broadcast([P, NR])).then_inc(router_loaded, 16)

            def load_ln(k):
                if k:
                    normed(pool, k - 1, NT - 1)
                if k % 2:
                    filled(pool, f"w2_1.{k // 2}first")
                pool.dma_start(gain, a["ln"][2 * k:2 * k + 1, :].to_broadcast([P, D])).then_inc(ln_loaded, 16)
                pool.dma_start(shift, a["ln"][2 * k + 1:2 * k + 2, :].to_broadcast([P, D])).then_inc(ln_loaded, 16)

            pool.wait_ge(consts_set, 2)

            def inverse_root(k, out, in_):
                pool.wait_ge(var_ready, k + 1)
                pool.tensor_tensor(out, in_, neg_half[:, 0:out.shape[1]], ALU.pow).then_inc(rstd_ready, 1)

            def norm_roots(k):
                for t in range(NT):
                    inverse_root(1 + NT * k + t, rstd[:, t:t + 1], var_eps[:, t:t + 1])

            filled(pool, "lat1")
            pool.dma_start(x_tok, a["x"].rearrange("(t p) d -> p t d", t=NT)).then_inc(x_loaded, 16)
            load_ln(0)
            load_router(0)
            inverse_root(0, rms, sumsq)
            norm_roots(0)
            load_ln(1)
            norm_roots(1)
            load_ln(2)
            load_router(1)
            pool.dma_start(pos_t[:, :], a["cmp_posT"]).then_inc(nsa_loaded, 16)
            pool.memset(kbd_f, 0.0).then_inc(nsa_zeroed, 1)
            pool.memset(vrep_f, 0.0).then_inc(nsa_zeroed, 1)
            pool.memset(kz_f, 0.0).then_inc(nsa_zeroed, 1)
            pool.wait_ge(const_loaded, 16)
            for h in range(H):
                if h >= 2:
                    drained(pool, f"far{h - 2}")
                pool.tensor_scalar(n_bias[h % 2], dist, float(slopes[h]), None, ALU.mult).then_inc(bias_ready, 1)
            norm_roots(2)
            load_ln(3)
            norm_roots(3)

        @block.tensor
        def _(pe):
            def transposes(name, k, after=lambda t: None):
                for s in range(4):
                    t, kh = divmod(s, 2)
                    if kh == 0:
                        normed(pe, k, t)
                    may_fill(pe, f"{name}{s}")
                    for c in range(4):
                        ins = pe.transpose(bk(f"{name}{s}")[:, c * P:(c + 1) * P], x_tok[:, t, 4 * kh + c::KD], ident)
                    fill(ins, f"{name}{s}")
                    if kh == 1:
                        after(t)

            def alpha_x(l, t):
                for half in range(2):
                    nm = f"moe_y{l}{2 * t + half}"
                    may_fill(pe, nm)
                    ins = pe.matmul(bk(nm)[:, :], alpha_ident, x_tok[:, t, half * NB:(half + 1) * NB],
                                    start=True, stop=False, skip_group_check=True)
                if t == NT - 1:
                    ins.then_inc(scattered, 1)

            def out_projection(name, j, outs):
                for i in (H // 2 - 2, H // 2 - 1):
                    drained(pe, f"{outs}{i}")
                for t in range(NT):
                    for half in range(2):
                        may_fill(pe, f"{name}{2 * t + half}")
                    for k in range(KD):
                        if t == 0 and k % 4 == 0:
                            loaded(pe, j + k // 4)
                        w = s3((j + k // 4) % RING, D, 4)
                        for half in range(2):
                            nm = f"{name}{2 * t + half}"
                            ins = pe.matmul(bk(nm)[:, :], oT[:, k, t * P:(t + 1) * P],
                                            w[:, k % 4, half * NB:(half + 1) * NB], start=(k == 0), stop=(k == KD - 1))
                            if k == KD - 1:
                                fill(ins, nm)

            def experts(l, xname):
                for s in range(4):
                    drained(pe, f"{xname}{s}")
                pe.wait_ge(router_loaded, 32 * (l + 1))
                nm = f"logitsT{l}"
                may_fill(pe, nm)
                tiles = P // NRP
                for k in range(KD):
                    c = k % tiles
                    ins = pe.matmul(bk(nm)[c * NRP:(c + 1) * NRP, 0:S], rw[:, k, :], xT[:, k, :],
                                    start=(k < tiles), stop=(k >= KD - tiles))
                fill(ins, nm)
                drained(pe, nm)
                may_fill(pe, f"logits{l}")
                for u in range(NT):
                    ins = pe.matmul(bk(f"logits{l}")[:, u * NRP:(u + 1) * NRP], lgT[:, u * P:(u + 1) * P], stacked_ident,
                                    start=True, stop=True)
                fill(ins, f"logits{l}")
                alpha_x(l, 1)
                pe.wait_ge(member_ready, l + 1)
                may_fill(pe, f"position{l}")
                pos = bk(f"position{l}")
                pe.matmul(pos[:, 0:NE], tri, member[:, 0, :], start=True, stop=True)
                pe.matmul(pos[:, NE:2 * NE], ones[:, :], member[:, 0, :], start=True, stop=False)
                fill(pe.matmul(pos[:, NE:2 * NE], tri, member[:, 1, :], start=False, stop=True), f"position{l}")

                def gather(nm, half, i):
                    may_fill(pe, nm, i)
                    for c in range(4):
                        for t in range(NT):
                            ins = pe.matmul(bk(nm)[:, c * P:(c + 1) * P], x_tok[:, t, 4 * half + c::KD], pick[:, t, :],
                                            start=(t == 0), stop=(t == NT - 1))
                    fill(ins, nm)

                pe.wait_ge(pick_ready, l * PAIRS + 1)
                gather(f"gather_a{l}", 0, None)
                gather(f"gather_b{l}", 1, None)
                pe.wait_ge(over_ready, l + 1)
                may_fill(pe, f"overflow{l}")
                fill(pe.matmul(bk(f"overflow{l}")[:, 0:NT * NE], ones[:, :], over.rearrange("p t c -> p (t c)"),
                               start=True, stop=True), f"overflow{l}")
                j0 = LOAD0[f"moe{l}"]

                def two_experts(out, src, ws, chunks, cols):
                    for k in range(chunks):
                        for x in range(2):
                            ins = pe.matmul(out[CAP * x:CAP * (x + 1), :], src[:, k, CAP * x:CAP * (x + 1)],
                                            ws[x][:, k, cols], start=(k == 0), stop=(k == chunks - 1))
                    return ins

                def pair(i, tag, nth):
                    first, last = tag == "first", tag == "last"
                    j = j0 + 6 - EXTRA + (RING * (PAIRS - 2) if last else 0)
                    h1, h3, hT, sT, y0, y1 = [f"{k}.{l}{tag}" for k in ("h1", "h3", "hidT", "scatT", "w2_0", "w2_1")]

                    def slots(a_, b_, cols, chunks):
                        out = []
                        for s in (a_, b_):
                            if first and s >= 6 - EXTRA:
                                x = s - (6 - EXTRA)
                                pe.wait_ge(extra_loaded[x], 16 * (l + 1))
                                out.append(extra_slot(x, cols, chunks))
                            else:
                                js = j0 + s if first else j + s
                                loaded(pe, js, i)
                                out.append(s3(js % RING, cols, chunks))
                        return out

                    may_fill(pe, h1, i)
                    ws = slots(0, 1, FF, KD)
                    fill(two_experts(bk(h1), xe, ws, KD, slice(0, FF)), h1)
                    may_fill(pe, h3, i)
                    ws = slots(2, 3, FF, KD)
                    fill(two_experts(bk(h3), xe, ws, KD, slice(0, FF)), h3)
                    if not last:
                        pe.wait_ge(pick_ready, nth + 1)
                        gather(f"next_a.{l}{tag}", 0, i)
                    drained(pe, h3, i)
                    may_fill(pe, hT, i)
                    for c in range(KF):
                        ins = pe.transpose(bk(hT)[:, c * P:(c + 1) * P], hid[:, c::KF], ident)
                    fill(ins, hT)
                    if not last:
                        gather(f"next_b.{l}{tag}", 1, i)
                    pe.wait_ge(scat_ready, nth)
                    may_fill(pe, sT, i)
                    for t in range(NT):
                        ins = pe.transpose(bk(sT)[:, t * P:(t + 1) * P], scat[:, t, :], ident)
                    fill(ins, sT)
                    drained(pe, hT, i)
                    ws = slots(4, 5, D, KF)
                    for half, nm in enumerate((y0, y1)):
                        may_fill(pe, nm, i)
                        fill(two_experts(bk(nm), hidT, ws, KF, slice(half * NB, (half + 1) * NB)), nm)
                    drained(pe, sT, i)
                    for half, nm in enumerate((y0, y1)):
                        drained(pe, nm, i)
                        for t in range(NT):
                            q = 2 * t + half
                            ins = pe.matmul(bk(f"moe_y{l}{q}")[:, :], scatT_f[:, t * P:(t + 1) * P],
                                            ye[:, half * NB:(half + 1) * NB], start=False, stop=last, skip_group_check=True)
                            if last:
                                fill(ins, f"moe_y{l}{q}")
                    if not last:
                        ins.then_inc(scattered, 1)

                for nm in (f"gather_a{l}", f"gather_b{l}"):
                    drained(pe, nm)
                pair(None, "first", l * PAIRS + 1)
                for nm in (f"next_a.{l}first", f"next_b.{l}first"):
                    drained(pe, nm)
                with pe.Fori(0, PAIRS - 2) as i:
                    pair(i, "", i + (l * PAIRS + 2))
                    for nm in (f"next_a.{l}", f"next_b.{l}"):
                        drained(pe, nm, i)
                pair(None, "last", (l + 1) * PAIRS)

            def rest_of_tokens(l):
                r = rest[l]
                pe.wait_ge(count_ready, l + 1)
                total = pe.value_load(counts[0:1, l:l + 1], min_val=0, max_val=S * 2)
                with pe.If(total > 0):
                    pe.wait_ge(r["rounds"], 1)
                    with pe.Fori(0, NE) as i:
                        pe.wait_ge(r["loaded"], i * 48 + 48)
                        for t in range(NT):
                            u = i * NT + t
                            for b, s in ((0, 0), (1, 1)):
                                for k in range(KD):
                                    ins = pe.matmul(bank[b][:, :], xT[:, k, t * P:(t + 1) * P], s3(s, FF, KD)[:, k, :],
                                                    start=(k == 0), stop=(k == KD - 1))
                            ins.then_inc(r["h"], 1)
                            pe.wait_ge(r["hid"], u + 1)
                            for c in range(KF):
                                ins = pe.transpose(bank[2][:, c * P:(c + 1) * P], hid[:, c::KF], ident)
                            ins.then_inc(r["hidT"], 1)
                            pe.wait_ge(r["hidT_copied"], u + 1)
                            for half in range(2):
                                for c in range(KF):
                                    ins = pe.matmul(bank[4 + 2 * t + half][:, :], hidT[:, c, :],
                                                    s3(2, D, KF)[:, c, half * NB:(half + 1) * NB],
                                                    start=False, stop=True, skip_group_check=True)
                            ins.then_inc(r["rounds"], 1)
                pe.nop()

            pe.wait_ge(consts_set, 2)
            for k in range(KD):
                if k % 2 == 0:
                    pe.wait_ge(xT_loaded[k // 2], 16)
                    if k < KD - 2:
                        pe.wait_ge(w_in_loaded[k // 2], 16)
                    else:
                        loaded(pe, 0)
                w = s3(0, LAT, KD)[:, k, :]
                for q in range(4):
                    t, part = divmod(q, 2)
                    c0, c1 = (0, NB) if part == 0 else (NB, LAT)
                    ins = pe.matmul(bk(f"lat{q}")[:, 0:c1 - c0], xT[:, k, t * P:(t + 1) * P], w[:, c0:c1],
                                    start=(k == 0), stop=(k == KD - 1))
                    if k == KD - 1:
                        fill(ins, f"lat{q}")
            pe.wait_ge(const_loaded, 16)
            for q in range(4):
                drained(pe, f"lat{q}")
            for c in range(CQ + CKV):
                nm = f"latT{c // 2}"
                for t in range(NT):
                    src = lat3[:, t, c:QR:CQ] if c < CQ else lat3[:, t, QR + c - CQ:QR + KVR:CKV]
                    ins = pe.transpose(bk(nm)[:, (c % 2) * S + t * P:(c % 2) * S + (t + 1) * P], src, ident)
                if c % 2 or c == CQ + CKV - 1:
                    fill(ins, nm)
            wq = [s3(2, H * DQ, 2)[:, 0, :], s3(2, H * DQ, 2)[:, 1, :], s3(0, H * DQ, 1, off=KD * LAT)[:, 0, :]]
            wkv = s3(3, H * (NOPE + VD), CKV)
            loaded(pe, 2)
            loaded(pe, 1)
            for o in range(14):
                may_fill(pe, f"qkv{o}")
                if o == 0:
                    for q in range(2):
                        drained(pe, f"latT{q}")
                if o == 6:
                    loaded(pe, 3)
                    drained(pe, "latT2")
                t, nn = divmod(o, 3) if o < 6 else divmod(o - 6, 4)
                chunks = CQ if o < 6 else CKV
                for c in range(chunks):
                    w = wq[c] if o < 6 else wkv[:, c, :]
                    j = c if o < 6 else CQ + c
                    ins = pe.matmul(bk(f"qkv{o}")[:, :], latT3[:, j, t * P:(t + 1) * P], w[:, nn * NB:(nn + 1) * NB],
                                    start=(c == 0), stop=(c == chunks - 1))
                fill(ins, f"qkv{o}")
            for o in range(14):
                drained(pe, f"qkv{o}")
            pe.wait_ge(rope_ready, 2)
            for step in range(H + 4):
                h = step
                if h < H:
                    may_fill(pe, f"headT{h}")
                    b = bk(f"headT{h}")
                    for w in range(2):
                        for t in range(NT):
                            src = (q4, k4d)[w][:, t, h, :]
                            ins = pe.transpose(b[0:DQ, w * S + t * P:w * S + (t + 1) * P], src, ident)
                    fill(ins, f"headT{h}")
                h = step - 1
                if 0 <= h < H:
                    drained(pe, f"headT{h}")
                    may_fill(pe, f"score{h}")
                    qk, b = m_qk[h % 3], bk(f"score{h}")
                    pe.matmul(b[:, 0:P], qk[0:DQ, 0:P], qk[0:DQ, S:S + P], start=True, stop=True)
                    fill(pe.matmul(b[:, P:3 * P], qk[0:DQ, P:S], qk[0:DQ, S:2 * S], start=True, stop=True), f"score{h}")
                h = step - 3
                if 0 <= h < H:
                    pe.wait_ge(prob_ready, h + 1)
                    may_fill(pe, f"probT{h}")
                    for c in range(3):
                        ins = pe.transpose(bk(f"probT{h}")[:, c * P:(c + 1) * P], m_s[h % 4][:, c * P:(c + 1) * P], ident)
                    fill(ins, f"probT{h}")
                if step >= 5 and step % 2:
                    i = (step - 5) // 2
                    nm = f"mla_o{i}"
                    may_fill(pe, nm)
                    for x in range(2):
                        drained(pe, f"probT{2 * i + x}")
                    for c0, c1, kt in ((0, S, 0), (P, S, 1)):
                        for x in range(2):
                            h = 2 * i + x
                            src = m_pt[h % 4][:, 0:S] if kt == 0 else m_pt[h % 4][:, S:S + P]
                            ins = pe.matmul(bk(nm)[VD * x:VD * (x + 1), c0:c1], v4[:, kt, h, :], src,
                                            start=(kt == 0), stop=(kt == 1), skip_group_check=True)
                    fill(ins, nm)
            out_projection("mla_y", 4, "mla_o")
            transposes("x1T", 0, after=lambda t: alpha_x(0, t) if t == 0 else None)
            experts(0, "x1T")
            rest_of_tokens(0)

            transposes("x2T", 1)
            for s in range(4):
                drained(pe, f"x2T{s}")
            j0 = LOAD0["nsa"]

            def columns_T(out, w, c0):
                for k in range(KD):
                    ins = pe.matmul(out, w[:, k, c0:c0 + P], xT[:, k, :], start=(k == 0), stop=(k == KD - 1))
                return ins

            def bank_of_columns(nm, w, c0):
                may_fill(pe, nm)
                for x in range(2):
                    ins = columns_T(bk(nm)[:, x * S:(x + 1) * S], w, c0 + x * P)
                fill(ins, nm)

            for c in range(3):
                loaded(pe, j0 + c)
                w = s3((j0 + c) % RING, NSA_COLS, KD)
                for half in range(2):
                    bank_of_columns(f"nq{2 * c + half}" if c < 2 else ("kc", "vc")[half], w, 2 * half * P)
            loaded(pe, j0 + 4)
            w = s3((j0 + 4) % RING, KVC + NGATE, KD)
            for t in range(NT):
                nm = f"vwg{t}"
                may_fill(pe, nm)
                for k in range(KD):
                    ins = pe.matmul(bk(nm)[:, 0:KVC + NGATE], xT[:, k, t * P:(t + 1) * P], w[:, k, :],
                                    start=(k == 0), stop=(k == KD - 1))
                fill(ins, nm)
            pe.wait_ge(phi_loaded, 16)
            phi = s3((j0 + 3) % RING, P, CMP_STRIDE)
            drained(pe, "kc")
            drained(pe, "vc")
            pe.wait_ge(pos_placed, 1)
            may_fill(pe, "cmp")
            for r in range(CMP_STRIDE):
                ins = pe.matmul(bk("cmp")[:, 0:2 * G * CMP_PAD], phi[:, r, :], streams_f[:, r::CMP_STRIDE],
                                start=(r == 0), stop=(r == CMP_STRIDE - 1))
            fill(ins, "cmp")
            loaded(pe, j0 + 5)
            w_s = s3((j0 + 5) % RING, NSA_COLS, KD)
            bank_of_columns("ks", w_s, 0)
            pe.wait_ge(cmp_kv_ready, 1)
            may_fill(pe, "vrep")
            for u in range(2):
                ins = pe.matmul(bk("vrep")[:, u * HD:(u + 1) * HD], vrep_f[:, u * P:(u + 1) * P], ident[:, HD:2 * HD],
                                start=True, stop=True)
            fill(ins, "vrep")
            for q in range(4):
                drained(pe, f"nq{q}")
            may_fill(pe, "cs")
            for t in range(NT):
                for i in range(H // 2):
                    c0 = (t * (H // 2) + i) * 2 * CMP_PAD
                    ins = pe.matmul(bk("cs")[:, c0:c0 + 2 * CMP_PAD], nqT[:, i, t * P:(t + 1) * P], kbd[:, i // 2, :],
                                    start=True, stop=True)
            fill(ins, "cs")
            loaded(pe, j0 + 3)
            bank_of_columns("kw", s3((j0 + 3) % RING, KVC, KD, off=SLOT // 2), 0)
            def nsa_scores(h):
                i, x = divmod(h, 2)
                for t, nm in enumerate((f"near{h}", f"far{h}")):
                    may_fill(pe, nm)
                    w = (t + 1) * P
                    out = bk(nm)[:, 0:2 * w].rearrange("p (b s) -> p b s", b=2)
                    fill(pe.matmul(out, nqT[:, i, t * P:(t + 1) * P], kz[:, x, h // HPG, :, 0:w], start=True, stop=True), nm)

            def selected_values(t):
                for k in range(KD):
                    ins = pe.matmul(bk("vs")[:, t * S:(t + 1) * S], xT[:, k, t * P:(t + 1) * P], w_s[:, k, KVC:2 * KVC],
                                    start=(k == 0), stop=(k == KD - 1))
                return ins

            may_fill(pe, "vs")
            selected_values(0)
            drained(pe, "ks")
            drained(pe, "kw")
            nsa_scores(0)
            nsa_scores(1)
            fill(selected_values(1), "vs")
            pe.wait_ge(cmp_prob, 1)
            may_fill(pe, "pcT")
            for u in range(2):
                for t in range(NT):
                    ins = pe.transpose(bk("pcT")[:, u * S + t * P:u * S + (t + 1) * P],
                                       sc_f[:, t * S + u * P:t * S + (u + 1) * P], ident)
            fill(ins, "pcT")
            for step in range(H + 5):
                h = step
                if 2 <= h < H:
                    nsa_scores(h)
                h = step - 3
                if 0 <= h < H:
                    pe.wait_ge(nprob_ready, h + 1)
                    s = n_s[h % 4]
                    may_fill(pe, f"nprobT_a{h}")
                    for b in range(2):
                        for t in range(NT):
                            c0 = b * P if t == 0 else 2 * P + b * S
                            ins = pe.transpose(bk(f"nprobT_a{h}")[:, b * S + t * P:b * S + (t + 1) * P], s[:, c0:c0 + P], ident)
                    fill(ins, f"nprobT_a{h}")
                    may_fill(pe, f"nprobT_b{h}")
                    for b in range(2):
                        c0 = 2 * P + b * S + P
                        ins = pe.transpose(bk(f"nprobT_b{h}")[:, b * P:(b + 1) * P], s[:, c0:c0 + P], ident)
                    fill(ins, f"nprobT_b{h}")
                if step >= 5 and step % 2:
                    i = (step - 5) // 2
                    nm = f"nsa_o{i}"
                    if i == 0:
                        for src in ("pcT", "vrep", "vs", "vwg0", "vwg1"):
                            drained(pe, src)
                    may_fill(pe, nm)
                    pe.matmul(bk(nm)[:, 0:S], vbd[:, i, :], pct[:, i // 4, :], start=True, stop=False, skip_group_check=True)
                    for part in "ab":
                        for x in range(2):
                            drained(pe, f"nprobT_{part}{2 * i + x}")
                        for b in range(2):
                            for x in range(2):
                                h = 2 * i + x
                                g, kt = h // HPG, "ab".index(part)
                                src = n_pt[h % 4][:, b * S:(b + 1) * S] if kt == 0 else \
                                    n_pt[h % 4][:, 2 * S + b * P:2 * S + (b + 1) * P]
                                ins = pe.matmul(bk(nm)[HD * x:HD * (x + 1), kt * P:S], vsw[:, b, kt, g * HD:(g + 1) * HD], src,
                                                start=False, stop=(kt == 1 and b == 1), skip_group_check=True)
                    fill(ins, nm)
            out_projection("nsa_y", j0 + 6, "nsa_o")
            transposes("x3T", 2, after=lambda t: alpha_x(1, t) if t == 0 else None)
            experts(1, "x3T")
            rest_of_tokens(1)

        @block.scalar
        def _(act):
            def copy(out, in_):
                return act.activation(out, in_, ACT.Copy)

            def times(out, in_, factor):
                return act.activation(out, in_, ACT.Copy, scale=factor)

            def xT_copies(name):
                for s in (0, 1, 3):
                    t, kh = divmod(s, 2)
                    filled(act, f"{name}{s}")
                    drain(copy(xT[:, 4 * kh:4 * kh + 4, t * P:(t + 1) * P],
                               bk(f"{name}{s}")[:, :].rearrange("p (k s) -> p k s", k=4)), f"{name}{s}")

            def router_copy(l):
                filled(act, f"logitsT{l}")
                drain(copy(lgT, bk(f"logitsT{l}")[:, 0:S]), f"logitsT{l}")

            def experts(l):
                filled(act, f"gather_a{l}")
                drain(copy(xe[:, 0:4, :], bk(f"gather_a{l}")[:, :].rearrange("p (k s) -> p k s", k=4)), f"gather_a{l}")
                act.wait_ge(logit_exp_in, l + 1)
                for e_ in (e4, p4):
                    act.activation(e_, e_, ACT.Exp).then_inc(logit_exp_out, 1)

                def pair(i, tag, nth):
                    last = tag == "last"
                    h1, h3, hT, sT, y0, y1 = [f"{k}.{l}{tag}" for k in ("h1", "h3", "hidT", "scatT", "w2_0", "w2_1")]
                    filled(act, h1, i)
                    b, k = number(h3, i)
                    act.wait_ge(bank_drained[b], k - 2)
                    drain(act.activation(silu, bk(h1)[:, :], ACT.Silu), h1)
                    if not last:
                        filled(act, f"next_a.{l}{tag}", i)
                        drain(copy(xe[:, 0:4, :], bk(f"next_a.{l}{tag}")[:, :].rearrange("p (k s) -> p k s", k=4)), f"next_a.{l}{tag}")
                    filled(act, sT, i)
                    act.wait_ge(scattered, nth)
                    drain(copy(scatT_f, bk(sT)[:, 0:NT * P]), sT)
                    filled(act, y0, i)
                    drain(copy(ye[:, 0:NB], bk(y0)[:, :]), y0)

                pair(None, "first", l * PAIRS + 1)
                with act.Fori(0, PAIRS - 2) as i:
                    pair(i, "", i + (l * PAIRS + 2))
                pair(None, "last", (l + 1) * PAIRS)

            def rest_of_tokens(l):
                r = rest[l]
                act.wait_ge(count_ready, l + 1)
                total = act.value_load(counts[0:1, l:l + 1], min_val=0, max_val=S * 2)
                with act.If(total > 0):
                    act.wait_ge(r["rounds"], 1)
                    with act.Fori(0, NE) as i:
                        for t in range(NT):
                            act.wait_ge(r["h"], i * NT + t + 1)
                            act.activation(silu, bank[0][:, :], ACT.Silu).then_inc(r["silu"], 1)
                            act.wait_ge(r["hid"], i * NT + t + 1)
                act.nop()

            for q in (2, 3):
                c0, c1 = (0, NB) if q == 2 else (NB, LAT)
                filled(act, f"lat{q}")
                drain(copy(lat3[:, 1, c0:c1], bk(f"lat{q}")[:, 0:c1 - c0]), f"lat{q}")
            for q in range(4):
                drained(act, f"lat{q}")
            for t in range(NT):
                for w, (c0, c1) in enumerate(((0, QR), (QR, QR + KVR))):
                    act.activation(square[:, 0:c1 - c0], lat3[:, t, c0:c1], ACT.Square,
                                   accum_out=sumsq[:, 2 * t + w:2 * t + w + 1]).then_inc(sumsq_ready, 1)
                    act.wait_ge(sumsq_ready, 2 * t + w + 1)
            act.wait_ge(key_rms_ready, 1)
            for o in range(1, 14, 2):
                filled(act, f"qkv{o}")
                qkv_copy(times, o)
            for step in range(H + 5):
                h = step
                if h < H and h % 2:
                    filled(act, f"headT{h}")
                    if h >= 3:
                        filled(act, f"score{h - 3}")
                    drain(copy(m_qk[h % 3][0:DQ, :], bk(f"headT{h}")[0:DQ, :]), f"headT{h}")
                h = step - 1
                if 0 <= h < H:
                    drained(act, f"score{h}")
                    s = m_s[h % 4]
                    for t, (c0, c1) in enumerate(TILE_COLS):
                        act.activation(s[:, c0:c1], s[:, c0:c1], ACT.Exp, bias=nm3[:, h, t:t + 1], scale=-1.0,
                                       accum_out=z3[:, h, t:t + 1]).then_inc(raw_prob, 1)
                h = step - 3
                if 0 <= h < H:
                    filled(act, f"probT{h}")
                    if h >= 4:
                        filled(act, f"mla_o{(h - 4) // 2}")
                    src = bk(f"probT{h}")
                    drain(copy(m_pt[h % 4], src[:, 0:3 * P]), f"probT{h}")
                if step >= 5 and step % 4 == 3:
                    i = (step - 5) // 2
                    filled(act, f"mla_o{i}")
                    drain(copy(oT[:, i, :], bk(f"mla_o{i}")[:, 0:S]), f"mla_o{i}")
            xT_copies("x1T")
            router_copy(0)
            experts(0)
            rest_of_tokens(0)

            xT_copies("x2T")
            for q in (1, 3):
                filled(act, f"nq{q}")
                drain(times(nqT[:, 2 * q:2 * q + 2, :], bk(f"nq{q}")[:, :].rearrange("p (i s) -> p i s", i=2), NSA_SCALE), f"nq{q}")
            filled(act, "vc")
            shifted_streams(times, "vc", 1)
            for t in range(NT):
                filled(act, f"vwg{t}")
                copy(vsw[:, 1, t, :], bk(f"vwg{t}")[:, 0:KVC])
                drain(act.activation(n_gate[:, t * NGATE:(t + 1) * NGATE], bk(f"vwg{t}")[:, KVC:KVC + NGATE], ACT.Exp, scale=-1.0),
                      f"vwg{t}")
            filled(act, "ks")
            act.wait_ge(nsa_zeroed, 3)
            padded_keys(times, "ks", 0)
            act.wait_ge(cmp_in, 1)
            act.activation(sc_f, sc_f, ACT.Exp).then_inc(cmp_exp, 1)
            for step in range(H + 6):
                h = step
                if h < H:
                    s = n_s[h % 4]
                    for t in range(NT):
                        drained(act, (f"near{h}", f"far{h}")[t])
                        for b in range(2):
                            c0 = b * P if t == 0 else 2 * P + b * S
                            c1 = c0 + (t + 1) * P
                            act.activation(s[:, c0:c1], s[:, c0:c1], ACT.Exp, bias=v4d["nm"][:, h, t, b:b + 1], scale=-1.0,
                                           accum_out=v4d["z"][:, h, t, b:b + 1]).then_inc(nraw_prob, 1)
                h = step - 3
                if 0 <= h < H:
                    if h >= 4:
                        filled(act, f"nsa_o{(h - 4) // 2}")
                    filled(act, f"nprobT_a{h}")
                    drain(copy(n_pt[h % 4][:, 0:2 * S], bk(f"nprobT_a{h}")[:, :]), f"nprobT_a{h}")
                    filled(act, f"nprobT_b{h}")
                    drain(copy(n_pt[h % 4][:, 2 * S:3 * S], bk(f"nprobT_b{h}")[:, 0:S]), f"nprobT_b{h}")
            xT_copies("x3T")
            router_copy(1)
            experts(1)
            rest_of_tokens(1)

        @block.vector
        def _(dve):
            st = Steps(dve, dve_step)
            copy = dve.tensor_copy

            def bc(ap, shape):
                return ap.to_broadcast(shape)

            def times(out, in_, factor):
                return dve.tensor_scalar(out, in_, factor, None, ALU.mult)

            def xT_copies(name):
                t, kh = divmod(2, 2)
                filled(dve, f"{name}2")
                drain(copy(xT[:, 4 * kh:4 * kh + 4, t * P:(t + 1) * P],
                           bk(f"{name}2")[:, :].rearrange("p (k s) -> p k s", k=4)), f"{name}2")

            def layer_norm(k, t, banks=None):
                halves = [slice(c * NB, (c + 1) * NB) for c in range(2)]
                src = [bk(nm)[:, :] for nm in banks] if banks else [x_tok[:, t, cols] for cols in halves]
                for c in range(2):
                    st(dve.bn_stats(bn[:, t, c, :], src[c]))
                st.wait()
                st(dve.bn_aggr(mv[:, t, :], bn[:, t, :, :].rearrange("p c s -> p (c s)")))
                st.wait()
                dve.tensor_scalar(var_eps[:, t:t + 1], mv[:, t, 1:2], LN_EPS, None, ALU.add).then_inc(var_ready, 1)
                if t == 0:
                    dve.wait_ge(ln_loaded, 32 * (k + 1))
                for c in range(2):
                    ins = dve.scalar_tensor_tensor(out=x_tok[:, t, halves[c]], in0=src[c], scalar=mv[:, t, 0:1], in1=gain[:, halves[c]],
                                                   op0=ALU.subtract, op1=ALU.mult)
                    if banks:
                        drain(ins, banks[c])
                    else:
                        st(ins)
                dve.wait_ge(rstd_ready, 1 + NT * k + t + 1)
                if not banks:
                    st.wait()
                for c in range(2):
                    if banks:
                        drained(dve, banks[c])
                    dve.scalar_tensor_tensor(out=x_tok[:, t, halves[c]], in0=x_tok[:, t, halves[c]], scalar=rstd[:, t:t + 1],
                                             in1=shift[:, halves[c]], op0=ALU.mult, op1=ALU.add).then_inc(x_ready, 1)

            def residual_norm(name, k):
                for t in range(NT):
                    for half in range(2):
                        nm = f"{name}{2 * t + half}"
                        filled(dve, nm)
                        cols = slice(half * NB, (half + 1) * NB)
                        drain(dve.scalar_tensor_tensor(out=x_tok[:, t, cols], in0=x_tok[:, t, cols], scalar=ALPHA,
                                                       in1=bk(nm)[:, :], op0=ALU.mult, op1=ALU.add), nm)
                    for half in range(2):
                        drained(dve, f"{name}{2 * t + half}")
                    layer_norm(k, t)

            def reduce(out, in_, op):
                st(dve.tensor_reduce(out, in_, AX, op))
                st.wait()

            def tt(out, a_, b_, op):
                st(dve.tensor_tensor(out, a_, b_, op))
                st.wait()

            W4 = [P, NT, EPG]
            W16 = [P, NT, NG, EPG]

            def first_of_largest(out, vals, top):
                reduce(top[:, :, 0], vals, ALU.max)
                tt(k4, vals, bc(top, W4), ALU.is_equal)
                tt(k4, k4, bc(desc.unsqueeze(1), W4), ALU.mult)
                reduce(r1[:, :, 0], k4, ALU.max)
                tt(out, k4, bc(r1, W4), ALU.is_equal)

            def grouped(x):
                return x.rearrange("p t (g e) -> p t g e", g=NG)

            def route(l):
                dve.wait_ge(router_loaded, 32 * (l + 1))
                filled(dve, f"logits{l}")
                drain(dve.tensor_tensor(lg, bk(f"logits{l}")[:, 0:NT * NRP].rearrange("p (t c) -> p t c", t=NT)[:, :, 0:NR],
                                        bc(router_b.unsqueeze(1), [P, NT, NR]), ALU.add), f"logits{l}")
                drained(dve, f"logits{l}")
                first_of_largest(group1h, lg[:, :, 0:NG], gmax)
                tt(grouped(prod16), grouped(lg[:, :, NG:]), bc(group1h.unsqueeze(3), W16), ALU.mult)
                reduce(le4, prod16.rearrange("p t (g e) -> p t e g", g=NG), ALU.add)
                first_of_largest(first1h, le4, v1)
                st(dve.scalar_tensor_tensor(out=m4, in0=first1h, scalar=NEG, in1=le4, op0=ALU.mult, op1=ALU.add))
                st.wait()
                first_of_largest(second1h, m4, v2)
                tt(both, first1h, second1h, ALU.add)
                dve.tensor_tensor(grouped(member), bc(group1h.unsqueeze(3), W16), bc(both.unsqueeze(2), W16),
                                  ALU.mult).then_inc(member_ready, 1)
                dve.tensor_tensor(e4, lg[:, :, 0:NG], bc(gmax, W4), ALU.subtract)
                dve.tensor_tensor(p4, le4, bc(v1, W4), ALU.subtract).then_inc(logit_exp_in, 1)
                dve.wait_ge(member_ready, l + 1)
                filled(dve, f"position{l}")
                drain(dve.scalar_tensor_tensor(out=posm, in0=bk(f"position{l}")[:, 0:NT * NE].rearrange("p (t c) -> p t c", t=NT),
                                               scalar=1.0, in1=member, op0=ALU.add, op1=ALU.mult), f"position{l}")
                drained(dve, f"position{l}")
                st(dve.tensor_scalar(posm, posm, -1.0, None, ALU.add))
                st.wait()

            def router_gates(l):
                dve.tensor_scalar(over, posm, float(CAP), None, ALU.is_ge).then_inc(over_ready, 1)
                dve.wait_ge(logit_exp_out, 2 * l + 2)
                st(dve.tensor_reduce(r1[:, :, 0], e4, AX, ALU.add))
                st(dve.tensor_reduce(v1[:, :, 0], p4, AX, ALU.add))
                st.wait()
                st(dve.reciprocal(r2, r1))
                st(dve.reciprocal(v2, v1))
                st.wait()
                tt(p4, p4, bc(v2, W4), ALU.mult)
                tt(m4, p4, both, ALU.mult)
                reduce(v1[:, :, 0], m4, ALU.add)
                st(dve.reciprocal(v2, v1))
                st.wait()
                tt(m4, m4, bc(v2, W4), ALU.mult)
                tt(gate4, m4, bc(r2, W4), ALU.mult)
                tt(grouped(gates), bc(group1h.unsqueeze(3), W16), bc(gate4.unsqueeze(2), W16), ALU.mult)
                dve.wait_ge(over_ready, l + 1)
                st(dve.tensor_tensor(rest_gates, gates, over, ALU.mult))

            def picks(l, e0):
                for t in range(NT):
                    for x in range(2):
                        ins = dve.tensor_scalar(pick[:, t, CAP * x:CAP * (x + 1)], iota, posm[:, t, bass.ds(e0 + x, 1)], None,
                                                ALU.is_equal)
                ins.then_inc(pick_ready, 1)

            def scatters(l, e0):
                for t in range(NT):
                    for x in range(2):
                        ins = dve.tensor_scalar(scat[:, t, CAP * x:CAP * (x + 1)], iota, posm[:, t, bass.ds(e0 + x, 1)],
                                                gates[:, t, bass.ds(e0 + x, 1)], ALU.is_equal, ALU.mult)
                ins.then_inc(scat_ready, 1)

            def experts(l):
                picks(l, 0)
                router_gates(l)
                filled(dve, f"gather_b{l}")
                drain(copy(xe[:, 4:8, :], bk(f"gather_b{l}")[:, :].rearrange("p (k s) -> p k s", k=4)), f"gather_b{l}")
                filled(dve, f"overflow{l}")
                drain(dve.tensor_reduce(k4[:, 0, 0:1], bk(f"overflow{l}")[:, 0:NT * NE], AX, ALU.add), f"overflow{l}")
                drained(dve, f"overflow{l}")
                dve.tensor_copy(counts[:, l:l + 1], k4[:, 0, 0:1]).then_inc(count_ready, 1)

                def pair(i, tag, e0, nth):
                    last = tag == "last"
                    h1, h3, hT, sT, y0, y1 = [f"{k}.{l}{tag}" for k in ("h1", "h3", "hidT", "scatT", "w2_0", "w2_1")]
                    b, k = number(sT, i)
                    dve.wait_ge(bank_drained[b], k - 2)
                    scatters(l, e0)
                    if not last:
                        filled(dve, h1, i)
                        picks(l, e0 + 2)
                    drained(dve, h1, i)
                    filled(dve, h3, i)
                    drain(dve.tensor_tensor(hid, silu, bk(h3)[:, :], ALU.mult), h3)
                    filled(dve, hT, i)
                    drain(copy(hidT_f, bk(hT)[:, :]), hT)
                    if not last:
                        filled(dve, f"next_b.{l}{tag}", i)
                        drain(copy(xe[:, 4:8, :], bk(f"next_b.{l}{tag}")[:, :].rearrange("p (k s) -> p k s", k=4)), f"next_b.{l}{tag}")
                    filled(dve, y1, i)
                    dve.wait_ge(scattered, nth)
                    drain(copy(ye[:, NB:2 * NB], bk(y1)[:, :]), y1)

                pair(None, "first", 0, l * PAIRS + 1)
                with dve.Fori(0, PAIRS - 2) as i:
                    pair(i, "", i * 2 + 2, i + (l * PAIRS + 2))
                pair(None, "last", 2 * (PAIRS - 1), (l + 1) * PAIRS)
                for q in range(4):
                    filled(dve, f"moe_y{l}{q}")

            def rest_of_tokens(l):
                r = rest[l]
                dve.wait_ge(count_ready, l + 1)
                total = dve.value_load(counts[0:1, l:l + 1], min_val=0, max_val=S * 2)
                with dve.If(total > 0):
                    dve.memset(k4[:, 0, 0:1], 0.0).then_inc(r["rounds"], 1)
                    with dve.Fori(0, NE) as i:
                        for t in range(NT):
                            u = i * NT + t
                            dve.wait_ge(r["silu"], u + 1)
                            dve.scalar_tensor_tensor(out=hid, in0=bank[1][:, :], scalar=rest_gates[:, t, bass.ds(i, 1)],
                                                     in1=silu, op0=ALU.mult, op1=ALU.mult).then_inc(r["hid"], 1)
                            dve.wait_ge(r["hidT"], u + 1)
                            dve.wait_ge(r["rounds"], u + 1)
                            dve.tensor_copy(hidT_f, bank[2][:, :]).then_inc(r["hidT_copied"], 1)
                    dve.wait_ge(r["rounds"], NE * NT + 1)
                dve.nop()

            for q in (0, 1):
                c0, c1 = (0, NB) if q == 0 else (NB, LAT)
                filled(dve, f"lat{q}")
                drain(copy(lat3[:, 0, c0:c1], bk(f"lat{q}")[:, 0:c1 - c0]), f"lat{q}")
            for q in range(4):
                drained(dve, f"lat{q}")
            dve.wait_ge(const_loaded, 16)
            half = ROPE // 2

            def rotate(out1, out2, a1, a2, shape, heads):
                tmp = [r_[:, 0:NT * heads * half].rearrange("p (t h f) -> p t h f", t=NT, h=heads) for r_ in rt]
                cs, sn = bc(cos.unsqueeze(2), shape), bc(sin.unsqueeze(2), shape)
                for buf, (x, y) in zip(tmp, ((a1, cs), (a2, sn), (a1, sn), (a2, cs))):
                    st(dve.tensor_tensor(buf, x, y, ALU.mult))
                st.wait()
                dve.tensor_tensor(out1, tmp[0], tmp[1], ALU.subtract)
                return dve.tensor_tensor(out2, tmp[2], tmp[3], ALU.add)

            dve.wait_ge(rms_loaded, 16)
            for c in range(CQ + CKV):
                nm = f"latT{c // 2}"
                if c % 2 == 0:
                    filled(dve, nm)
                ins = dve.tensor_scalar(latT3[:, c, :], bk(nm)[:, (c % 2) * S:(c % 2 + 1) * S], rms_gain[:, c:c + 1], None, ALU.mult)
                if c % 2 or c == CQ + CKV - 1:
                    drain(ins, nm)
            dve.wait_ge(sumsq_ready, 2 * NT)
            for t in range(NT):
                for w, c in enumerate((QR, KVR)):
                    ins = dve.tensor_scalar(sumsq[:, 2 * t + w:2 * t + w + 1], sumsq[:, 2 * t + w:2 * t + w + 1], 1.0 / c, RMS_EPS,
                                            ALU.mult, ALU.add)
            ins.then_inc(var_ready, 1)
            dve.wait_ge(rstd_ready, 1)
            times(key_rms, rms[:, 1::2], -MLA_SCALE).then_inc(key_rms_ready, 1)
            kr = lat3[:, :, QR + KVR:LAT].unsqueeze(2)

            def rope_of_keys():
                st(rotate(kr[:, :, :, 0:half], kr[:, :, :, half:], kr[:, :, :, 0:half], kr[:, :, :, half:], [P, NT, 1, half], 1))
                st.wait()
                for t in range(NT):
                    ins = times(k4d[:, t, :, NOPE:], bc(kr[:, t, :, :], [P, H, ROPE]), -MLA_SCALE)
                ins.then_inc(rope_ready, 1)

            dve.wait_ge(key_rms_ready, 1)
            for o in range(0, 14, 2):
                filled(dve, f"qkv{o}")
                qkv_copy(times, o)
                if o == 0:
                    rope_of_keys()
                if o == 6:
                    for u in range(6):
                        drained(dve, f"qkv{u}")
                    q1, q2 = q4[:, :, :, NOPE:NOPE + half], q4[:, :, :, NOPE + half:]
                    rotate(q1, q2, q1, q2, [P, NT, H, half], H).then_inc(rope_ready, 1)
            dve.wait_ge(rope_ready, 2)
            for step in range(H + 5):
                h = step
                if h < H and h % 2 == 0:
                    filled(dve, f"headT{h}")
                    if h >= 3:
                        filled(dve, f"score{h - 3}")
                    drain(copy(m_qk[h % 3][0:DQ, :], bk(f"headT{h}")[0:DQ, :]), f"headT{h}")
                h2 = step - 2
                if 0 <= h2 < H:
                    dve.wait_ge(raw_prob, NT * (h2 + 1))
                    st(dve.reciprocal(rz3[:, h2, :], z3[:, h2, :]))
                h = step - 1
                if 0 <= h < H:
                    filled(dve, f"score{h}")
                    if h >= 4:
                        filled(dve, f"probT{h - 4}")
                    for t, (c0, c1) in enumerate(TILE_COLS):
                        ins = dve.tensor_tensor_reduce(m_s[h % 4][:, c0:c1], bk(f"score{h}")[:, c0:c1], mask[:, c0:c1], 1.0, HUGE,
                                                       ALU.add, ALU.min, nm3[:, h, t:t + 1])
                    drain(ins, f"score{h}")
                if 0 <= h2 < H:
                    st.wait()
                    for t, (c0, c1) in enumerate(TILE_COLS):
                        ins = times(m_s[h2 % 4][:, c0:c1], m_s[h2 % 4][:, c0:c1], rz3[:, h2, t:t + 1])
                    ins.then_inc(prob_ready, 1)
                if step >= 5 and step % 4 == 1:
                    i = (step - 5) // 2
                    filled(dve, f"mla_o{i}")
                    drain(copy(oT[:, i, :], bk(f"mla_o{i}")[:, 0:S]), f"mla_o{i}")
            dve.wait_ge(x_loaded, 16)
            residual_norm("mla_y", 0)
            xT_copies("x1T")
            route(0)
            experts(0)
            rest_of_tokens(0)
            for t in range(NT):
                layer_norm(1, t, [f"moe_y0{2 * t + half}" for half in range(2)])

            xT_copies("x2T")
            for q in (0, 2):
                filled(dve, f"nq{q}")
                drain(times(nqT[:, 2 * q:2 * q + 2, :], bk(f"nq{q}")[:, :].rearrange("p (i s) -> p i s", i=2), NSA_SCALE), f"nq{q}")
            dve.wait_ge(nsa_loaded, 16)
            copy(streams_f.rearrange("p (w s) -> p w s", w=2 * G)[:, :, CMP_STRIDE * NCMP:],
                 bc(pos_t[:, :].unsqueeze(1), [P, 2 * G, CMP_STRIDE])).then_inc(pos_placed, 1)
            filled(dve, "kc")
            shifted_streams(times, "kc", 0)
            for t in range(NT):
                drained(dve, f"vwg{t}")
            st(dve.tensor_scalar(n_gate, n_gate, 1.0, None, ALU.add))
            st.wait()
            st(dve.reciprocal(n_gate, n_gate))
            filled(dve, "cmp")
            dve.wait_ge(nsa_zeroed, 3)
            drain(copy(cmp_f, bk("cmp")[:, 0:2 * G * CMP_PAD]), "cmp")
            drained(dve, "cmp")
            cmp4 = cmp_f.rearrange("p (g n) -> p g n", n=CMP_PAD)
            for x in range(2):
                dve.tensor_tensor(kbd[HD * x:HD * (x + 1), :, CMP_PAD * x:CMP_PAD * x + NCMP], cmp4[0:HD, 0:G, 0:NCMP],
                                  bc(cmp4[0:HD, 0:G, NCMP:], [HD, G, NCMP]), ALU.add)
            dve.tensor_tensor(vrep_f[HD:P, :].rearrange("p (g r n) -> p g r n", g=G, r=HPG)[:, :, :, 0:NCMP],
                                    bc(cmp4[HD:P, G:, 0:NCMP].unsqueeze(2), [HD, G, HPG, NCMP]),
                                    bc(cmp4[HD:P, G:, NCMP:].unsqueeze(2), [HD, G, HPG, NCMP]), ALU.add).then_inc(cmp_kv_ready, 1)
            filled(dve, "vrep")
            for u in range(2):
                heads = P // CMP_PAD
                ins = dve.tensor_tensor(vbd_f[:, u * heads * HD:(u + 1) * heads * HD].rearrange("p (h d) -> p h d", h=heads),
                                        bc(bk("vrep")[:, u * HD:(u + 1) * HD].unsqueeze(1), [P, heads, HD]),
                                        bc(own_block.unsqueeze(2), [P, heads, HD]), ALU.mult)
            drain(ins, "vrep")
            filled(dve, "cs")
            R = NT * H
            wide = [P, R, CMP_PAD]
            drain(dve.tensor_tensor(sc, bk("cs")[:, :].rearrange("p (r n) -> p r n", r=R),
                                    cmp_bias.rearrange("p t h n -> p (t h) n"), ALU.add), "cs")
            drained(dve, "cs")
            reduce(c_mx, sc, ALU.max)
            dve.tensor_tensor(sc, sc, bc(c_mx.unsqueeze(2), wide), ALU.subtract).then_inc(cmp_in, 1)
            dve.wait_ge(cmp_exp, 1)
            reduce(c_z, sc, ALU.add)
            st(dve.reciprocal(c_cf, c_z))
            st.wait()
            tt(c_cf.rearrange("p (t h) -> p t h", t=NT), c_cf.rearrange("p (t h) -> p t h", t=NT),
               bc(any_visible.unsqueeze(2), [P, NT, H]), ALU.mult)
            tt(c_cf, c_cf, gate3[:, :, 0], ALU.mult)
            dve.tensor_tensor(sc, sc, bc(c_cf.unsqueeze(2), wide), ALU.mult).then_inc(cmp_prob, 1)
            filled(dve, "kw")
            padded_keys(times, "kw", 1)
            for step in range(H + 5):
                h2 = step - 2
                if 0 <= h2 < H:
                    dve.wait_ge(nraw_prob, 4 * (h2 + 1))
                    st(dve.reciprocal(v4d["rz"][:, h2], v4d["z"][:, h2]))
                h = step
                if h < H:
                    if h >= 4:
                        filled(dve, f"nprobT_b{h - 4}")
                    dve.wait_ge(bias_ready, h + 1)
                    for t, nm in enumerate((f"near{h}", f"far{h}")):
                        filled(dve, nm)
                        w = (t + 1) * P
                        bias = n_bias[h % 2][:, t * P:t * P + w]
                        for b in range(2):
                            c0 = b * P if t == 0 else 2 * P + b * S
                            ins = dve.tensor_tensor_reduce(n_s[h % 4][:, c0:c0 + w], bk(nm)[:, b * w:(b + 1) * w], bias, 1.0, HUGE,
                                                           ALU.add, ALU.min, v4d["nm"][:, h, t, b:b + 1])
                        drain(ins, nm)
                if h == 1:
                    filled(dve, "vs")
                    drain(copy(vsw[:, 0, :, :], bk("vs")[:, :].rearrange("p (t c) -> p t c", t=NT)), "vs")
                    filled(dve, "pcT")
                    drain(copy(pct_f, bk("pcT")[:, :]), "pcT")
                if 0 <= h2 < H:
                    st.wait()
                    tt(v4d["cf"][:, h2], v4d["rz"][:, h2], gate4d[:, :, h2, 1:3], ALU.mult)
                    for t in range(NT):
                        for b in range(2):
                            c0 = b * P if t == 0 else 2 * P + b * S
                            cols = slice(c0, c0 + (t + 1) * P)
                            ins = times(n_s[h2 % 4][:, cols], n_s[h2 % 4][:, cols], v4d["cf"][:, h2, t, b:b + 1])
                    ins.then_inc(nprob_ready, 1)
                if step >= 5 and step % 2:
                    i = (step - 5) // 2
                    filled(dve, f"nsa_o{i}")
                    drain(copy(oT[:, i, :], bk(f"nsa_o{i}")[:, 0:S]), f"nsa_o{i}")
            residual_norm("nsa_y", 2)
            xT_copies("x3T")
            route(1)
            experts(1)
            rest_of_tokens(1)
            for t in range(NT):
                layer_norm(3, t, [f"moe_y1{2 * t + half}" for half in range(2)])


def kernel(**inputs):
    import concourse.bacc as bacc
    from concourse.bass_utils import run_bass_kernel_spmd

    f = {k: np.asarray(v) for k, v in inputs.items()}
    const, _ = shape_constants()
    lay = {
        "x": f["x"][0],
        "xT": f["x"][0].T.reshape(P, KD * S),
        "const": const,
        "rms_gain": np.concatenate([f["mla_q_norm"][0].reshape(P, CQ), f["mla_kv_norm"][0].reshape(P, CKV)], 1),
        "mla_w_in": f["mla_w_in"][0],
        "mla_w_qb": f["mla_w_qb"][0],
        "mla_w_kvb": f["mla_w_kvb"][0],
        "mla_w_o": f["mla_w_o"][0],
        "nsa_w_in": f["nsa_w_in"][0],
        "nsa_w_o": f["nsa_w_o"][0],
        "phi": np.stack([f[k][0].reshape(2, CMP_STRIDE, HD, HD) for k in ("nsa_w_phi_k", "nsa_w_phi_v")])
        .transpose(1, 3, 2, 0, 4).reshape(P, CMP_STRIDE * 2 * HD),
        "cmp_posT": f["nsa_cmp_pos"][0].reshape(2, CMP_STRIDE, HD).transpose(0, 2, 1).reshape(P, CMP_STRIDE),
        "ln": np.stack([f[k][l] for l in range(DEPTH) for k in ("ln1_g", "ln1_b", "ln2_g", "ln2_b")]),
        "router_w": np.stack([np.pad(np.concatenate([f["moe_wg"][l], f["moe_we"][l].transpose(1, 0, 2).reshape(D, NE)], 1),
                                     ((0, 0), (0, NRP - NR))).reshape(P, KD * NRP) for l in range(DEPTH)]),
        "router_b": np.concatenate([f["moe_bg"], f["moe_be"].reshape(DEPTH, NE)], 1),
        "moe_w1": f["moe_w1"].reshape(DEPTH * NE, D, FF),
        "moe_w3": f["moe_w3"].reshape(DEPTH * NE, D, FF),
        "moe_w2": f["moe_w2"].reshape(DEPTH * NE, FF, D),
    }
    nc = bacc.Bacc("TRN2", target_bir_lowering=False, num_devices=1)
    arrays, a = {}, {}
    for name, v in lay.items():
        arrays[f"in_{name}"] = np.ascontiguousarray(v)
        a[name] = nc.dram_tensor(f"in_{name}", v.shape, F32, kind="ExternalInput").ap()
    a["out"] = nc.dram_tensor("out_0", (S, D), F32, kind="ExternalOutput").ap()
    build(nc, a)
    r = run_bass_kernel_spmd(nc, [arrays], core_ids=[0])
    return r.results[0]["out_0"].reshape(1, S, D)
```

```python
from contextlib import ExitStack

import numpy as np

import concourse.bass as bass
from concourse import mybir

F32 = mybir.dt.float32
I32 = mybir.dt.int32
ALU = mybir.AluOpType
ACT = mybir.ActivationFunctionType
AX = mybir.AxisListType.X

P = 128
S = 256
NT = S // P
D = 1024
KD = D // P
DEPTH = 2
ALPHA = (2.0 * DEPTH) ** 0.25
LN_EPS = 1e-5
RMS_EPS = 1e-6
NEG = -1e30
HUGE = 3e38
H = 16
QR, KVR, NOPE, ROPE, VD = 384, 256, 64, 32, 64
CQ, CKV = QR // P, KVR // P
LAT = QR + KVR + ROPE
DQ = NOPE + ROPE
MLA_SCALE = DQ ** -0.5
HD = 64
G = 4
HPG = H // G
CMP_LEN, CMP_STRIDE = 32, 16
NCMP = (S - CMP_LEN) // CMP_STRIDE + 1
CMP_PAD = 16
NSA_SCALE = HD ** -0.5
NSA_COLS = 512
NGATE = 3 * H
KVC = G * HD
NE = 16
NG = 4
EPG = NE // NG
FF = 512
KF = FF // P
SCORE_BUFS = 5
PROB_BUFS = 4
CAP = 64
PAIRS = NE // 2
NR = NG + NE
NRP = 32
PIECES = ((0, 1), (1, 2), (2, 4), (4, 6), (6, 8))
EXTRA = 4
OWN = 6
SLOT = 4096
NB = 512

C_ID = 0
C_AID = C_ID + P
C_TRI = C_AID + P
C_MASK = C_TRI + P
C_IOTA = C_MASK + 3 * P
C_DESC = C_IOTA + CAP
C_COS = C_DESC + EPG
C_SIN = C_COS + NT * ROPE // 2
C_CB = C_SIN + NT * ROPE // 2
C_VIS = C_CB + NT * H * CMP_PAD
C_DIST = C_VIS + NT
C_BLK = C_DIST + 3 * P
C_STK = C_BLK + P // CMP_PAD
C_END = C_STK + NRP
FAR = 1e32


def shape_constants():
    c = np.zeros((P, C_END), np.float32)
    p = np.arange(P)
    c[:, C_ID:C_ID + P] = np.eye(P)
    c[:, C_AID:C_AID + P] = np.eye(P) * ALPHA
    c[:, C_TRI:C_TRI + P] = p[:, None] < p[None, :]
    hidden = np.where(p[None, :] <= p[:, None], 0.0, -NEG)
    c[:, C_MASK:C_MASK + P] = hidden
    c[:, C_MASK + 2 * P:C_MASK + 3 * P] = hidden
    c[:, C_IOTA:C_IOTA + CAP] = np.arange(1, CAP + 1)
    c[:, C_DESC:C_DESC + EPG] = EPG - np.arange(EPG)
    half = ROPE // 2
    freq = np.float32(10000.0) ** (-np.arange(half, dtype=np.float32) / half)
    tok = (np.arange(NT)[None, :] * P + p[:, None])
    ang = tok[:, :, None].astype(np.float32) * freq
    c[:, C_COS:C_SIN] = np.cos(ang).reshape(P, -1)
    c[:, C_SIN:C_CB] = np.sin(ang).reshape(P, -1)
    slopes = (2.0 ** (-8.0 * np.arange(1, H + 1) / H)).astype(np.float32)
    end = np.arange(NCMP) * CMP_STRIDE + CMP_LEN - 1
    dist = (tok[:, :, None] - end).astype(np.float32)
    cb = np.full((P, NT, H, CMP_PAD), NEG, np.float32)
    cb[..., 0:NCMP] = np.where(dist[:, :, None, :] >= 0, -slopes[:, None] * dist[:, :, None, :], NEG)
    c[:, C_CB:C_VIS] = cb.reshape(P, -1)
    c[:, C_VIS:C_DIST] = (dist >= 0).any(-1)
    d = np.concatenate([tok[:, t, None] - np.arange((t + 1) * P) for t in range(NT)], 1)
    c[:, C_DIST:C_BLK] = np.where(d >= 0, d, FAR)
    c[:, C_BLK:C_STK] = p[:, None] // CMP_PAD == np.arange(P // CMP_PAD)
    c[:, C_STK:C_END] = p[:, None] % NRP == np.arange(NRP)
    return c, slopes


class PsumPlan:

    def __init__(self):
        self.count = [0] * 8
        self.at = {}

    def add(self, name, bank):
        self.count[bank] += 1
        self.at[name] = (bank, self.count[bank], 0)

    def add_loop(self, names_banks, iterations):
        per = [sum(1 for _, b in names_banks if b == k) for k in range(8)]
        seen = [0] * 8
        for name, bank in names_banks:
            seen[bank] += 1
            self.at[name] = (bank, self.count[bank] + seen[bank], per[bank])
        for k in range(8):
            self.count[k] += per[k] * iterations


def psum_plan():
    plan = PsumPlan()

    def transposed(name):
        for s in range(4):
            plan.add(f"{name}{s}", s)

    def experts(l):
        plan.add(f"logitsT{l}", 0)
        plan.add(f"logits{l}", 1)
        plan.add(f"position{l}", 0)
        plan.add(f"gather_a{l}", 2)
        plan.add(f"gather_b{l}", 3)
        plan.add(f"overflow{l}", 1)
        names = [("h1", 0), ("h3", 1), ("next_a", 2), ("next_b", 3), ("hidT", 0), ("scatT", 1), ("w2_0", 2), ("w2_1", 3)]
        plan.add_loop([(f"{n}.{l}", b) for n, b in names], PAIRS - 1)
        for n, b in names:
            if not n.startswith("next"):
                plan.add(f"{n}.{l}last", b)
        for q in range(4):
            plan.add(f"moe_y{l}{q}", 4 + q)

    for q in range(4):
        plan.add(f"lat{q}", q)
    for q in range(3):
        plan.add(f"latT{q}", 4 + q)
    for o in range(14):
        plan.add(f"qkv{o}", (o + 7) % 8)
    for h in range(H):
        plan.add(f"headT{h}", h % 2)
        plan.add(f"score{h}", 2 + h % 2)
        plan.add(f"probT{h}", 4 + h % 2)
    for i in range(H // 2):
        plan.add(f"mla_o{i}", 6 + i % 2)
    for q in range(4):
        plan.add(f"mla_y{q}", q)
    transposed("x1T")
    experts(0)
    transposed("x2T")
    for q in range(4):
        plan.add(f"nq{q}", 4 + q)
    for n, b in (("kc", 0), ("vc", 1), ("vwg0", 2), ("vwg1", 3), ("cmp", 4), ("ks", 5), ("vrep", 6), ("cs", 7),
                 ("kw", 4), ("vs", 6), ("pcT", 7)):
        plan.add(n, b)
    for h in range(H):
        plan.add(f"near{h}", h % 2)
        plan.add(f"far{h}", 2 + h % 2)
        plan.add(f"nprobT_a{h}", 4)
        plan.add(f"nprobT_b{h}", 5)
    for i in range(H // 2):
        plan.add(f"nsa_o{i}", 6 + i % 2)
    for q in range(4):
        plan.add(f"nsa_y{q}", q)
    transposed("x3T")
    experts(1)
    return plan


MLA_SLOTS = {"w_in": (0, "lat3"), "w_qb2": (1, "qkv5"), "w_qb": (2, "qkv5"), "w_kvb": (3, "qkv13"),
             "w_o0": (4, "mla_y3"), "w_o1": (5, "mla_y3")}
NSA_SLOTS = {"q0": (0, "nq1"), "q1": (1, "nq3"), "c": (2, "vc"), "phi_kw": (3, "kw"), "vwg": (4, "vwg1"), "s": (5, "vs"),
             "w_o0": (0, "nsa_y3"), "w_o1": (1, "nsa_y3")}
W13_SLOTS = [((0, 1, 2, 9), (6, 4, 5, 3)), ((2, 3, 4, 9), (6, 0, 1, 5))]
W2_SLOTS = (7, 8)
LOAD_ORDER = [("w1", "w3", "w2")] * 2 + [("w1", "w2", "w3")] * 2 + [("w2", "w1", "w3")] * 2 + [("w2",)]
DONE_W13 = ("h1", "h1", "h3", "h3")


class SlotPlan:

    def __init__(self):
        self.count = [0] * (OWN + EXTRA)
        self.at, self.freed_by, last = {}, {}, {}

        def straight(prefix, slots):
            for name, (s, done) in slots.items():
                self.count[s] += 1
                self.at[prefix + name] = (s, self.count[s])
                self.freed_by[prefix + name] = last.get(s)
                last[s] = done

        def mixture(l):
            for odd in range(2):
                for x, s in enumerate(W13_SLOTS[l][odd]):
                    self.at[f"w13.{l}{odd}{x}"] = (s, self.count[s] + 1)
                    self.freed_by[f"w13.{l}{odd}{x}"] = last.get(s) if s < OWN else None
                    self.count[s] += PAIRS // 2
                    last[s] = f"{DONE_W13[x]}.{l}last" if odd else (f"{DONE_W13[x]}.{l}", PAIRS - 2)
            for x, s in enumerate(W2_SLOTS):
                self.at[f"w2.{l}{x}"] = (s, self.count[s] + 1)
                self.count[s] += PAIRS

        straight("mla_", MLA_SLOTS)
        mixture(0)
        straight("nsa_", NSA_SLOTS)
        mixture(1)


def build(nc, a):
    plan = psum_plan()
    slots = SlotPlan()
    slopes = shape_constants()[1]
    with ExitStack() as ctx:
        def sb(name, cols, dt=F32):
            return ctx.enter_context(nc.sbuf_tensor(name, [P, cols], dt))

        def sem(name):
            return ctx.enter_context(nc.semaphore(name))

        own_slots = sb("weight_slots", OWN * SLOT)
        const = sb("const", C_END)
        x_t = sb("x_tok", NT * D)
        xT_t = sb("xT", KD * S)
        small = sb("small", 760)
        counts = sb("counts", 4, I32)
        WORK = 21060
        work = sb("work", WORK)
        bank = [ctx.enter_context(nc.psum_tensor(f"bank{b}", [P, NB], F32)) for b in range(8)]

        class Region:
            def __init__(self, base, at=0):
                self.base, self.at = base, at

            def take(self, cols):
                self.at += cols
                assert self.at <= self.base.shape[1], (self.at, self.base.shape)
                return self.base[:, self.at - cols:self.at]

        ident = const[:, C_ID:C_ID + P]
        alpha_ident = const[:, C_AID:C_AID + P]
        tri = const[:, C_TRI:C_TRI + P]
        mask = const[:, C_MASK:C_MASK + 3 * P]
        iota = const[:, C_IOTA:C_IOTA + CAP]
        desc = const[:, C_DESC:C_DESC + EPG]
        cos = const[:, C_COS:C_SIN].rearrange("p (t f) -> p t f", t=NT)
        sin = const[:, C_SIN:C_CB].rearrange("p (t f) -> p t f", t=NT)
        cmp_bias = const[:, C_CB:C_VIS].rearrange("p (t h n) -> p t h n", t=NT, h=H)
        any_visible = const[:, C_VIS:C_DIST]
        dist = const[:, C_DIST:C_BLK]
        own_block = const[:, C_BLK:C_STK]
        stacked_ident = const[:, C_STK:C_END]
        x_tok = x_t[:, :].rearrange("p (t d) -> p t d", t=NT)
        xT = xT_t[:, :].rearrange("p (k s) -> p k s", k=KD)
        gain, shift = work[:, 0:D], work[:, D:2 * D]

        sm = Region(small)
        bn = sm.take(NT * 2 * 6).rearrange("p (t c s) -> p t c s", t=NT, c=2)
        mv = sm.take(NT * 2).rearrange("p (t s) -> p t s", t=NT)
        var_eps = sm.take(4)
        neg_half = sm.take(4)
        rstd = sm.take(4)
        sumsq = sm.take(4)
        rms = sm.take(4)
        key_rms = sm.take(NT)
        rms_gain = sm.take(CQ + CKV)
        router_b = sm.take(NR)
        ones = sb("ones", P)
        lg = sm.take(NT * NR).rearrange("p (t c) -> p t c", t=NT)

        def per_token(cols):
            return sm.take(NT * cols).rearrange("p (t c) -> p t c", t=NT)
        r1, r2, gmax = per_token(1), per_token(1), per_token(1)
        e4, p4, k4, group1h = per_token(4), per_token(4), per_token(4), per_token(4)
        gate4 = per_token(4)
        emax, r4 = per_token(4), per_token(4)
        k16, first16, rest16, both16 = per_token(NE), per_token(NE), per_token(NE), per_token(NE)
        v1, v2 = per_token(1), per_token(1)
        m4, le4, both = per_token(4), per_token(4), per_token(4)
        prod16 = per_token(NE)
        member = per_token(NE)
        gates = per_token(NE)
        posm = per_token(NE)
        over = per_token(NE)
        rest_gates = per_token(NE)
        router_w = sb("router_w", KD * NRP)
        rw = router_w[:, :].rearrange("p (k c) -> p k c", k=KD)

        OT_AT = 2 * D
        assert OT_AT + KD * S == SLOT
        oT_f = work[:, OT_AT:SLOT]
        EXPERTS_AT = SLOT
        EXTRA_AT = [WORK - (EXTRA - 1 - x) * SLOT for x in range(EXTRA - 1)] + [0]

        m = Region(work, SLOT)
        q_tok = m.take(NT * H * DQ)
        k_tok = m.take(NT * H * DQ)
        v_tok = m.take(NT * H * VD)
        lat = m.take(NT * LAT)
        latT = m.take((CQ + CKV) * S)
        m_spt = m.take((SCORE_BUFS + PROB_BUFS) * 3 * P)
        m_s = [m_spt[:, i * 3 * P:(i + 1) * 3 * P] for i in range(SCORE_BUFS)]
        m_pt = [m_spt[:, (SCORE_BUFS + i) * 3 * P:(SCORE_BUFS + 1 + i) * 3 * P] for i in range(PROB_BUFS)]
        RT = NT * H * ROPE // 2
        rt = [m_spt[:, i * RT:(i + 1) * RT] for i in range(4)]
        square = m_spt[:, 0:QR]
        m_qk = [m.take(2 * S) for _ in range(3)]
        m_z = m.take(NT * H)
        m_rz = m.take(NT * H)
        m_nm = m.take(H * NT)
        q4 = q_tok.rearrange("p (t h d) -> p t h d", t=NT, h=H)
        k4d = k_tok.rearrange("p (t h d) -> p t h d", t=NT, h=H)
        v4 = v_tok.rearrange("p (t h d) -> p t h d", t=NT, h=H)
        lat3 = lat.rearrange("p (t c) -> p t c", t=NT)
        latT3 = latT.rearrange("p (j s) -> p j s", j=CQ + CKV)
        z3 = m_z.rearrange("p (h t) -> p h t", h=H)
        rz3 = m_rz.rearrange("p (h t) -> p h t", h=H)
        nm3 = m_nm.rearrange("p (h t) -> p h t", h=H)
        oT = oT_f.rearrange("p (i s) -> p i s", i=KD)

        n = Region(work, SLOT)
        nqT_f = oT_f
        kz_f = n.take(2 * G * 2 * S)
        kbd_f = n.take(G * 2 * CMP_PAD)
        vsw_f = n.take(2 * NT * KVC)
        vrep_f = n.take(G * HPG * CMP_PAD)
        vbd_f = n.take(H // 2 * P)
        pct_f = n.take(2 * S)
        n_s = [n.take(6 * P) for _ in range(SCORE_BUFS)]
        sc_f = n_s[3][:, 0:NT * H * CMP_PAD]
        n_pt_all = n.take(PROB_BUFS * 6 * P)
        n_pt = [n_pt_all[:, i * 6 * P:(i + 1) * 6 * P] for i in range(PROB_BUFS)]
        streams_f = n_pt_all[:, 0:2 * G * S]
        n_bias = [n.take(3 * P) for _ in range(2)]
        cmp_f = n.take(2 * G * CMP_PAD)
        nqT = nqT_f.rearrange("p (i s) -> p i s", i=H // 2)
        kz = kz_f.rearrange("p (x g b s) -> p x g b s", x=2, g=G, b=2)
        kbd = kbd_f.rearrange("p (g n) -> p g n", g=G)
        vsw = vsw_f.rearrange("p (b t c) -> p b t c", b=2, t=NT)
        streams = streams_f.rearrange("p (w g s) -> p w g s", w=2, g=G)
        vbd = vbd_f.rearrange("p (i c) -> p i c", i=H // 2)
        sc = sc_f.rearrange("p (r c) -> p r c", c=CMP_PAD)
        pct = pct_f.rearrange("p (u s) -> p u s", u=2)
        nsm = sb("nsa_small", NT * NGATE + 4 * H * 4 + 3 * NT * H)
        ns = Region(nsm)
        n_gate = ns.take(NT * NGATE)
        n_nm = ns.take(H * NT * 2)
        n_z = ns.take(H * NT * 2)
        n_rz = ns.take(H * NT * 2)
        n_cf = ns.take(H * NT * 2)
        c_mx = ns.take(NT * H)
        c_z = ns.take(NT * H)
        c_cf = ns.take(NT * H)
        pos_t = sb("cmp_posT", CMP_STRIDE)
        gate3 = n_gate.rearrange("p (r b) -> p r b", b=3)
        gate4d = n_gate.rearrange("p (t h b) -> p t h b", t=NT, b=3)
        v4d = {k: v.rearrange("p (h t b) -> p h t b", h=H, t=NT) for k, v in dict(nm=n_nm, z=n_z, rz=n_rz, cf=n_cf).items()}

        e = Region(work, EXPERTS_AT)
        xe_f = e.take(KD * 2 * CAP)
        xe = xe_f.rearrange("p (k c) -> p k c", k=KD)
        pick_f = e.take(NT * 2 * CAP)
        pick = pick_f.rearrange("p (t c) -> p t c", t=NT)
        scat_f = e.take(NT * 2 * CAP)
        scat = scat_f.rearrange("p (t c) -> p t c", t=NT)
        scatT_f = e.take(NT * P)
        silu = e.take(FF)
        lgT = silu[:, 0:S]
        hid = e.take(FF)
        hidT_f = e.take(KF * P)
        hidT = hidT_f.rearrange("p (c s) -> p c s", c=KF)
        ye = e.take(D)
        assert e.at <= EXTRA_AT[0]

        bank_filled = [sem(f"bank{b}_filled") for b in range(8)]
        bank_drained = [sem(f"bank{b}_drained") for b in range(8)]
        slot_loaded = [sem(f"slot{s}_loaded") for s in range(OWN + EXTRA)]
        x_loaded, const_loaded = sem("x_loaded"), sem("const_loaded")
        xT_loaded = [sem(f"xT{i}_loaded") for i in range(len(PIECES))]
        w_in_loaded = [sem(f"w_in{i}_loaded") for i in range(len(PIECES) - 1)]
        phi_loaded = sem("phi_loaded")
        first_w1_half_used = sem("first_w1_half_used")
        half_loaded = {w: [sem(f"{w}_half{x}_loaded") for x in range(2)] for w in ("w1", "w3", "w2")}
        rms_loaded, router_loaded = sem("rms_loaded"), sem("router_loaded")
        ln_loaded = [sem("first_norm_loaded"), sem("second_norm_loaded")]
        nsa_loaded = sem("nsa_tables_loaded")
        consts_set = sem("consts_set")
        dve_step = sem("dve_step")
        var_ready, rstd_ready = sem("variance_ready"), sem("rstd_ready")
        x_ready = sem("x_ready")
        sumsq_ready = sem("sumsq_ready")
        key_rms_ready, rope_ready = sem("key_rms_ready"), sem("rope_ready")
        raw_prob, prob_ready = sem("raw_probs_ready"), sem("probs_ready")
        logit_exp_in, logit_exp_out = sem("router_exp_in"), sem("router_exp_out")
        member_ready, over_ready, count_ready = sem("member_ready"), sem("over_ready"), sem("count_ready")
        pick_ready, scat_ready, scattered = sem("pick_ready"), sem("scat_ready"), sem("scattered")
        pos_placed, cmp_kv_ready = sem("cmp_pos_placed"), sem("cmp_keys_values_ready")
        cmp_in, cmp_exp, cmp_prob = sem("cmp_scores_ready"), sem("cmp_exp_ready"), sem("cmp_probs_ready")
        nsa_zeroed, bias_ready = sem("nsa_memory_zeroed"), sem("alibi_bias_ready")
        nraw_prob, nprob_ready = sem("nsa_raw_probs_ready"), sem("nsa_probs_ready")
        rest = [{k: sem(f"rest{l}_{k}") for k in ("loaded", "h", "silu", "hid", "hidT", "hidT_copied", "rounds")}
                for l in range(DEPTH)]
        out_written = sem("out_written")

        def number(name, i):
            b, first, per = plan.at[name]
            return b, first if i is None or not per else first + per * i

        def filled(eng, name, i=None):
            b, k = number(name, i)
            eng.wait_ge(bank_filled[b], k)

        def drained(eng, name, i=None):
            b, k = number(name, i)
            eng.wait_ge(bank_drained[b], k)

        def may_fill(eng, name, i=None):
            b, k = number(name, i)
            if not (isinstance(k, int) and k == 1):
                eng.wait_ge(bank_drained[b], k - 1)

        def normed(eng, k, t):
            eng.wait_ge(x_ready, 2 * (NT * k + t + 1))

        def fill(ins, name):
            ins.then_inc(bank_filled[plan.at[name][0]], 1)

        def drain(ins, name):
            ins.then_inc(bank_drained[plan.at[name][0]], 1)

        def bk(name):
            return bank[plan.at[name][0]]

        class Steps:

            def __init__(self, eng, sem_):
                self.eng, self.sem, self.n = eng, sem_, 0

            def __call__(self, ins):
                ins.then_inc(self.sem, 1)
                self.n += 1

            def wait(self):
                self.eng.wait_ge(self.sem, self.n)

        def loaded(eng, name, later=0):
            s, k = slots.at[name]
            eng.wait_ge(slot_loaded[s], later * 16 + 16 * k)

        block = ctx.enter_context(nc.Block())
        w_in = a["mla_w_in"].rearrange("(p k) n -> p k n", k=KD)
        w_qb = a["mla_w_qb"].rearrange("(p c) n -> p c n", c=CQ)
        w_kvb = a["mla_w_kvb"].rearrange("(p c) n -> p (c n)", c=CKV)
        w_o = [a[k].rearrange("(k p) n -> p k n", k=KD) for k in ("mla_w_o", "nsa_w_o")]
        n_in = a["nsa_w_in"].rearrange("(p k) n -> p k n", k=KD)
        w1 = a["moe_w1"].rearrange("e (p k) n -> e p (k n)", k=KD)
        w3 = a["moe_w3"].rearrange("e (p k) n -> e p (k n)", k=KD)
        w2 = a["moe_w2"].rearrange("e (p c) n -> e p (c n)", c=KF)
        def slot_view(s, cols=SLOT, chunks=1, off=0):
            base, at = (own_slots, s * SLOT) if s < OWN else (work, EXTRA_AT[s - OWN])
            return base[:, at + off:at + off + cols * chunks].rearrange("p (k n) -> p k n", k=chunks)

        def view(name, cols, chunks, off=0):
            return slot_view(slots.at[name][0], cols, chunks, off)

        def at_expert(w, idx):
            return w[bass.ds(idx, 1), :, :].rearrange("o p n -> p o n")

        def gained_latents(scaled, q):
            for c in range(2 * q, min(2 * q + 2, CQ + CKV)):
                ins = scaled(latT3[:, c, :], bk(f"latT{q}")[:, (c % 2) * S:(c % 2 + 1) * S], rms_gain[:, c:c + 1])
            drain(ins, f"latT{q}")

        def qkv_copy(scaled, o):
            nm = f"qkv{o}"
            b = bk(nm)
            if o < 6:
                t, nn = divmod(o, 3)
                drain(scaled(q_tok[:, (t * 3 + nn) * NB:(t * 3 + nn + 1) * NB], b[:, :], rms[:, 2 * t:2 * t + 1]), nm)
            else:
                t, nn = divmod(o - 6, 4)
                src = b[:, :].rearrange("p (h d) -> p h d", h=4)
                scaled(k4d[:, t, 4 * nn:4 * nn + 4, 0:NOPE], src[:, :, 0:NOPE], key_rms[:, t:t + 1])
                drain(scaled(v4[:, t, 4 * nn:4 * nn + 4, :], src[:, :, NOPE:], rms[:, 2 * t + 1:2 * t + 2]), nm)

        def shifted_streams(times, nm, w):
            psum = bk(nm)[:, :].rearrange("p (q s) -> p q s", q=2)
            for x in range(2):
                for y in range(2):
                    src = psum[64 * x:64 * x + 64, :, CMP_STRIDE * y:CMP_STRIDE * (y + NCMP)]
                    ins = times(streams[64 * y:64 * y + 64, w, x::2, 0:CMP_STRIDE * NCMP], src, 1.0)
            drain(ins, nm)

        def padded_keys(times, nm, b):
            src = bk(nm)[:, :].rearrange("p (q s) -> p q s", q=2)
            for gx in range(2):
                for x in range(2):
                    ins = times(kz[64 * x:64 * x + 64, x, gx::2, b, :], src[64 * gx:64 * gx + 64, :, :], -1.0)
            drain(ins, nm)

        TILE_COLS = ((0, P), (P, 3 * P))

        def load_ln(eng, k):
            eng.dma_start(gain, a["ln"][2 * k:2 * k + 1, :].to_broadcast([P, D])).then_inc(ln_loaded[k % 2], 16)
            eng.dma_start(shift, a["ln"][2 * k + 1:2 * k + 2, :].to_broadcast([P, D])).then_inc(ln_loaded[k % 2], 16)

        @block.sync
        def _(sp):
            def free(name):
                before = slots.freed_by.get(name)
                if before:
                    filled(sp, *(before if isinstance(before, tuple) else (before,)))

            def load(name, out, in_):
                free(name)
                sp.dma_start(out, in_).then_inc(slot_loaded[slots.at[name][0]], 16)

            for i, (k0, k1) in enumerate(PIECES):
                sp.dma_start(xT[:, k0:k1, :], a["xT"][:, k0 * S:k1 * S].rearrange("p (k s) -> p k s", k=k1 - k0)).then_inc(
                    xT_loaded[i], 16)
                sp.dma_start(view("mla_w_in", LAT, KD)[:, k0:k1, :], w_in[:, k0:k1, :]).then_inc(
                    w_in_loaded[i] if i < len(PIECES) - 1 else slot_loaded[0], 16)
            load("mla_w_qb2", view("mla_w_in", H * DQ, 1, off=KD * LAT), w_qb[:, 2:3, :])
            load("mla_w_qb", view("mla_w_qb", H * DQ, 2), w_qb[:, 0:2, :])
            load("mla_w_kvb", view("mla_w_kvb", SLOT, 1), w_kvb.unsqueeze(1))
            for x in range(2):
                load(f"mla_w_o{x}", view(f"mla_w_o{x}", D, 4), w_o[0][:, 4 * x:4 * x + 4, :])

            def experts(l):
                e0 = l * NE
                w13 = ((w1, 0), (w1, 1), (w3, 0), (w3, 1))

                def load_w13(odd, x, expert):
                    w, y = w13[x]
                    s = W13_SLOTS[l][odd][x]
                    sp.dma_start(slot_view(s), at_expert(w, expert + y)).then_inc(slot_loaded[s], 16)

                def load_halves(w, what, slot_ids, expert):
                    for c in range(2):
                        cols = slice(c * SLOT // 2, (c + 1) * SLOT // 2)
                        for x, s in enumerate(slot_ids):
                            sp.dma_start(slot_view(s)[:, :, cols], at_expert(w, expert + x)[:, :, cols]).then_inc(
                                slot_loaded[s] if c else half_loaded[what][x], 16)

                def load_w2(expert):
                    for x, s in enumerate(W2_SLOTS):
                        sp.dma_start(slot_view(s), at_expert(w2, expert + x)).then_inc(slot_loaded[s], 16)

                def first_w13(odd, x):
                    free(f"w13.{l}{odd}{x}")
                    load_w13(odd, x, e0 + 2 * odd)

                for x in range(3):
                    first_w13(0, x)
                first_w13(1, 3)
                for i in (H // 2 - 2, H // 2 - 1):
                    drained(sp, f"{('mla', 'nsa')[l]}_o{i}")
                load_w2(e0)
                for x in range(3):
                    first_w13(1, x)
                normed(sp, 2 * l, NT - 1)
                first_w13(0, 3)
                for p, order in enumerate(LOAD_ORDER):
                    for what in order:
                        if p == 0 and what == "w1":
                            for c in range(2):
                                if c == 0:
                                    sp.wait_ge(first_w1_half_used, l + 1)
                                else:
                                    filled(sp, f"h1.{l}", 0)
                                cols = slice(c * SLOT // 2, (c + 1) * SLOT // 2)
                                for x in range(2):
                                    s = W13_SLOTS[l][0][x]
                                    sp.dma_start(slot_view(s)[:, :, cols], at_expert(w1, e0 + 4 + x)[:, :, cols]).then_inc(
                                        slot_loaded[s] if c else half_loaded["w1"][x], 16)
                            continue
                        if what == "w2":
                            filled(sp, f"w2_1.{l}", p)
                            if p + 1 == PAIRS - 1:
                                load_halves(w2, "w2", W2_SLOTS, e0 + NE - 2)
                            else:
                                load_w2(e0 + 2 * (p + 1))
                            continue
                        for x in ((0, 1) if what == "w1" else (2, 3)):
                            filled(sp, f"{DONE_W13[x]}.{l}", p)
                            if what == "w1" or p + 2 < PAIRS - 1:
                                load_w13(p % 2, x, e0 + 2 * (p + 2))
                        if what == "w3" and p + 2 == PAIRS - 1:
                            load_halves(w3, "w3", W13_SLOTS[l][1][2:], e0 + NE - 2)
                filled(sp, f"h3.{l}", PAIRS - 2)
                load_ln(sp, 2 * l + 1)

            def rest_of_tokens(l):
                r = rest[l]
                sp.wait_ge(count_ready, l + 1)
                total = sp.value_load(counts[0:1, l:l + 1], min_val=0, max_val=S * 2)
                with sp.If(total > 0):
                    filled(sp, f"w2_1.{l}last")
                    with sp.Fori(0, NE) as i:
                        sp.wait_ge(r["rounds"], i * NT + 1)
                        for s, w in enumerate((w1, w3, w2)):
                            sp.dma_start(slot_view(s), at_expert(w, i + l * NE)).then_inc(r["loaded"], 16)
                    sp.wait_ge(r["rounds"], NE * NT + 1)
                sp.nop()

            experts(0)
            rest_of_tokens(0)
            for c, name in enumerate(("nsa_q0", "nsa_q1", "nsa_c")):
                load(name, view(name, NSA_COLS, KD), n_in[:, :, c * NSA_COLS:(c + 1) * NSA_COLS])
            free("nsa_phi_kw")
            sp.dma_start(view("nsa_phi_kw", SLOT // 2, 1), a["phi"].unsqueeze(1)).then_inc(phi_loaded, 16)
            sp.dma_start(view("nsa_phi_kw", KVC, KD, off=SLOT // 2), n_in[:, :, H * HD + 4 * KVC:H * HD + 5 * KVC]).then_inc(
                slot_loaded[slots.at["nsa_phi_kw"][0]], 16)
            load("nsa_vwg", view("nsa_vwg", KVC + NGATE, KD), n_in[:, :, H * HD + 5 * KVC:])
            load("nsa_s", view("nsa_s", NSA_COLS, KD), n_in[:, :, 3 * NSA_COLS:4 * NSA_COLS])
            for x in range(2):
                load(f"nsa_w_o{x}", view(f"nsa_w_o{x}", D, 4), w_o[1][:, 4 * x:4 * x + 4, :])
            experts(1)
            rest_of_tokens(1)
            for t in range(NT):
                for half in range(2):
                    sp.wait_ge(x_ready, 2 * (3 * NT + t) + half + 1)
                    cols = slice(half * NB, (half + 1) * NB)
                    sp.dma_start(a["out"][t * P:(t + 1) * P, cols], x_tok[:, t, cols]).then_inc(out_written, 16)
            sp.wait_ge(out_written, 16 * 2 * NT)

        @block.gpsimd
        def _(pool):
            pool.dma_start(rms_gain, a["rms_gain"]).then_inc(rms_loaded, 16)
            pool.memset(neg_half, -0.5).then_inc(consts_set, 1)
            pool.memset(ones[:, :], 1.0).then_inc(consts_set, 1)
            pool.wait_ge(w_in_loaded[0], 16)
            pool.dma_start(const[:, :], a["const"]).then_inc(const_loaded, 16)

            def load_router(l):
                pool.dma_start(router_w[:, :], a["router_w"][l]).then_inc(router_loaded, 16)
                pool.dma_start(router_b, a["router_b"][l:l + 1, :].to_broadcast([P, NR])).then_inc(router_loaded, 16)

            pool.wait_ge(consts_set, 2)

            def inverse_root(k, out, in_):
                pool.wait_ge(var_ready, k + 1)
                pool.tensor_tensor(out, in_, neg_half[:, 0:out.shape[1]], ALU.pow).then_inc(rstd_ready, 1)

            def norm_roots(k):
                for t in range(NT):
                    inverse_root(1 + NT * k + t, rstd[:, t:t + 1], var_eps[:, t:t + 1])

            filled(pool, "lat1")
            pool.dma_start(x_tok, a["x"].rearrange("(t p) d -> p t d", t=NT)).then_inc(x_loaded, 16)
            load_ln(pool, 0)
            load_router(0)
            inverse_root(0, rms, sumsq)
            norm_roots(0)
            norm_roots(1)
            normed(pool, 1, NT - 1)
            load_ln(pool, 2)
            load_router(1)
            pool.dma_start(pos_t[:, :], a["cmp_posT"]).then_inc(nsa_loaded, 16)
            pool.memset(kbd_f, 0.0).then_inc(nsa_zeroed, 1)
            pool.memset(vrep_f, 0.0).then_inc(nsa_zeroed, 1)
            pool.memset(kz_f, 0.0).then_inc(nsa_zeroed, 1)
            pool.wait_ge(const_loaded, 16)
            for h in range(H):
                if h >= 2:
                    drained(pool, f"far{h - 2}")
                pool.tensor_scalar(n_bias[h % 2], dist, float(slopes[h]), None, ALU.mult).then_inc(bias_ready, 1)
            norm_roots(2)
            norm_roots(3)

        @block.tensor
        def _(pe):
            def tile_transposes(name, k, t):
                normed(pe, k, t)
                for kh in range(2):
                    s = 2 * t + kh
                    may_fill(pe, f"{name}{s}")
                    for c in range(4):
                        ins = pe.transpose(bk(f"{name}{s}")[:, c * P:(c + 1) * P], x_tok[:, t, 4 * kh + c::KD], ident)
                    fill(ins, f"{name}{s}")

            def alpha_x(l, t, halves=(0, 1)):
                for half in halves:
                    nm = f"moe_y{l}{2 * t + half}"
                    may_fill(pe, nm)
                    ins = pe.matmul(bk(nm)[:, :], alpha_ident, x_tok[:, t, half * NB:(half + 1) * NB],
                                    start=True, stop=False, skip_group_check=True)
                if t == NT - 1 and half == 1:
                    ins.then_inc(scattered, 1)

            def project(kind, t, half, ks):
                nm = f"{kind}_y{2 * t + half}"
                for k in ks:
                    if k == 0:
                        may_fill(pe, nm)
                    if t == 0 and half == 0:
                        drained(pe, f"{kind}_o{k}")
                        if k % 4 == 0:
                            loaded(pe, f"{kind}_w_o{k // 4}")
                    w = view(f"{kind}_w_o{k // 4}", D, 4)
                    ins = pe.matmul(bk(nm)[:, :], oT[:, k, t * P:(t + 1) * P], w[:, k % 4, half * NB:(half + 1) * NB],
                                    start=(k == 0), stop=(k == KD - 1))
                    if k == KD - 1:
                        fill(ins, nm)

            EARLY = {H: (0, 1), H + 1: (2, 3), H + 2: (4,), H + 3: (5,)}

            def rest_of_projection(kind):
                project(kind, 0, 0, (6, 7))
                for t, half in ((0, 1), (1, 0), (1, 1)):
                    project(kind, t, half, range(KD))

            def experts(l, xname):
                pe.wait_ge(router_loaded, 32 * (l + 1))
                nm = f"logitsT{l}"
                may_fill(pe, nm)
                tiles = P // NRP
                for k in range(KD):
                    c = k % tiles
                    if c == 0:
                        for t in range(NT):
                            drained(pe, f"{xname}{2 * t + k // tiles}")
                    ins = pe.matmul(bk(nm)[c * NRP:(c + 1) * NRP, 0:S], rw[:, k, :], xT[:, k, :],
                                    start=(k < tiles), stop=(k >= KD - tiles))
                fill(ins, nm)
                drained(pe, nm)
                may_fill(pe, f"logits{l}")
                for u in range(NT):
                    ins = pe.matmul(bk(f"logits{l}")[:, u * NRP:(u + 1) * NRP], lgT[:, u * P:(u + 1) * P], stacked_ident,
                                    start=True, stop=True)
                fill(ins, f"logits{l}")
                alpha_x(l, 1, (0,))
                pe.wait_ge(consts_set, 2)
                pe.wait_ge(member_ready, l + 1)
                may_fill(pe, f"position{l}")
                pos = bk(f"position{l}")
                pe.matmul(pos[:, 0:NE], tri, member[:, 0, :], start=True, stop=True)
                pe.matmul(pos[:, NE:2 * NE], ones[:, :], member[:, 0, :], start=True, stop=False)
                fill(pe.matmul(pos[:, NE:2 * NE], tri, member[:, 1, :], start=False, stop=True), f"position{l}")

                def gather(nm, half, i):
                    may_fill(pe, nm, i)
                    for c in range(4):
                        for t in range(NT):
                            ins = pe.matmul(bk(nm)[:, c * P:(c + 1) * P], x_tok[:, t, 4 * half + c::KD], pick[:, t, :],
                                            start=(t == 0), stop=(t == NT - 1))
                    fill(ins, nm)

                alpha_x(l, 1, (1,))
                pe.wait_ge(pick_ready, l * PAIRS + 1)
                gather(f"gather_a{l}", 0, None)
                gather(f"gather_b{l}", 1, None)
                pe.wait_ge(over_ready, l + 1)
                may_fill(pe, f"overflow{l}")
                fill(pe.matmul(bk(f"overflow{l}")[:, 0:NT * NE], ones[:, :], over.rearrange("p t c -> p (t c)"),
                               start=True, stop=True), f"overflow{l}")

                def two_experts(out, src, ws, chunks, cols, ks=None):
                    for k in ks or range(chunks):
                        for x in range(2):
                            ins = pe.matmul(out[CAP * x:CAP * (x + 1), :], src[:, k, CAP * x:CAP * (x + 1)],
                                            ws[x][:, k, cols], start=(k == 0), stop=(k == chunks - 1))
                    return ins

                def pair(p, odd, half):
                    last = isinstance(p, int) and p == PAIRS - 1
                    i, tag = (None, "last") if last else (p, "")
                    nth = p + (l * PAIRS + 1)
                    h1, h3, hT, sT, y0, y1 = [f"{k}.{l}{tag}" for k in ("h1", "h3", "hidT", "scatT", "w2_0", "w2_1")]

                    def weights(names, later, cols, chunks):
                        for name in names:
                            loaded(pe, name, later)
                        return [view(name, cols, chunks) for name in names]

                    def first_halves(what):
                        for x in range(2):
                            pe.wait_ge(half_loaded[what][x], 16 * (l + 1))

                    may_fill(pe, h1, i)
                    ws = weights([f"w13.{l}{odd}{x}" for x in (0, 1)], half, FF, KD)
                    if isinstance(p, int) and p == 0:
                        drained(pe, f"gather_a{l}")
                        two_experts(bk(h1), xe, ws, KD, slice(0, FF), range(KD // 2)).then_inc(first_w1_half_used, 1)
                        drained(pe, f"gather_b{l}")
                        fill(two_experts(bk(h1), xe, ws, KD, slice(0, FF), range(KD // 2, KD)), h1)
                    else:
                        if not odd:
                            first_halves("w1")
                        fill(two_experts(bk(h1), xe, ws, KD, slice(0, FF)), h1)
                    may_fill(pe, h3, i)
                    if last:
                        first_halves("w3")
                        two_experts(bk(h3), xe, [view(f"w13.{l}{odd}{x}", FF, KD) for x in (2, 3)], KD, slice(0, FF), range(KD // 2))
                    ws = weights([f"w13.{l}{odd}{x}" for x in (2, 3)], half, FF, KD)
                    fill(two_experts(bk(h3), xe, ws, KD, slice(0, FF), range(KD // 2, KD) if last else None), h3)
                    if not last:
                        pe.wait_ge(pick_ready, nth + 1)
                        gather(f"next_a.{l}", 0, i)
                    drained(pe, h3, i)
                    may_fill(pe, hT, i)
                    for c in range(KF):
                        ins = pe.transpose(bk(hT)[:, c * P:(c + 1) * P], hid[:, c::KF], ident)
                    fill(ins, hT)
                    if not last:
                        gather(f"next_b.{l}", 1, i)
                    pe.wait_ge(scat_ready, nth)
                    may_fill(pe, sT, i)
                    for t in range(NT):
                        ins = pe.transpose(bk(sT)[:, t * P:(t + 1) * P], scat[:, t, :], ident)
                    fill(ins, sT)
                    drained(pe, hT, i)
                    if last:
                        first_halves("w2")
                        for c, nm in enumerate((y0, y1)):
                            may_fill(pe, nm, i)
                            two_experts(bk(nm), hidT, [view(f"w2.{l}{x}", D, KF) for x in (0, 1)], KF,
                                        slice(c * NB, (c + 1) * NB), range(KF // 2))
                    ws = weights([f"w2.{l}{x}" for x in (0, 1)], p, D, KF)
                    for c, nm in enumerate((y0, y1)):
                        if not last:
                            may_fill(pe, nm, i)
                        fill(two_experts(bk(nm), hidT, ws, KF, slice(c * NB, (c + 1) * NB),
                                         range(KF // 2, KF) if last else None), nm)
                    drained(pe, sT, i)
                    for c, nm in enumerate((y0, y1)):
                        drained(pe, nm, i)
                        for t in range(NT):
                            q = 2 * t + c
                            ins = pe.matmul(bk(f"moe_y{l}{q}")[:, :], scatT_f[:, t * P:(t + 1) * P],
                                            ye[:, c * NB:(c + 1) * NB], start=False, stop=last, skip_group_check=True)
                            if last:
                                fill(ins, f"moe_y{l}{q}")
                    if not last:
                        ins.then_inc(scattered, 1)
                        for nm in (f"next_a.{l}", f"next_b.{l}"):
                            drained(pe, nm, i)

                pair(0, 0, 0)
                with pe.Fori(0, PAIRS // 2 - 1) as i:
                    pair(i * 2 + 1, 1, i)
                    pair(i * 2 + 2, 0, i + 1)
                pair(PAIRS - 1, 1, PAIRS // 2 - 1)

            def rest_of_tokens(l):
                r = rest[l]
                pe.wait_ge(count_ready, l + 1)
                total = pe.value_load(counts[0:1, l:l + 1], min_val=0, max_val=S * 2)
                with pe.If(total > 0):
                    pe.wait_ge(r["rounds"], 1)
                    with pe.Fori(0, NE) as i:
                        pe.wait_ge(r["loaded"], i * 48 + 48)
                        for t in range(NT):
                            u = i * NT + t
                            for b, s in ((0, 0), (1, 1)):
                                for k in range(KD):
                                    ins = pe.matmul(bank[b][:, :], xT[:, k, t * P:(t + 1) * P], slot_view(s, FF, KD)[:, k, :],
                                                    start=(k == 0), stop=(k == KD - 1))
                            ins.then_inc(r["h"], 1)
                            pe.wait_ge(r["hid"], u + 1)
                            for c in range(KF):
                                ins = pe.transpose(bank[2][:, c * P:(c + 1) * P], hid[:, c::KF], ident)
                            ins.then_inc(r["hidT"], 1)
                            pe.wait_ge(r["hidT_copied"], u + 1)
                            for half in range(2):
                                for c in range(KF):
                                    ins = pe.matmul(bank[4 + 2 * t + half][:, :], hidT[:, c, :],
                                                    slot_view(2, D, KF)[:, c, half * NB:(half + 1) * NB],
                                                    start=False, stop=True, skip_group_check=True)
                            ins.then_inc(r["rounds"], 1)
                pe.nop()

            for k in range(KD):
                for i, (k0, _) in enumerate(PIECES):
                    if k == k0:
                        pe.wait_ge(xT_loaded[i], 16)
                        if i < len(PIECES) - 1:
                            pe.wait_ge(w_in_loaded[i], 16)
                        else:
                            loaded(pe, "mla_w_in")
                w = view("mla_w_in", LAT, KD)[:, k, :]
                for q in range(4):
                    t, part = divmod(q, 2)
                    c0, c1 = (0, NB) if part == 0 else (NB, LAT)
                    ins = pe.matmul(bk(f"lat{q}")[:, 0:c1 - c0], xT[:, k, t * P:(t + 1) * P], w[:, c0:c1],
                                    start=(k == 0), stop=(k == KD - 1))
                    if k == KD - 1:
                        fill(ins, f"lat{q}")
            pe.wait_ge(const_loaded, 16)
            for q in range(4):
                drained(pe, f"lat{q}")
            for c in range(CQ + CKV):
                nm = f"latT{c // 2}"
                for t in range(NT):
                    src = lat3[:, t, c:QR:CQ] if c < CQ else lat3[:, t, QR + c - CQ:QR + KVR:CKV]
                    ins = pe.transpose(bk(nm)[:, (c % 2) * S + t * P:(c % 2) * S + (t + 1) * P], src, ident)
                if c % 2 or c == CQ + CKV - 1:
                    fill(ins, nm)
            wq = [view("mla_w_qb", H * DQ, 2)[:, 0, :], view("mla_w_qb", H * DQ, 2)[:, 1, :],
                  view("mla_w_in", H * DQ, 1, off=KD * LAT)[:, 0, :]]
            wkv = view("mla_w_kvb", H * (NOPE + VD), CKV)
            loaded(pe, "mla_w_qb")
            loaded(pe, "mla_w_qb2")
            for o in range(14):
                may_fill(pe, f"qkv{o}")
                if o == 0:
                    for q in range(2):
                        drained(pe, f"latT{q}")
                if o == 6:
                    loaded(pe, "mla_w_kvb")
                    drained(pe, "latT2")
                t, nn = divmod(o, 3) if o < 6 else divmod(o - 6, 4)
                chunks = CQ if o < 6 else CKV
                for c in range(chunks):
                    w = wq[c] if o < 6 else wkv[:, c, :]
                    j = c if o < 6 else CQ + c
                    ins = pe.matmul(bk(f"qkv{o}")[:, :], latT3[:, j, t * P:(t + 1) * P], w[:, nn * NB:(nn + 1) * NB],
                                    start=(c == 0), stop=(c == chunks - 1))
                fill(ins, f"qkv{o}")
            for o in range(12):
                drained(pe, f"qkv{o}")
            pe.wait_ge(rope_ready, 2)
            for step in range(H + 5):
                h = step
                if h < H:
                    if h == H // 2:
                        for o in (12, 13):
                            drained(pe, f"qkv{o}")
                    may_fill(pe, f"headT{h}")
                    b = bk(f"headT{h}")
                    for w in range(2):
                        for t in range(NT):
                            src = (q4, k4d)[w][:, t, h, :]
                            ins = pe.transpose(b[0:DQ, w * S + t * P:w * S + (t + 1) * P], src, ident)
                    fill(ins, f"headT{h}")
                h = step - 1
                if 0 <= h < H:
                    drained(pe, f"headT{h}")
                    may_fill(pe, f"score{h}")
                    qk, b = m_qk[h % 3], bk(f"score{h}")
                    pe.matmul(b[:, 0:P], qk[0:DQ, 0:P], qk[0:DQ, S:S + P], start=True, stop=True)
                    fill(pe.matmul(b[:, P:3 * P], qk[0:DQ, P:S], qk[0:DQ, S:2 * S], start=True, stop=True), f"score{h}")
                h = step - 4
                if 0 <= h < H:
                    pe.wait_ge(prob_ready, h + 1)
                    may_fill(pe, f"probT{h}")
                    for c in range(3):
                        ins = pe.transpose(bk(f"probT{h}")[:, c * P:(c + 1) * P], m_s[h % SCORE_BUFS][:, c * P:(c + 1) * P], ident)
                    fill(ins, f"probT{h}")
                if step >= 6 and step % 2 == 0:
                    i = (step - 6) // 2
                    nm = f"mla_o{i}"
                    may_fill(pe, nm)
                    for x in range(2):
                        drained(pe, f"probT{2 * i + x}")
                    for c0, c1, kt in ((0, S, 0), (P, S, 1)):
                        for x in range(2):
                            h = 2 * i + x
                            src = m_pt[h % PROB_BUFS][:, 0:S] if kt == 0 else m_pt[h % PROB_BUFS][:, S:S + P]
                            ins = pe.matmul(bk(nm)[VD * x:VD * (x + 1), c0:c1], v4[:, kt, h, :], src,
                                            start=(kt == 0), stop=(kt == 1), skip_group_check=True)
                    fill(ins, nm)
                project("mla", 0, 0, EARLY.get(step, ()))
            rest_of_projection("mla")
            tile_transposes("x1T", 0, 0)
            alpha_x(0, 0)
            tile_transposes("x1T", 0, 1)
            experts(0, "x1T")
            rest_of_tokens(0)

            tile_transposes("x2T", 1, 0)

            def columns_T(out, w, c0):
                for k in range(KD):
                    ins = pe.matmul(out, w[:, k, c0:c0 + P], xT[:, k, :], start=(k == 0), stop=(k == KD - 1))
                return ins

            def bank_of_columns(nm, w, c0):
                may_fill(pe, nm)
                for x in range(2):
                    ins = columns_T(bk(nm)[:, x * S:(x + 1) * S], w, c0 + x * P)
                fill(ins, nm)

            loaded(pe, "nsa_q0")
            w = view("nsa_q0", NSA_COLS, KD)
            for t in range(NT):
                for s in (2 * t, 2 * t + 1):
                    drained(pe, f"x2T{s}")
                for q in range(2):
                    if t == 0:
                        may_fill(pe, f"nq{q}")
                    for x in range(2):
                        for k in range(KD):
                            ins = pe.matmul(bk(f"nq{q}")[:, x * S + t * P:x * S + (t + 1) * P], w[:, k, (2 * q + x) * P:(2 * q + x + 1) * P],
                                            xT[:, k, t * P:(t + 1) * P], start=(k == 0), stop=(k == KD - 1))
                    if t == 1:
                        fill(ins, f"nq{q}")
                if t == 0:
                    tile_transposes("x2T", 1, 1)
            for c in range(1, 3):
                name = ("nsa_q0", "nsa_q1", "nsa_c")[c]
                loaded(pe, name)
                w = view(name, NSA_COLS, KD)
                for half in range(2):
                    bank_of_columns(f"nq{2 * c + half}" if c < 2 else ("kc", "vc")[half], w, 2 * half * P)
            loaded(pe, "nsa_vwg")
            w = view("nsa_vwg", KVC + NGATE, KD)
            for t in range(NT):
                nm = f"vwg{t}"
                may_fill(pe, nm)
                for k in range(KD):
                    ins = pe.matmul(bk(nm)[:, 0:KVC + NGATE], xT[:, k, t * P:(t + 1) * P], w[:, k, :],
                                    start=(k == 0), stop=(k == KD - 1))
                fill(ins, nm)
            pe.wait_ge(phi_loaded, 16)
            phi = view("nsa_phi_kw", P, CMP_STRIDE)
            drained(pe, "kc")
            drained(pe, "vc")
            pe.wait_ge(pos_placed, 1)
            may_fill(pe, "cmp")
            for r in range(CMP_STRIDE):
                ins = pe.matmul(bk("cmp")[:, 0:2 * G * CMP_PAD], phi[:, r, :], streams_f[:, r::CMP_STRIDE],
                                start=(r == 0), stop=(r == CMP_STRIDE - 1))
            fill(ins, "cmp")
            loaded(pe, "nsa_s")
            w_s = view("nsa_s", NSA_COLS, KD)
            bank_of_columns("ks", w_s, 0)
            pe.wait_ge(cmp_kv_ready, 1)
            may_fill(pe, "vrep")
            for u in range(2):
                ins = pe.matmul(bk("vrep")[:, u * HD:(u + 1) * HD], vrep_f[:, u * P:(u + 1) * P], ident[:, HD:2 * HD],
                                start=True, stop=True)
            fill(ins, "vrep")
            for q in range(4):
                drained(pe, f"nq{q}")
            may_fill(pe, "cs")
            for t in range(NT):
                for i in range(H // 2):
                    c0 = (t * (H // 2) + i) * 2 * CMP_PAD
                    ins = pe.matmul(bk("cs")[:, c0:c0 + 2 * CMP_PAD], nqT[:, i, t * P:(t + 1) * P], kbd[:, i // 2, :],
                                    start=True, stop=True)
            fill(ins, "cs")
            loaded(pe, "nsa_phi_kw")
            bank_of_columns("kw", view("nsa_phi_kw", KVC, KD, off=SLOT // 2), 0)
            def nsa_scores(h):
                i, x = divmod(h, 2)
                for t, nm in enumerate((f"near{h}", f"far{h}")):
                    may_fill(pe, nm)
                    w = (t + 1) * P
                    out = bk(nm)[:, 0:2 * w].rearrange("p (b s) -> p b s", b=2)
                    fill(pe.matmul(out, nqT[:, i, t * P:(t + 1) * P], kz[:, x, h // HPG, :, 0:w], start=True, stop=True), nm)

            def selected_values(t):
                for k in range(KD):
                    ins = pe.matmul(bk("vs")[:, t * S:(t + 1) * S], xT[:, k, t * P:(t + 1) * P], w_s[:, k, KVC:2 * KVC],
                                    start=(k == 0), stop=(k == KD - 1))
                return ins

            may_fill(pe, "vs")
            selected_values(0)
            drained(pe, "ks")
            drained(pe, "kw")
            nsa_scores(0)
            nsa_scores(1)
            fill(selected_values(1), "vs")
            pe.wait_ge(cmp_prob, 1)
            may_fill(pe, "pcT")
            for u in range(2):
                for t in range(NT):
                    ins = pe.transpose(bk("pcT")[:, u * S + t * P:u * S + (t + 1) * P],
                                       sc_f[:, t * S + u * P:t * S + (u + 1) * P], ident)
            fill(ins, "pcT")
            for step in range(H + 5):
                h = step
                if 2 <= h < H:
                    nsa_scores(h)
                h = step - 4
                if 0 <= h < H:
                    pe.wait_ge(nprob_ready, h + 1)
                    s = n_s[h % SCORE_BUFS]
                    may_fill(pe, f"nprobT_a{h}")
                    for b in range(2):
                        for t in range(NT):
                            c0 = b * P if t == 0 else 2 * P + b * S
                            ins = pe.transpose(bk(f"nprobT_a{h}")[:, b * S + t * P:b * S + (t + 1) * P], s[:, c0:c0 + P], ident)
                    fill(ins, f"nprobT_a{h}")
                    may_fill(pe, f"nprobT_b{h}")
                    for b in range(2):
                        c0 = 2 * P + b * S + P
                        ins = pe.transpose(bk(f"nprobT_b{h}")[:, b * P:(b + 1) * P], s[:, c0:c0 + P], ident)
                    fill(ins, f"nprobT_b{h}")
                if step >= 6 and step % 2 == 0:
                    i = (step - 6) // 2
                    nm = f"nsa_o{i}"
                    if i == 0:
                        for src in ("pcT", "vrep", "vs", "vwg0", "vwg1"):
                            drained(pe, src)
                    may_fill(pe, nm)
                    pe.matmul(bk(nm)[:, 0:S], vbd[:, i, :], pct[:, i // 4, :], start=True, stop=False, skip_group_check=True)
                    for part in "ab":
                        for x in range(2):
                            drained(pe, f"nprobT_{part}{2 * i + x}")
                        for b in range(2):
                            for x in range(2):
                                h = 2 * i + x
                                g, kt = h // HPG, "ab".index(part)
                                src = n_pt[h % PROB_BUFS][:, b * S:(b + 1) * S] if kt == 0 else \
                                    n_pt[h % PROB_BUFS][:, 2 * S + b * P:2 * S + (b + 1) * P]
                                ins = pe.matmul(bk(nm)[HD * x:HD * (x + 1), kt * P:S], vsw[:, b, kt, g * HD:(g + 1) * HD], src,
                                                start=False, stop=(kt == 1 and b == 1), skip_group_check=True)
                    fill(ins, nm)
                project("nsa", 0, 0, EARLY.get(step, ()))
            rest_of_projection("nsa")
            tile_transposes("x3T", 2, 0)
            alpha_x(1, 0)
            tile_transposes("x3T", 2, 1)
            experts(1, "x3T")
            rest_of_tokens(1)

        @block.scalar
        def _(act):
            def copy(out, in_):
                return act.activation(out, in_, ACT.Copy)

            def times(out, in_, factor):
                return act.activation(out, in_, ACT.Copy, scale=factor)

            def xT_copies(name):
                for s in (0, 1, 3):
                    t, kh = divmod(s, 2)
                    filled(act, f"{name}{s}")
                    drain(copy(xT[:, 4 * kh:4 * kh + 4, t * P:(t + 1) * P],
                               bk(f"{name}{s}")[:, :].rearrange("p (k s) -> p k s", k=4)), f"{name}{s}")

            def router_copy(l):
                filled(act, f"logitsT{l}")
                drain(copy(lgT, bk(f"logitsT{l}")[:, 0:S]), f"logitsT{l}")

            def experts(l):
                act.wait_ge(logit_exp_in, l + 1)
                for e_ in (e4, p4):
                    act.activation(e_, e_, ACT.Exp).then_inc(logit_exp_out, 1)
                filled(act, f"gather_a{l}")
                drain(copy(xe[:, 0:4, :], bk(f"gather_a{l}")[:, :].rearrange("p (k s) -> p k s", k=4)), f"gather_a{l}")

                def pair(i, tag, nth):
                    last = tag == "last"
                    h1, h3, hT, sT, y0, y1 = [f"{k}.{l}{tag}" for k in ("h1", "h3", "hidT", "scatT", "w2_0", "w2_1")]
                    filled(act, h1, i)
                    b, k = number(h3, i)
                    act.wait_ge(bank_drained[b], k - 2)
                    drain(act.activation(silu, bk(h1)[:, :], ACT.Silu), h1)
                    if not last:
                        filled(act, f"next_a.{l}", i)
                        drain(copy(xe[:, 0:4, :], bk(f"next_a.{l}")[:, :].rearrange("p (k s) -> p k s", k=4)), f"next_a.{l}")
                    filled(act, sT, i)
                    act.wait_ge(scattered, nth)
                    drain(copy(scatT_f, bk(sT)[:, 0:NT * P]), sT)
                    filled(act, y0, i)
                    drain(copy(ye[:, 0:NB], bk(y0)[:, :]), y0)

                with act.Fori(0, PAIRS - 1) as i:
                    pair(i, "", i + (l * PAIRS + 1))
                pair(None, "last", (l + 1) * PAIRS)

            def rest_of_tokens(l):
                r = rest[l]
                act.wait_ge(count_ready, l + 1)
                total = act.value_load(counts[0:1, l:l + 1], min_val=0, max_val=S * 2)
                with act.If(total > 0):
                    act.wait_ge(r["rounds"], 1)
                    with act.Fori(0, NE) as i:
                        for t in range(NT):
                            act.wait_ge(r["h"], i * NT + t + 1)
                            act.activation(silu, bank[0][:, :], ACT.Silu).then_inc(r["silu"], 1)
                            act.wait_ge(r["hid"], i * NT + t + 1)
                act.nop()

            for q in (2, 3):
                c0, c1 = (0, NB) if q == 2 else (NB, LAT)
                filled(act, f"lat{q}")
                drain(copy(lat3[:, 1, c0:c1], bk(f"lat{q}")[:, 0:c1 - c0]), f"lat{q}")
            for q in range(4):
                drained(act, f"lat{q}")
            act.wait_ge(rms_loaded, 16)
            filled(act, "latT1")
            gained_latents(times, 1)
            for t in range(NT):
                for w, (c0, c1) in enumerate(((0, QR), (QR, QR + KVR))):
                    act.activation(square[:, 0:c1 - c0], lat3[:, t, c0:c1], ACT.Square,
                                   accum_out=sumsq[:, 2 * t + w:2 * t + w + 1]).then_inc(sumsq_ready, 1)
                    act.wait_ge(sumsq_ready, 2 * t + w + 1)
            act.wait_ge(key_rms_ready, 1)
            for o in range(1, 14, 2):
                filled(act, f"qkv{o}")
                qkv_copy(times, o)
            for step in range(H + 5):
                h = step
                if h < H and h % 2:
                    filled(act, f"headT{h}")
                    if h >= 3:
                        filled(act, f"score{h - 3}")
                    drain(copy(m_qk[h % 3][0:DQ, :], bk(f"headT{h}")[0:DQ, :]), f"headT{h}")
                h = step - 4
                if 0 <= h < H:
                    filled(act, f"probT{h}")
                    if h >= PROB_BUFS:
                        filled(act, f"mla_o{(h - PROB_BUFS) // 2}")
                    src = bk(f"probT{h}")
                    drain(copy(m_pt[h % PROB_BUFS], src[:, 0:3 * P]), f"probT{h}")
                h = step - 1
                if 0 <= h < H:
                    drained(act, f"score{h}")
                    s = m_s[h % SCORE_BUFS]
                    for t, (c0, c1) in enumerate(TILE_COLS):
                        act.activation(s[:, c0:c1], s[:, c0:c1], ACT.Exp, bias=nm3[:, h, t:t + 1], scale=-1.0,
                                       accum_out=z3[:, h, t:t + 1]).then_inc(raw_prob, 1)
                if step >= 8 and step % 4 == 0:
                    i = (step - 6) // 2
                    filled(act, f"mla_o{i}")
                    drain(copy(oT[:, i, :], bk(f"mla_o{i}")[:, 0:S]), f"mla_o{i}")
            xT_copies("x1T")
            router_copy(0)
            experts(0)
            rest_of_tokens(0)

            xT_copies("x2T")
            for q in (1, 3):
                filled(act, f"nq{q}")
                drain(times(nqT[:, 2 * q:2 * q + 2, :], bk(f"nq{q}")[:, :].rearrange("p (i s) -> p i s", i=2), NSA_SCALE), f"nq{q}")
            filled(act, "vc")
            shifted_streams(times, "vc", 1)
            for t in range(NT):
                filled(act, f"vwg{t}")
                copy(vsw[:, 1, t, :], bk(f"vwg{t}")[:, 0:KVC])
                drain(act.activation(n_gate[:, t * NGATE:(t + 1) * NGATE], bk(f"vwg{t}")[:, KVC:KVC + NGATE], ACT.Exp, scale=-1.0),
                      f"vwg{t}")
            filled(act, "ks")
            act.wait_ge(nsa_zeroed, 3)
            padded_keys(times, "ks", 0)
            act.wait_ge(cmp_in, 1)
            act.activation(sc_f, sc_f, ACT.Exp).then_inc(cmp_exp, 1)
            for step in range(H + 5):
                h = step - 4
                if 0 <= h < H:
                    if h >= PROB_BUFS:
                        filled(act, f"nsa_o{(h - PROB_BUFS) // 2}")
                    filled(act, f"nprobT_a{h}")
                    drain(copy(n_pt[h % PROB_BUFS][:, 0:2 * S], bk(f"nprobT_a{h}")[:, :]), f"nprobT_a{h}")
                    filled(act, f"nprobT_b{h}")
                    drain(copy(n_pt[h % PROB_BUFS][:, 2 * S:3 * S], bk(f"nprobT_b{h}")[:, 0:S]), f"nprobT_b{h}")
                h = step
                if h < H:
                    s = n_s[h % SCORE_BUFS]
                    for t in range(NT):
                        drained(act, (f"near{h}", f"far{h}")[t])
                        for b in range(2):
                            c0 = b * P if t == 0 else 2 * P + b * S
                            c1 = c0 + (t + 1) * P
                            act.activation(s[:, c0:c1], s[:, c0:c1], ACT.Exp, bias=v4d["nm"][:, h, t, b:b + 1], scale=-1.0,
                                           accum_out=v4d["z"][:, h, t, b:b + 1]).then_inc(nraw_prob, 1)
            xT_copies("x3T")
            router_copy(1)
            experts(1)
            rest_of_tokens(1)

        @block.vector
        def _(dve):
            st = Steps(dve, dve_step)
            copy = dve.tensor_copy

            def bc(ap, shape):
                return ap.to_broadcast(shape)

            def times(out, in_, factor):
                return dve.tensor_scalar(out, in_, factor, None, ALU.mult)

            def xT_copies(name):
                t, kh = divmod(2, 2)
                filled(dve, f"{name}2")
                drain(copy(xT[:, 4 * kh:4 * kh + 4, t * P:(t + 1) * P],
                           bk(f"{name}2")[:, :].rearrange("p (k s) -> p k s", k=4)), f"{name}2")

            def layer_norm(k, t, banks=None):
                halves = [slice(c * NB, (c + 1) * NB) for c in range(2)]
                src = [bk(nm)[:, :] for nm in banks] if banks else [x_tok[:, t, cols] for cols in halves]
                st.wait()
                st(dve.bn_aggr(mv[:, t, :], bn[:, t, :, :].rearrange("p c s -> p (c s)")))
                st.wait()
                dve.tensor_scalar(var_eps[:, t:t + 1], mv[:, t, 1:2], LN_EPS, None, ALU.add).then_inc(var_ready, 1)
                if t == 0:
                    dve.wait_ge(ln_loaded[k % 2], 32 * (k // 2 + 1))
                for c in range(2):
                    ins = dve.scalar_tensor_tensor(out=x_tok[:, t, halves[c]], in0=src[c], scalar=mv[:, t, 0:1], in1=gain[:, halves[c]],
                                                   op0=ALU.subtract, op1=ALU.mult)
                    if banks:
                        drain(ins, banks[c])
                    else:
                        st(ins)
                dve.wait_ge(rstd_ready, 1 + NT * k + t + 1)
                if not banks:
                    st.wait()
                for c in range(2):
                    if banks:
                        drained(dve, banks[c])
                    dve.scalar_tensor_tensor(out=x_tok[:, t, halves[c]], in0=x_tok[:, t, halves[c]], scalar=rstd[:, t:t + 1],
                                             in1=shift[:, halves[c]], op0=ALU.mult, op1=ALU.add).then_inc(x_ready, 1)

            def mixture_norm(l):
                def statistics(t, half):
                    filled(dve, f"moe_y{l}{2 * t + half}")
                    st(dve.bn_stats(bn[:, t, half, :], bk(f"moe_y{l}{2 * t + half}")[:, :]))

                for t, half in ((0, 0), (1, 0), (0, 1)):
                    statistics(t, half)
                layer_norm(2 * l + 1, 0, [f"moe_y{l}{half}" for half in range(2)])
                statistics(1, 1)
                layer_norm(2 * l + 1, 1, [f"moe_y{l}{2 + half}" for half in range(2)])

            def residual_norm(name, k):
                for t in range(NT):
                    for half in range(2):
                        nm = f"{name}{2 * t + half}"
                        filled(dve, nm)
                        cols = slice(half * NB, (half + 1) * NB)
                        drain(dve.scalar_tensor_tensor(out=x_tok[:, t, cols], in0=x_tok[:, t, cols], scalar=ALPHA,
                                                       in1=bk(nm)[:, :], op0=ALU.mult, op1=ALU.add), nm)
                        drained(dve, nm)
                        st(dve.bn_stats(bn[:, t, half, :], x_tok[:, t, cols]))
                    layer_norm(k, t)

            def reduce(out, in_, op):
                st(dve.tensor_reduce(out, in_, AX, op))
                st.wait()

            def tt(out, a_, b_, op):
                st(dve.tensor_tensor(out, a_, b_, op))
                st.wait()

            W4 = [P, NT, EPG]
            W16 = [P, NT, NG, EPG]

            def grouped(x):
                return x.rearrange("p t (g e) -> p t g e", g=NG)

            def route(l):
                dve.wait_ge(router_loaded, 32 * (l + 1))
                filled(dve, f"logits{l}")
                drain(dve.tensor_tensor(lg, bk(f"logits{l}")[:, 0:NT * NRP].rearrange("p (t c) -> p t c", t=NT)[:, :, 0:NR],
                                        bc(router_b.unsqueeze(1), [P, NT, NR]), ALU.add), f"logits{l}")
                drained(dve, f"logits{l}")
                glog, elog = lg[:, :, 0:NG], grouped(lg[:, :, NG:])
                desc16 = bc(desc.unsqueeze(1).unsqueeze(1), W16)

                def tensor2(*ops):
                    for out, x, y, op in ops:
                        st(dve.tensor_tensor(out, x, y, op))
                    st.wait()

                def reduce2(*ops):
                    for out, x, op in ops:
                        st(dve.tensor_reduce(out, x, AX, op))
                    st.wait()

                reduce2((gmax[:, :, 0], glog, ALU.max), (emax, elog, ALU.max))
                tensor2((k4, glog, bc(gmax, W4), ALU.is_equal), (grouped(k16), elog, bc(emax.unsqueeze(3), W16), ALU.is_equal))
                tensor2((k4, k4, bc(desc.unsqueeze(1), W4), ALU.mult), (grouped(k16), grouped(k16), desc16, ALU.mult))
                reduce2((r1[:, :, 0], k4, ALU.max), (r4, grouped(k16), ALU.max))
                tensor2((group1h, k4, bc(r1, W4), ALU.is_equal),
                        (grouped(first16), grouped(k16), bc(r4.unsqueeze(3), W16), ALU.is_equal))
                st(dve.scalar_tensor_tensor(out=grouped(rest16), in0=grouped(first16), scalar=NEG, in1=elog, op0=ALU.mult, op1=ALU.add))
                tensor2((grouped(prod16), elog, bc(group1h.unsqueeze(3), W16), ALU.mult), (e4, glog, bc(gmax, W4), ALU.subtract))
                reduce2((emax, grouped(rest16), ALU.max), (le4, prod16.rearrange("p t (g e) -> p t e g", g=NG), ALU.add))
                st(dve.tensor_reduce(v1[:, :, 0], le4, AX, ALU.max))
                tensor2((grouped(k16), grouped(rest16), bc(emax.unsqueeze(3), W16), ALU.is_equal))
                dve.tensor_tensor(p4, le4, bc(v1, W4), ALU.subtract).then_inc(logit_exp_in, 1)
                tensor2((grouped(k16), grouped(k16), desc16, ALU.mult))
                reduce2((r4, grouped(k16), ALU.max))
                tensor2((grouped(k16), grouped(k16), bc(r4.unsqueeze(3), W16), ALU.is_equal))
                tensor2((both16, first16, k16, ALU.add))
                dve.tensor_tensor(grouped(member), bc(group1h.unsqueeze(3), W16), grouped(both16), ALU.mult).then_inc(member_ready, 1)
                dve.wait_ge(member_ready, l + 1)
                filled(dve, f"position{l}")
                drain(dve.scalar_tensor_tensor(out=posm, in0=bk(f"position{l}")[:, 0:NT * NE].rearrange("p (t c) -> p t c", t=NT),
                                               scalar=1.0, in1=member, op0=ALU.add, op1=ALU.mult), f"position{l}")
                drained(dve, f"position{l}")

            def router_gates(l):
                dve.tensor_scalar(over, posm, CAP + 1.0, None, ALU.is_ge).then_inc(over_ready, 1)
                dve.wait_ge(logit_exp_out, 2 * l + 2)
                st(dve.tensor_reduce(r1[:, :, 0], e4, AX, ALU.add))
                st(dve.tensor_reduce(v1[:, :, 0], p4, AX, ALU.add))
                st(dve.tensor_reduce(both, member.rearrange("p t (g e) -> p t e g", g=NG), AX, ALU.add))
                st.wait()
                st(dve.reciprocal(r2, r1))
                st(dve.reciprocal(v2, v1))
                st.wait()
                tt(p4, p4, bc(v2, W4), ALU.mult)
                tt(m4, p4, both, ALU.mult)
                reduce(v1[:, :, 0], m4, ALU.add)
                st(dve.reciprocal(v2, v1))
                st.wait()
                tt(m4, m4, bc(v2, W4), ALU.mult)
                tt(gate4, m4, bc(r2, W4), ALU.mult)
                tt(grouped(gates), bc(group1h.unsqueeze(3), W16), bc(gate4.unsqueeze(2), W16), ALU.mult)
                dve.wait_ge(over_ready, l + 1)
                st(dve.tensor_tensor(rest_gates, gates, over, ALU.mult))

            def picks(l, e0):
                for t in range(NT):
                    for x in range(2):
                        ins = dve.tensor_scalar(pick[:, t, CAP * x:CAP * (x + 1)], iota, posm[:, t, bass.ds(e0 + x, 1)], None,
                                                ALU.is_equal)
                ins.then_inc(pick_ready, 1)

            def scatters(l, e0):
                for t in range(NT):
                    for x in range(2):
                        ins = dve.tensor_scalar(scat[:, t, CAP * x:CAP * (x + 1)], iota, posm[:, t, bass.ds(e0 + x, 1)],
                                                gates[:, t, bass.ds(e0 + x, 1)], ALU.is_equal, ALU.mult)
                ins.then_inc(scat_ready, 1)

            def experts(l):
                ins = dve.tensor_tensor(pick_f.rearrange("p (t x c) -> p t x c", t=NT, x=2),
                                        bc(iota.unsqueeze(1).unsqueeze(1), [P, NT, 2, CAP]),
                                        bc(posm[:, :, 0:2].unsqueeze(3), [P, NT, 2, CAP]), ALU.is_equal)
                ins.then_inc(pick_ready, 1)
                router_gates(l)
                filled(dve, f"gather_b{l}")
                drain(copy(xe[:, 4:8, :], bk(f"gather_b{l}")[:, :].rearrange("p (k s) -> p k s", k=4)), f"gather_b{l}")
                filled(dve, f"overflow{l}")
                drain(dve.tensor_reduce(k4[:, 0, 0:1], bk(f"overflow{l}")[:, 0:NT * NE], AX, ALU.add), f"overflow{l}")
                drained(dve, f"overflow{l}")
                dve.tensor_copy(counts[:, l:l + 1], k4[:, 0, 0:1]).then_inc(count_ready, 1)

                def pair(i, tag, e0, nth):
                    last = tag == "last"
                    h1, h3, hT, sT, y0, y1 = [f"{k}.{l}{tag}" for k in ("h1", "h3", "hidT", "scatT", "w2_0", "w2_1")]
                    b, k = number(sT, i)
                    dve.wait_ge(bank_drained[b], k - 2)
                    scatters(l, e0)
                    if not last:
                        filled(dve, h1, i)
                        picks(l, e0 + 2)
                    drained(dve, h1, i)
                    filled(dve, h3, i)
                    drain(dve.tensor_tensor(hid, silu, bk(h3)[:, :], ALU.mult), h3)
                    filled(dve, hT, i)
                    drain(copy(hidT_f, bk(hT)[:, :]), hT)
                    if not last:
                        filled(dve, f"next_b.{l}", i)
                        drain(copy(xe[:, 4:8, :], bk(f"next_b.{l}")[:, :].rearrange("p (k s) -> p k s", k=4)), f"next_b.{l}")
                    filled(dve, y1, i)
                    dve.wait_ge(scattered, nth)
                    drain(copy(ye[:, NB:2 * NB], bk(y1)[:, :]), y1)

                with dve.Fori(0, PAIRS - 1) as i:
                    pair(i, "", i * 2, i + (l * PAIRS + 1))
                pair(None, "last", 2 * (PAIRS - 1), (l + 1) * PAIRS)

            def rest_of_tokens(l):
                r = rest[l]
                dve.wait_ge(count_ready, l + 1)
                total = dve.value_load(counts[0:1, l:l + 1], min_val=0, max_val=S * 2)
                with dve.If(total > 0):
                    dve.memset(k4[:, 0, 0:1], 0.0).then_inc(r["rounds"], 1)
                    with dve.Fori(0, NE) as i:
                        for t in range(NT):
                            u = i * NT + t
                            dve.wait_ge(r["silu"], u + 1)
                            dve.scalar_tensor_tensor(out=hid, in0=bank[1][:, :], scalar=rest_gates[:, t, bass.ds(i, 1)],
                                                     in1=silu, op0=ALU.mult, op1=ALU.mult).then_inc(r["hid"], 1)
                            dve.wait_ge(r["hidT"], u + 1)
                            dve.wait_ge(r["rounds"], u + 1)
                            dve.tensor_copy(hidT_f, bank[2][:, :]).then_inc(r["hidT_copied"], 1)
                    dve.wait_ge(r["rounds"], NE * NT + 1)
                dve.nop()

            for q in (0, 1):
                c0, c1 = (0, NB) if q == 0 else (NB, LAT)
                filled(dve, f"lat{q}")
                drain(copy(lat3[:, 0, c0:c1], bk(f"lat{q}")[:, 0:c1 - c0]), f"lat{q}")
            for q in range(4):
                drained(dve, f"lat{q}")
            dve.wait_ge(const_loaded, 16)
            half = ROPE // 2

            def rotate(out1, out2, a1, a2, shape, heads):
                tmp = [r_[:, 0:NT * heads * half].rearrange("p (t h f) -> p t h f", t=NT, h=heads) for r_ in rt]
                cs, sn = bc(cos.unsqueeze(2), shape), bc(sin.unsqueeze(2), shape)
                for buf, (x, y) in zip(tmp, ((a1, cs), (a2, sn), (a1, sn), (a2, cs))):
                    st(dve.tensor_tensor(buf, x, y, ALU.mult))
                st.wait()
                dve.tensor_tensor(out1, tmp[0], tmp[1], ALU.subtract)
                return dve.tensor_tensor(out2, tmp[2], tmp[3], ALU.add)

            dve.wait_ge(rms_loaded, 16)
            for q in (0, 2):
                filled(dve, f"latT{q}")
                gained_latents(times, q)
            dve.wait_ge(sumsq_ready, 2 * NT)
            for t in range(NT):
                for w, c in enumerate((QR, KVR)):
                    ins = dve.tensor_scalar(sumsq[:, 2 * t + w:2 * t + w + 1], sumsq[:, 2 * t + w:2 * t + w + 1], 1.0 / c, RMS_EPS,
                                            ALU.mult, ALU.add)
            ins.then_inc(var_ready, 1)
            dve.wait_ge(rstd_ready, 1)
            times(key_rms, rms[:, 1::2], -MLA_SCALE).then_inc(key_rms_ready, 1)
            kr = lat3[:, :, QR + KVR:LAT].unsqueeze(2)

            def rope_of_keys():
                st(rotate(kr[:, :, :, 0:half], kr[:, :, :, half:], kr[:, :, :, 0:half], kr[:, :, :, half:], [P, NT, 1, half], 1))
                st.wait()
                for t in range(NT):
                    ins = times(k4d[:, t, :, NOPE:], bc(kr[:, t, :, :], [P, H, ROPE]), -MLA_SCALE)
                ins.then_inc(rope_ready, 1)

            dve.wait_ge(key_rms_ready, 1)
            for o in range(0, 14, 2):
                filled(dve, f"qkv{o}")
                qkv_copy(times, o)
                if o == 0:
                    rope_of_keys()
                if o == 6:
                    for u in range(6):
                        drained(dve, f"qkv{u}")
                    q1, q2 = q4[:, :, :, NOPE:NOPE + half], q4[:, :, :, NOPE + half:]
                    rotate(q1, q2, q1, q2, [P, NT, H, half], H).then_inc(rope_ready, 1)
            dve.wait_ge(rope_ready, 2)
            for step in range(H + 5):
                h = step
                if h < H and h % 2 == 0:
                    filled(dve, f"headT{h}")
                    if h >= 3:
                        filled(dve, f"score{h - 3}")
                    drain(copy(m_qk[h % 3][0:DQ, :], bk(f"headT{h}")[0:DQ, :]), f"headT{h}")
                h2 = step - 2
                if 0 <= h2 < H:
                    dve.wait_ge(raw_prob, NT * (h2 + 1))
                    st(dve.reciprocal(rz3[:, h2, :], z3[:, h2, :]))
                h = step - 1
                if 0 <= h < H:
                    filled(dve, f"score{h}")
                    if h >= SCORE_BUFS:
                        filled(dve, f"probT{h - SCORE_BUFS}")
                    for t, (c0, c1) in enumerate(TILE_COLS):
                        ins = dve.tensor_tensor_reduce(m_s[h % SCORE_BUFS][:, c0:c1], bk(f"score{h}")[:, c0:c1], mask[:, c0:c1], 1.0, HUGE,
                                                       ALU.add, ALU.min, nm3[:, h, t:t + 1])
                    drain(ins, f"score{h}")
                if 0 <= h2 < H:
                    st.wait()
                    for t, (c0, c1) in enumerate(TILE_COLS):
                        ins = times(m_s[h2 % SCORE_BUFS][:, c0:c1], m_s[h2 % SCORE_BUFS][:, c0:c1], rz3[:, h2, t:t + 1])
                    ins.then_inc(prob_ready, 1)
                if step >= 6 and step % 4 == 2:
                    i = (step - 6) // 2
                    filled(dve, f"mla_o{i}")
                    drain(copy(oT[:, i, :], bk(f"mla_o{i}")[:, 0:S]), f"mla_o{i}")
            dve.wait_ge(x_loaded, 16)
            residual_norm("mla_y", 0)
            xT_copies("x1T")
            route(0)
            experts(0)
            rest_of_tokens(0)
            mixture_norm(0)

            xT_copies("x2T")
            for q in (0, 2):
                filled(dve, f"nq{q}")
                drain(times(nqT[:, 2 * q:2 * q + 2, :], bk(f"nq{q}")[:, :].rearrange("p (i s) -> p i s", i=2), NSA_SCALE), f"nq{q}")
            dve.wait_ge(nsa_loaded, 16)
            copy(streams_f.rearrange("p (w s) -> p w s", w=2 * G)[:, :, CMP_STRIDE * NCMP:],
                 bc(pos_t[:, :].unsqueeze(1), [P, 2 * G, CMP_STRIDE])).then_inc(pos_placed, 1)
            filled(dve, "kc")
            shifted_streams(times, "kc", 0)
            for t in range(NT):
                drained(dve, f"vwg{t}")
            st(dve.tensor_scalar(n_gate, n_gate, 1.0, None, ALU.add))
            st.wait()
            st(dve.reciprocal(n_gate, n_gate))
            filled(dve, "cmp")
            dve.wait_ge(nsa_zeroed, 3)
            drain(copy(cmp_f, bk("cmp")[:, 0:2 * G * CMP_PAD]), "cmp")
            drained(dve, "cmp")
            cmp4 = cmp_f.rearrange("p (g n) -> p g n", n=CMP_PAD)
            for x in range(2):
                dve.tensor_tensor(kbd[HD * x:HD * (x + 1), :, CMP_PAD * x:CMP_PAD * x + NCMP], cmp4[0:HD, 0:G, 0:NCMP],
                                  bc(cmp4[0:HD, 0:G, NCMP:], [HD, G, NCMP]), ALU.add)
            dve.tensor_tensor(vrep_f[HD:P, :].rearrange("p (g r n) -> p g r n", g=G, r=HPG)[:, :, :, 0:NCMP],
                                    bc(cmp4[HD:P, G:, 0:NCMP].unsqueeze(2), [HD, G, HPG, NCMP]),
                                    bc(cmp4[HD:P, G:, NCMP:].unsqueeze(2), [HD, G, HPG, NCMP]), ALU.add).then_inc(cmp_kv_ready, 1)
            filled(dve, "vrep")
            for u in range(2):
                heads = P // CMP_PAD
                ins = dve.tensor_tensor(vbd_f[:, u * heads * HD:(u + 1) * heads * HD].rearrange("p (h d) -> p h d", h=heads),
                                        bc(bk("vrep")[:, u * HD:(u + 1) * HD].unsqueeze(1), [P, heads, HD]),
                                        bc(own_block.unsqueeze(2), [P, heads, HD]), ALU.mult)
            drain(ins, "vrep")
            filled(dve, "cs")
            R = NT * H
            wide = [P, R, CMP_PAD]
            drain(dve.tensor_tensor(sc, bk("cs")[:, :].rearrange("p (r n) -> p r n", r=R),
                                    cmp_bias.rearrange("p t h n -> p (t h) n"), ALU.add), "cs")
            drained(dve, "cs")
            reduce(c_mx, sc, ALU.max)
            dve.tensor_tensor(sc, sc, bc(c_mx.unsqueeze(2), wide), ALU.subtract).then_inc(cmp_in, 1)
            dve.wait_ge(cmp_exp, 1)
            reduce(c_z, sc, ALU.add)
            st(dve.reciprocal(c_cf, c_z))
            st.wait()
            tt(c_cf.rearrange("p (t h) -> p t h", t=NT), c_cf.rearrange("p (t h) -> p t h", t=NT),
               bc(any_visible.unsqueeze(2), [P, NT, H]), ALU.mult)
            tt(c_cf, c_cf, gate3[:, :, 0], ALU.mult)
            dve.tensor_tensor(sc, sc, bc(c_cf.unsqueeze(2), wide), ALU.mult).then_inc(cmp_prob, 1)
            filled(dve, "kw")
            padded_keys(times, "kw", 1)
            for step in range(H + 5):
                h2 = step - 2
                if 0 <= h2 < H:
                    dve.wait_ge(nraw_prob, 4 * (h2 + 1))
                    st(dve.reciprocal(v4d["rz"][:, h2], v4d["z"][:, h2]))
                h = step
                if h < H:
                    if h >= SCORE_BUFS:
                        filled(dve, f"nprobT_b{h - SCORE_BUFS}")
                    dve.wait_ge(bias_ready, h + 1)
                    for t, nm in enumerate((f"near{h}", f"far{h}")):
                        filled(dve, nm)
                        w = (t + 1) * P
                        bias = n_bias[h % 2][:, t * P:t * P + w]
                        for b in range(2):
                            c0 = b * P if t == 0 else 2 * P + b * S
                            ins = dve.tensor_tensor_reduce(n_s[h % SCORE_BUFS][:, c0:c0 + w], bk(nm)[:, b * w:(b + 1) * w], bias, 1.0, HUGE,
                                                           ALU.add, ALU.min, v4d["nm"][:, h, t, b:b + 1])
                        drain(ins, nm)
                if h == 1:
                    filled(dve, "vs")
                    drain(copy(vsw[:, 0, :, :], bk("vs")[:, :].rearrange("p (t c) -> p t c", t=NT)), "vs")
                    filled(dve, "pcT")
                    drain(copy(pct_f, bk("pcT")[:, :]), "pcT")
                if 0 <= h2 < H:
                    st.wait()
                    tt(v4d["cf"][:, h2], v4d["rz"][:, h2], gate4d[:, :, h2, 1:3], ALU.mult)
                    for t in range(NT):
                        for b in range(2):
                            c0 = b * P if t == 0 else 2 * P + b * S
                            cols = slice(c0, c0 + (t + 1) * P)
                            ins = times(n_s[h2 % SCORE_BUFS][:, cols], n_s[h2 % SCORE_BUFS][:, cols], v4d["cf"][:, h2, t, b:b + 1])
                    ins.then_inc(nprob_ready, 1)
                if step >= 6 and step % 2 == 0:
                    i = (step - 6) // 2
                    filled(dve, f"nsa_o{i}")
                    drain(copy(oT[:, i, :], bk(f"nsa_o{i}")[:, 0:S]), f"nsa_o{i}")
            residual_norm("nsa_y", 2)
            xT_copies("x3T")
            route(1)
            experts(1)
            rest_of_tokens(1)
            mixture_norm(1)


def kernel(**inputs):
    import concourse.bacc as bacc
    from concourse.bass_utils import run_bass_kernel_spmd

    f = {k: np.asarray(v) for k, v in inputs.items()}
    const, _ = shape_constants()
    lay = {
        "x": f["x"][0],
        "xT": f["x"][0].T.reshape(P, KD * S),
        "const": const,
        "rms_gain": np.concatenate([f["mla_q_norm"][0].reshape(P, CQ), f["mla_kv_norm"][0].reshape(P, CKV)], 1),
        "mla_w_in": f["mla_w_in"][0],
        "mla_w_qb": f["mla_w_qb"][0],
        "mla_w_kvb": f["mla_w_kvb"][0],
        "mla_w_o": f["mla_w_o"][0],
        "nsa_w_in": f["nsa_w_in"][0],
        "nsa_w_o": f["nsa_w_o"][0],
        "phi": np.stack([f[k][0].reshape(2, CMP_STRIDE, HD, HD) for k in ("nsa_w_phi_k", "nsa_w_phi_v")])
        .transpose(1, 3, 2, 0, 4).reshape(P, CMP_STRIDE * 2 * HD),
        "cmp_posT": f["nsa_cmp_pos"][0].reshape(2, CMP_STRIDE, HD).transpose(0, 2, 1).reshape(P, CMP_STRIDE),
        "ln": np.stack([f[k][l] for l in range(DEPTH) for k in ("ln1_g", "ln1_b", "ln2_g", "ln2_b")]),
        "router_w": np.stack([np.pad(np.concatenate([f["moe_wg"][l], f["moe_we"][l].transpose(1, 0, 2).reshape(D, NE)], 1),
                                     ((0, 0), (0, NRP - NR))).reshape(P, KD * NRP) for l in range(DEPTH)]),
        "router_b": np.concatenate([f["moe_bg"], f["moe_be"].reshape(DEPTH, NE)], 1),
        "moe_w1": f["moe_w1"].reshape(DEPTH * NE, D, FF),
        "moe_w3": f["moe_w3"].reshape(DEPTH * NE, D, FF),
        "moe_w2": f["moe_w2"].reshape(DEPTH * NE, FF, D),
    }
    nc = bacc.Bacc("TRN2", target_bir_lowering=False, num_devices=1)
    arrays, a = {}, {}
    for name, v in lay.items():
        arrays[f"in_{name}"] = np.ascontiguousarray(v)
        a[name] = nc.dram_tensor(f"in_{name}", v.shape, F32, kind="ExternalInput").ap()
    a["out"] = nc.dram_tensor("out_0", (S, D), F32, kind="ExternalOutput").ap()
    build(nc, a)
    r = run_bass_kernel_spmd(nc, [arrays], core_ids=[0])
    return r.results[0]["out_0"].reshape(1, S, D)
```
